# Optimizing a Trainium2 kernel written in Bass

```python
import jax, jax.numpy as jnp
from jax import lax
import numpy as np

D_MODEL = 1024
BATCH = 1
SEQ = 256
DEPTH = 2
DEC_BATCH = 8
DEC_SEQ = 1
PAST_LEN = 2048
PAGE_SIZE = 128

D_POOL = D_MODEL // 2
POOL_WINDOWS = (2, 4, 8, 16)
N_POOL_GROUPS = len(POOL_WINDOWS)
POOL_GROUP = D_POOL // N_POOL_GROUPS
POOL_HIST = max(POOL_WINDOWS) - 1
D_RNN = D_MODEL // 2
RNN_HEADS = 8
RNN_HEAD_DIM = D_RNN // RNN_HEADS
CONV_WIDTH = 4
RGLRU_C = 8.0
D_MIX = D_POOL + D_RNN
D_IN = D_POOL + 2 * D_RNN
N_MEM = 256
MEM_HEADS = 4
MEM_HEAD_DIM = D_MODEL // MEM_HEADS
D_FF = 2816
N_EXPERTS = 8
TOP_K = 2
D_FF_EXPERT = D_FF // TOP_K
N_DENSE = (DEPTH + 1) // 2
N_MOE = DEPTH // 2
EPS = 1e-6

kernel_name = 'hybrid_pool_rglru_decoder_step'

def rmsnorm(x, g):
    xf = x.astype(jnp.float32)
    y = xf * lax.rsqrt(jnp.mean(xf * xf, axis=-1, keepdims=True) + EPS)
    return (y * g.astype(jnp.float32)).astype(x.dtype)

def pool_mixer(u, hist, pos, w_blk, scale):
    B, T, _ = u.shape
    full = jnp.concatenate([hist, u], axis=1).astype(jnp.float32)
    cs = lax.cumsum(full, axis=1)
    cs = jnp.concatenate([jnp.zeros_like(cs[:, :1]), cs], axis=1)
    end = cs[:, POOL_HIST + 1:]
    outs = []
    for g, w in enumerate(POOL_WINDOWS):
        sl = slice(g * POOL_GROUP, (g + 1) * POOL_GROUP)
        start = cs[:, POOL_HIST + 1 - w:POOL_HIST + 1 - w + T, sl]
        cnt = jnp.minimum(pos + 1, w).astype(jnp.float32)[None, :, None]
        outs.append((end[..., sl] - start) / cnt)
    z = jnp.concatenate(outs, axis=-1) - u.astype(jnp.float32)
    z = z.reshape(B, T, N_POOL_GROUPS, POOL_GROUP)
    z = jnp.einsum('btgc,gcd->btgd', z, w_blk.astype(jnp.float32)).reshape(B, T, D_POOL)
    y = z * scale.astype(jnp.float32)
    return y.astype(u.dtype), full[:, -POOL_HIST:].astype(u.dtype)

def causal_conv(x, buf, w, b):
    T = x.shape[1]
    full = jnp.concatenate([buf.astype(x.dtype), x], axis=1)
    y = b.astype(x.dtype)
    for k in range(CONV_WIDTH):
        y = y + full[:, k:k + T] * w[k].astype(x.dtype)
    return y, full[:, -(CONV_WIDTH - 1):]

def _scan_combine(left, right):
    a1, b1 = left
    a2, b2 = right
    return a1 * a2, a2 * b1 + b2

def rglru(x, h0, pos, wa, ba, wx, bx, lam):
    B, T, _ = x.shape
    f32 = jnp.float32
    xf = x.astype(f32)
    xh = xf.reshape(B, T, RNN_HEADS, RNN_HEAD_DIM)
    r = jax.nn.sigmoid(jnp.einsum('bthi,hij->bthj', xh, wa.astype(f32)).reshape(B, T, D_RNN) + ba.astype(f32))
    i = jax.nn.sigmoid(jnp.einsum('bthi,hij->bthj', xh, wx.astype(f32)).reshape(B, T, D_RNN) + bx.astype(f32))
    log_a = -RGLRU_C * r * jax.nn.softplus(-lam.astype(f32))
    a = jnp.exp(log_a)
    mult = jnp.sqrt(-jnp.expm1(2.0 * log_a))
    mult = jnp.where((pos == 0)[None, :, None], 1.0, mult)
    bterm = mult * (i * xf)
    bterm = bterm.at[:, 0].add(a[:, 0] * h0.astype(f32))
    _, h = lax.associative_scan(_scan_combine, (a, bterm), axis=1)
    return h, h[:, -1]

def mem_kv(mem, g, wk, wv):
    B = mem.shape[0]
    mn = rmsnorm(mem, g)
    k = (mn @ wk).reshape(B, N_MEM, MEM_HEADS, MEM_HEAD_DIM)
    v = (mn @ wv).reshape(B, N_MEM, MEM_HEADS, MEM_HEAD_DIM)
    return k, v

def mem_attend(xn, k, v, wq, wo):
    B, T, _ = xn.shape
    q = (xn @ wq).reshape(B, T, MEM_HEADS, MEM_HEAD_DIM)
    s = jnp.einsum('bthd,bmhd->bhtm', q, k.astype(q.dtype)).astype(jnp.float32) * (MEM_HEAD_DIM ** -0.5)
    p = jax.nn.softmax(s, axis=-1).astype(xn.dtype)
    o = jnp.einsum('bhtm,bmhd->bthd', p, v.astype(xn.dtype)).reshape(B, T, D_MODEL)
    return o @ wo

def swiglu(x, wg, wu, wd):
    return (jax.nn.silu(x @ wg) * (x @ wu)) @ wd

def moe(x, router_w, wg, wu, wd):
    B, T, D = x.shape
    xt = x.reshape(B * T, D)
    logits = (xt @ router_w).astype(jnp.float32)
    top_v, top_i = lax.top_k(logits, TOP_K)
    gates = jax.nn.softmax(top_v, axis=-1)
    combine = jnp.sum(jax.nn.one_hot(top_i, N_EXPERTS, dtype=jnp.float32) * gates[..., None], axis=1)
    out = jnp.zeros_like(xt)
    for e in range(N_EXPERTS):
        out = out + combine[:, e:e + 1].astype(x.dtype) * swiglu(xt, wg[e], wu[e], wd[e])
    return out.reshape(B, T, D)

def _layer(x, l, pos, pool_hist, conv_buf, h0, mk, mv, P):
    hn = rmsnorm(x, P['norm_mix'][l])
    proj = hn @ P['w_in'][l]
    u_pool = proj[..., :D_POOL]
    u_rnn = proj[..., D_POOL:D_MIX]
    u_gate = proj[..., D_MIX:]
    y_pool, new_hist = pool_mixer(u_pool, pool_hist, pos, P['pool_w'][l], P['pool_scale'][l])
    c, new_conv = causal_conv(u_rnn, conv_buf, P['conv_w'][l], P['conv_b'][l])
    h, h_last = rglru(c, h0, pos, P['gate_a_w'][l], P['gate_a_b'][l], P['gate_x_w'][l], P['gate_x_b'][l], P['rglru_lambda'][l])
    y_rnn = (h * jax.nn.gelu(u_gate.astype(jnp.float32))).astype(x.dtype)
    mixed = jnp.concatenate([rmsnorm(y_pool, P['out_norm_pool'][l]), rmsnorm(y_rnn, P['out_norm_rnn'][l])], axis=-1)
    x = x + mixed @ P['w_out'][l]
    x = x + mem_attend(rmsnorm(x, P['norm_mem'][l]), mk, mv, P['w_mq'][l], P['w_mo'][l])
    hn = rmsnorm(x, P['norm_ffn'][l])
    j = l // 2
    if l % 2 == 0:
        x = x + swiglu(hn, P['ffn_w_gate'][j], P['ffn_w_up'][j], P['ffn_w_down'][j])
    else:
        x = x + moe(hn, P['router_w'][j], P['moe_w_gate'][j], P['moe_w_up'][j], P['moe_w_down'][j])
    return x, new_hist, new_conv, h_last.astype(x.dtype)

def _trunk(x, pos, pool_hist, conv_buf, h0, mem_k, mem_v, P):
    hists, convs, hs = [], [], []
    for l in range(DEPTH):
        x, nh, nc, hl = _layer(x, l, pos, pool_hist[l], conv_buf[l], h0[l], mem_k[l], mem_v[l], P)
        hists.append(nh)
        convs.append(nc)
        hs.append(hl)
    return rmsnorm(x, P['final_norm']), jnp.stack(hists), jnp.stack(convs), jnp.stack(hs)

def setup_inputs(seed: int = 0) -> dict:
    key = jax.random.key(seed)
    ks = iter(jax.random.split(key, 48))
    f32 = jnp.float32
    L = DEPTH

    def nrm(shape, scale=1.0):
        return scale * jax.random.normal(next(ks), shape, f32)

    def gain(shape):
        return 1.0 + 0.05 * jax.random.normal(next(ks), shape, f32)

    x_prompt = nrm((BATCH, SEQ, D_MODEL))
    x_sample = nrm((DEC_BATCH, DEC_SEQ, D_MODEL))
    mem_prompt = nrm((BATCH, N_MEM, D_MODEL))
    state_pool = nrm((L, DEC_BATCH, POOL_HIST, D_POOL))
    state_conv = nrm((L, DEC_BATCH, CONV_WIDTH - 1, D_RNN))
    state_h = nrm((L, DEC_BATCH, D_RNN), 0.5)
    cache_mem_k = nrm((L, DEC_BATCH, N_MEM, MEM_HEADS, MEM_HEAD_DIM))
    cache_mem_v = nrm((L, DEC_BATCH, N_MEM, MEM_HEADS, MEM_HEAD_DIM))
    norm_mix = gain((L, D_MODEL))
    w_in = nrm((L, D_MODEL, D_IN), D_MODEL ** -0.5)
    pool_w = nrm((L, N_POOL_GROUPS, POOL_GROUP, POOL_GROUP), POOL_GROUP ** -0.5)
    pool_scale = gain((L, D_POOL))
    conv_w = nrm((L, CONV_WIDTH, D_RNN), CONV_WIDTH ** -0.5)
    conv_b = nrm((L, D_RNN), 0.02)
    gate_a_w = nrm((L, RNN_HEADS, RNN_HEAD_DIM, RNN_HEAD_DIM), RNN_HEAD_DIM ** -0.5)
    gate_a_b = nrm((L, D_RNN), 0.02)
    gate_x_w = nrm((L, RNN_HEADS, RNN_HEAD_DIM, RNN_HEAD_DIM), RNN_HEAD_DIM ** -0.5)
    gate_x_b = nrm((L, D_RNN), 0.02)
    u = jax.random.uniform(next(ks), (L, D_RNN), f32, 0.9 ** 2, 0.999 ** 2)
    s = -0.5 * jnp.log(u)
    rglru_lambda = -jnp.log(jnp.expm1(s))
    out_norm_pool = gain((L, D_POOL))
    out_norm_rnn = gain((L, D_RNN))
    w_out = nrm((L, D_MIX, D_MODEL), D_MIX ** -0.5)
    norm_mem = gain((L, D_MODEL))
    mem_norm = gain((L, D_MODEL))
    w_mq = nrm((L, D_MODEL, D_MODEL), D_MODEL ** -0.5)
    w_mk = nrm((L, D_MODEL, D_MODEL), D_MODEL ** -0.5)
    w_mv = nrm((L, D_MODEL, D_MODEL), D_MODEL ** -0.5)
    w_mo = nrm((L, D_MODEL, D_MODEL), D_MODEL ** -0.5)
    norm_ffn = gain((L, D_MODEL))
    ffn_w_gate = nrm((N_DENSE, D_MODEL, D_FF), D_MODEL ** -0.5)
    ffn_w_up = nrm((N_DENSE, D_MODEL, D_FF), D_MODEL ** -0.5)
    ffn_w_down = nrm((N_DENSE, D_FF, D_MODEL), D_FF ** -0.5)
    router_w = nrm((N_MOE, D_MODEL, N_EXPERTS), D_MODEL ** -0.5)
    moe_w_gate = nrm((N_MOE, N_EXPERTS, D_MODEL, D_FF_EXPERT), D_MODEL ** -0.5)
    moe_w_up = nrm((N_MOE, N_EXPERTS, D_MODEL, D_FF_EXPERT), D_MODEL ** -0.5)
    moe_w_down = nrm((N_MOE, N_EXPERTS, D_FF_EXPERT, D_MODEL), D_FF_EXPERT ** -0.5)
    final_norm = gain((D_MODEL,))
    return {'x_prompt': x_prompt, 'x_sample': x_sample, 'mem_prompt': mem_prompt,
            'state_pool': state_pool, 'state_conv': state_conv, 'state_h': state_h,
            'cache_mem_k': cache_mem_k, 'cache_mem_v': cache_mem_v,
            'norm_mix': norm_mix, 'w_in': w_in, 'pool_w': pool_w, 'pool_scale': pool_scale,
            'conv_w': conv_w, 'conv_b': conv_b, 'gate_a_w': gate_a_w, 'gate_a_b': gate_a_b,
            'gate_x_w': gate_x_w, 'gate_x_b': gate_x_b, 'rglru_lambda': rglru_lambda,
            'out_norm_pool': out_norm_pool, 'out_norm_rnn': out_norm_rnn, 'w_out': w_out,
            'norm_mem': norm_mem, 'mem_norm': mem_norm, 'w_mq': w_mq, 'w_mk': w_mk, 'w_mv': w_mv, 'w_mo': w_mo,
            'norm_ffn': norm_ffn, 'ffn_w_gate': ffn_w_gate, 'ffn_w_up': ffn_w_up, 'ffn_w_down': ffn_w_down,
            'router_w': router_w, 'moe_w_gate': moe_w_gate, 'moe_w_up': moe_w_up, 'moe_w_down': moe_w_down,
            'final_norm': final_norm}

def reference(x_prompt, x_sample, mem_prompt, state_pool, state_conv, state_h, cache_mem_k, cache_mem_v,
              norm_mix, w_in, pool_w, pool_scale, conv_w, conv_b, gate_a_w, gate_a_b, gate_x_w, gate_x_b,
              rglru_lambda, out_norm_pool, out_norm_rnn, w_out, norm_mem, mem_norm, w_mq, w_mk, w_mv, w_mo,
              norm_ffn, ffn_w_gate, ffn_w_up, ffn_w_down, router_w, moe_w_gate, moe_w_up, moe_w_down, final_norm):
    P = dict(norm_mix=norm_mix, w_in=w_in, pool_w=pool_w, pool_scale=pool_scale, conv_w=conv_w, conv_b=conv_b,
             gate_a_w=gate_a_w, gate_a_b=gate_a_b, gate_x_w=gate_x_w, gate_x_b=gate_x_b, rglru_lambda=rglru_lambda,
             out_norm_pool=out_norm_pool, out_norm_rnn=out_norm_rnn, w_out=w_out, norm_mem=norm_mem,
             w_mq=w_mq, w_mo=w_mo, norm_ffn=norm_ffn, ffn_w_gate=ffn_w_gate, ffn_w_up=ffn_w_up,
             ffn_w_down=ffn_w_down, router_w=router_w, moe_w_gate=moe_w_gate, moe_w_up=moe_w_up,
             moe_w_down=moe_w_down, final_norm=final_norm)
    B, T, _ = x_prompt.shape
    dt = x_prompt.dtype
    mks, mvs = [], []
    for l in range(DEPTH):
        k, v = mem_kv(mem_prompt, mem_norm[l], w_mk[l], w_mv[l])
        mks.append(k)
        mvs.append(v)
    mem_k_p = jnp.stack(mks)
    mem_v_p = jnp.stack(mvs)
    pos_p = jnp.arange(T, dtype=jnp.int32)
    zeros_pool = jnp.zeros((DEPTH, B, POOL_HIST, D_POOL), dt)
    zeros_conv = jnp.zeros((DEPTH, B, CONV_WIDTH - 1, D_RNN), dt)
    zeros_h = jnp.zeros((DEPTH, B, D_RNN), dt)
    y_prompt, pool_p, conv_p, h_p = _trunk(x_prompt, pos_p, zeros_pool, zeros_conv, zeros_h, mem_k_p, mem_v_p, P)
    pos_s = PAST_LEN + jnp.arange(x_sample.shape[1], dtype=jnp.int32)
    y_sample, pool_s, conv_s, h_s = _trunk(x_sample, pos_s, state_pool, state_conv, state_h, cache_mem_k, cache_mem_v, P)
    return (y_prompt, y_sample, pool_p, conv_p, h_p, mem_k_p, mem_v_p, pool_s, conv_s, h_s)


_drawn_inputs = setup_inputs


def setup_inputs(seed=0):
    import zlib

    import numpy as np

    out = dict(_drawn_inputs(seed))
    spreads = {}
    factors = {'gate_a_b': 4.916, 'gate_x_b': 6.622, 'norm_mem': 4.541}
    for name, (base, spread) in spreads.items():
        noise = np.random.default_rng([zlib.crc32(name.encode()), seed]).standard_normal(out[name].shape)
        drawn = base * np.exp(spread * noise) if base else spread * noise
        out[name] = __import__('jax').numpy.asarray(drawn.astype(out[name].dtype))
    for name, factor in factors.items():
        out[name] = (out[name] * factor).astype(out[name].dtype)
    return out
```

```python
from contextlib import ExitStack

import concourse.bass as bass
from concourse import mybir

ALU = mybir.AluOpType
ACT = mybir.ActivationFunctionType
F32 = mybir.dt.float32
U32 = mybir.dt.uint32
I32 = mybir.dt.int32
AX_X = mybir.AxisListType.X

P = 128
D = 1024
KC = D // P
TP, TS = 256, 8
T = TP + TS
DEPTH = 2
NM = 256
MC = NM // P
NH, HD = 4, 256
HC = HD // P
WINDOWS = (2, 4, 8, 16)
HIST = 15
CW = 4
RC = 4
FF = 2816
FC = FF // P
NE = 8
FE = FF // 2
FEC = FE // P
EPS = 1e-6

PIECE = 256
SLAB = 8 * PIECE
GW = FE // 4
PAIR = 2 * KC * GW
RING = 4 * PAIR
NSLOT = RING // SLAB
HALF_DOWN = FEC * D // 2

VEC = {}
_n = 0
for _name, _cols in (("norm_mix", 8), ("norm_mem", 8), ("mem_norm", 8), ("norm_ffn", 8), ("out_norm_pool", 4),
                     ("out_norm_rnn", 4), ("pool_scale", 4), ("conv_w", 16), ("conv_b", 4), ("gate_a_b", 4),
                     ("gate_x_b", 4), ("rglru_lambda", 4)):
    VEC[_name] = _n
    _n += _cols
LVEC = _n
VEC_FINAL = DEPTH * LVEC
VEC_H0 = VEC_FINAL + KC
VEC_CONV = VEC_H0 + DEPTH * RC * TS
VEC_POOL = VEC_CONV + DEPTH * RC * TS * (CW - 1)
NVEC = VEC_POOL + DEPTH * RC * TS * HIST
C_ID, C_TRI, C_IOTA, C_CORR, C_VALID = 0, P, 2 * P, 3 * P, 3 * P + 4 * 16
NCONST = C_VALID + 3
O_PP = 0
O_PC = O_PP + RC * HIST
O_PH = O_PC + RC * (CW - 1)
O_SP = O_PH + RC
O_SC = O_SP + RC * TS * HIST
O_SH = O_SC + RC * TS * (CW - 1)
NOUT = O_SH + RC * TS

TOK = [(0, P), (P, P), (TP, TS)]
BLOCKS = NE
MAXB = (T + P - 1) // P
CAP = P


def stream_plan():
    out = []
    for l in range(DEPTH):
        out += [("in", l, s) for s in range(6)]
        out += [("mk", l, s) for s in range(4)]
        out += [("mv", l, s) for s in range(4)]
        out += [("out", l, s) for s in range(4)]
        out += [("mq", l, s) for s in range(4)]
        out += [("kc", l, s) for s in range(8)]
        out += [("vc", l, s) for s in range(8)]
        out += [("mo", l, s) for s in range(4)]
        if l % 2 == 0:
            for s in range(11):
                out += [("fg", l, s), ("fu", l, s)]
            out += [("fd", l, s) for s in range(11)]
    return out


def bank_plan():
    out = []
    for l in range(DEPTH):
        if l == 0:
            out += [("msq",)]
        out += [("ssq", 3 * l)]
        out += [("in", l, m) for m in range(12)]
        out += [("mk", l, m) for m in range(8)]
        out += [("ga", l, c) for c in range(RC)] + [("gx", l, c) for c in range(RC)]
        out += [("mv", l, s, mc) for s in range(4) for mc in range(MC)]
        out += [("pw", l, c) for c in range(RC)]
        out += [("psq", l), ("rsq", l)]
        out += [("out", l, m) for m in range(KC)]
        out += [("ssq", 3 * l + 1)]
        out += [("mq", l, m) for m in range(KC)]
        out += [("sc", l, t, hp) for t in range(3) for hp in range(2)]
        out += [("pt", l, h) for h in range(NH)]
        out += [("pv", l, m) for m in range(KC)]
        out += [("pts", l)]
        out += [("pvs", l, hp) for hp in range(2)]
        out += [("ots", l)]
        out += [("mo", l, m) for m in range(KC)]
        out += [("ssq", 3 * l + 2)]
        if l % 2 == 0:
            for s in range(FC // 2):
                out += [("fg", l, 2 * s), ("fg", l, 2 * s + 1), ("fu", l, 2 * s), ("fu", l, 2 * s + 1)]
            out += [("fd", l, m) for m in range(KC)]
        else:
            out += [("lg", l)]
            out += [("tk", l, t, hp) for t in range(3) for hp in range(2)]
            out += [("ps", l)]
    return out


def trunk_kernel(nc, xT, memT, vecs, consts, pool_w, gate_w, router_w, dense, experts,
                 o_y, o_small, o_k, o_v):
    slabs = {name: k for k, name in enumerate(stream_plan())}
    tiles = {name: n for n, name in enumerate(bank_plan())}
    NSLAB = len(slabs)
    NT0 = len(tiles)

    FIRST = ["G0", "U0", "G1", "U1", "G2", "U2", "T0", "G3", "U3", "T1", "X0", "X1", "T2", "D0", "D1"]
    MID = ["G0", "U0", "G1", "U1", "G2", "U2", "T0", "G3", "U3", "T1", "S", "C0", "C1", "C2", "C3", "C4", "C5", "C6",
           "C7", "X0", "X1", "T2", "D0", "D1"]
    TAIL = ["S"] + [f"C{c}" for c in range(KC)]
    LAST = [x for x in MID if x[0] != "X"]

    assert len(MID) == 24 and FIRST == ["G0", "U0", "G1", "U1", "G2", "U2", "T0", "G3", "U3", "T1"] + MID[19:]

    class Pass:

        def __init__(self, n0, v0, nv):
            self.n0, self.v0, self.nv = n0, v0, nv
            self.mid = n0 + 2 + len(FIRST)
            self.tail = self.mid + len(MID) * (nv - 2) + len(LAST)
            self.end = self.tail + len(TAIL)

        def first(self, kind):
            return self.n0 + 2 + FIRST.index(kind), 0

        def middle(self, v):
            return lambda kind: (self.mid + MID.index(kind), v - (self.v0 + 1))

        def last(self, kind):
            return self.mid + len(MID) * (self.nv - 2) + LAST.index(kind), 0

        def after(self, kind):
            return self.tail + TAIL.index(kind), 0

        def earlier(self, v):
            return lambda kind: (self.mid + MID.index(kind) - len(MID), v - (self.v0 + 1))

        def prologue(self, kind):
            return self.n0 + int(kind[1]), 0

    with ExitStack() as ctx:
        def sb(name, shape, dt=F32):
            return ctx.enter_context(nc.sbuf_tensor(name, shape, dt))

        def sem(name):
            return ctx.enter_context(nc.semaphore(name))

        ring = sb("ring", [P, RING])
        x = sb("x", [P, KC, T])
        xn = sb("xn", [P, KC, T])
        sq = sb("sq", [P, KC, T])
        vec = sb("vec", [P, NVEC])
        con = sb("con", [P, NCONST])
        ones = sb("ones", [P, P])
        eps = sb("eps", [P, 1])
        rms = sb("rms", [P, 2, T])
        rstd = sb("rstd", [P, 2, T])
        mem = sb("mem", [P, KC, NM])
        poolw = sb("poolw", [P, DEPTH, RC, P])
        gatew = sb("gatew", [P, DEPTH, 2, RC, P])
        rw = sb("rw", [P, KC, NE])
        coef = sb("coef", [P, 6, DEPTH * RC])
        kv = sb("kv", [P, KC * NM + MC * D])
        kT = kv[:, 0:KC * NM].rearrange("p (c m) -> p c m", c=KC)
        vN = kv[:, KC * NM:].rearrange("p (c n) -> p c n", c=MC)
        qm = sb("qm", [P, KC * T])
        q = qm[:, :].rearrange("p (c t) -> p c t", c=KC)
        mn = qm[:, 0:KC * NM].rearrange("p (c m) -> p c m", c=KC)
        small = sb("small", [P, 320])

        WORK = 9152
        work = sb("work", [P, WORK])
        at = [0]

        def take(n):
            at[0] += n
            assert at[0] <= WORK, at[0]
            return work[:, at[0] - n:at[0]]

        PADP = HIST + TP
        pp = take(RC * PADP).rearrange("p (c t) -> p c t", c=RC)
        spool = take(RC * TS * 16).rearrange("p (c b t) -> p c b t", c=RC, b=TS)
        PADC = CW - 1 + TP
        cp = take(RC * PADC).rearrange("p (c t) -> p c t", c=RC)
        sconv = take(RC * TS * CW).rearrange("p (c b t) -> p c b t", c=RC, b=TS)
        gel = take(RC * T).rearrange("p (c t) -> p c t", c=RC)
        cv = take(RC * T).rearrange("p (c t) -> p c t", c=RC)
        wA = take(RC * 270)
        wB = take(RC * 270)
        lad = [wA.rearrange("p (c t) -> p c t", c=RC), wB.rearrange("p (c t) -> p c t", c=RC)]
        r_g = take(RC * T).rearrange("p (c t) -> p c t", c=RC)
        i_g = take(RC * T).rearrange("p (c t) -> p c t", c=RC)
        dd = wA[:, 0:RC * T].rearrange("p (c t) -> p c t", c=RC)
        ml = wB[:, 0:RC * T].rearrange("p (c t) -> p c t", c=RC)
        z = sq[:, 0:RC, :]
        ss = small[:, 0:RC * TS].rearrange("p (c b) -> p c b", c=RC)
        mx = small[:, 32:32 + 12]
        nmx = small[:, 44:44 + 12]
        sm = small[:, 56:56 + 12]
        rs = small[:, 68:68 + 12]

        at[0] = 0
        pr = take(3 * NH * NM).rearrange("p (t h m) -> p t h m", t=3, h=NH)
        pT = take(NH * MC * TP).rearrange("p (h c t) -> p h c t", h=NH, c=MC)
        qz = take(KC * TS * TS).rearrange("p (c b s) -> p c b s", c=KC, b=TS)
        pz = take(NH * MC * TS * TS).rearrange("p (h c b s) -> p h c b s", h=NH, c=MC, b=TS)
        o8 = take(D)
        at[0] = 0
        hT = take(FC * T).rearrange("p (c t) -> p c t", c=FC)
        sg = take(2 * T).rearrange("p (c t) -> p c t", c=2)
        at[0] = 0
        xtok = take(3 * D).rearrange("p (t n) -> p t n", t=3)
        xg = take(KC * CAP).rearrange("p (c s) -> p c s", c=KC)
        gsel = take(3 * CAP).rearrange("p (t s) -> p t s", t=3)
        wsel = take(3 * CAP).rearrange("p (t s) -> p t s", t=3)
        esg = take(2 * GW).rearrange("p (i n) -> p i n", i=2)
        eh = take(FE)
        ehT = take(FEC * CAP).rearrange("p (c s) -> p c s", c=FEC)
        eo = kv[:, 0:D]
        scat = kv[:, D:D + T]
        rt = kv[:, 2 * D:3 * D]
        lg = rt[:, 0:24].rearrange("p (t e) -> p t e", t=3)
        m8 = rt[:, 24:48].rearrange("p (t e) -> p t e", t=3)
        fi = rt[:, 48:72].rearrange("p (t e) -> p t e", t=3)
        ed = rt[:, 72:75]
        g1 = rt[:, 75:78]
        g2 = rt[:, 78:81]
        oh = rt[:, 81:105].rearrange("p (t e) -> p t e", t=3)
        msk = rt[:, 105:129].rearrange("p (t e) -> p t e", t=3)
        wts = rt[:, 129:129 + 72].rearrange("p (t b e) -> p t b e", t=3, b=MAXB)
        wcol = rt[:, 129:129 + 72].rearrange("p (t v) -> p t v", t=3)
        psm = rt[:, 201:201 + 72].rearrange("p (t b e) -> p t b e", t=3, b=MAXB)
        pcol = rt[:, 201:201 + 72].rearrange("p (t v) -> p t v", t=3)
        pos = rt[:, 273:305].rearrange("p (t e) -> p t e", t=4)
        cmax = rt[:, 305:306]
        g1a = rt[:, 306:309]
        i8 = sb("i8", [P, 3, 8], U32)
        need = sb("need", [P, 1], I32)

        ident = con[:, C_ID:C_ID + P]
        tri = con[:, C_TRI:C_TRI + P]
        iota = con[:, C_IOTA:C_IOTA + P]
        corr = con[:, C_CORR:C_CORR + 64].rearrange("p (g t) -> p g t", g=4)
        valid = con[:, C_VALID:C_VALID + 3]

        psum = [ctx.enter_context(nc.psum_tensor(f"bank{b}", [P, 512], F32)) for b in range(8)]

        bank_full = [sem(f"bank_full{b}") for b in range(8)]
        bank_read = [sem(f"bank_read{b}") for b in range(8)]
        slot_loaded = [sem(f"slot_loaded{s}") for s in range(NSLOT)]
        slab_used = sem("slab_used")
        pair_loaded = [sem(f"pair_loaded{i}") for i in range(2)]
        down_loaded = [sem(f"down_loaded{i}") for i in range(2)]
        block_used = sem("block_used")
        s_x = sem("x_loaded")
        s_vec = sem("vectors_loaded")
        s_mem = sem("mem_loaded")
        s_con = sem("consts_loaded")
        s_pw = sem("pool_w_loaded")
        s_gw = sem("gate_w_loaded")
        s_rw = sem("router_loaded")
        s_set = sem("constants_set")
        sq_ready = sem("squares_ready")
        xn_ready = sem("normed_ready")
        msq_ready = sem("mem_squares_ready")
        mem_normed = sem("mem_normed")
        mn_ready = sem("gained_memory_ready")
        padded = sem("histories_ready")
        cv_ready = sem("conv_ready")
        gates_ready = sem("gates_ready")
        z_ready = sem("pool_difference_ready")
        yr_ready = sem("y_rnn_ready")
        psq_ready = sem("y_pool_squares_ready")
        rsq_ready = sem("y_rnn_squares_ready")
        mixed_ready = sem("mixed_ready")
        decay_exp = sem("decay_exp_ready")
        decay_in = sem("decay_abs_ready")
        coef_ready = sem("decay_ready")
        h_last = sem("recurrence_ready")
        small_written = sem("small_outputs_written")
        kv_written = sem("keys_values_written")
        qz_ready = sem("sample_queries_ready")
        max_ready = sem("max_ready")
        exp_done = sem("exp_half_done")
        p_ready = sem("probs_ready")
        pz_ready = sem("sample_probs_ready")
        xos_ready = sem("sample_attended_ready")
        lmax_ready = sem("top_ready")
        lexp_ready = sem("gate_exp_ready")
        mask_ready = sem("mask_ready")
        route_ready = sem("route_ready")
        gsel_ready = sem("gather_matrix_ready")
        wsel_ready = sem("scatter_matrix_ready")
        x_final = sem("x_final")
        fsq_ready = sem("final_squares_ready")
        fsum_ready = sem("final_sum_ready")
        frms_ready = sem("final_rms_ready")
        y_ready = sem("y_ready")
        y_written = sem("y_written")
        dve_chain = sem("dve_chain")
        act_chain = sem("act_chain")
        pool_chain = sem("pool_chain")

        def col(name, l, c):
            k = l * LVEC + VEC[name] + c
            return vec[:, k:k + 1]

        def bank(n):
            return psum[n % 8]

        def slab(k):
            s = (k % NSLOT) * SLAB
            return ring[:, s:s + SLAB].rearrange("p (k n) -> p k n", k=8)

        def pair(i):
            return ring[:, i * PAIR:(i + 1) * PAIR].rearrange("p (i k n) -> p i k n", i=2, k=KC)

        down = ring[:, 2 * PAIR:4 * PAIR].rearrange("p (k n) -> p k n", k=FEC)

        def wait_full(eng, n, more=0):
            eng.wait_ge(bank_full[n % 8], n // 8 + 1 + 3 * more)

        def wait_read(eng, n, more=0):
            eng.wait_ge(bank_read[n % 8], n // 8 + 1 + 3 * more)

        block = ctx.enter_context(nc.Block())
        main = Pass(NT0, 0, NE)
        extra = Pass(main.end, NE, NE * (MAXB - 1))

        @block.sync
        def _(sp):
            sp.dma_start(x[:, :, :], xT).then_inc(s_x, 16)
            sp.dma_start(mem[:, :, :], memT).then_inc(s_mem, 16)

            def load(k, dram_k):
                s = k % NSLOT
                sp.dma_start(ring[:, s * SLAB:(s + 1) * SLAB], dense[dram_k]).then_inc(slot_loaded[s], 16)

            for k in range(NSLOT):
                load(k, k)
            rounds = NSLAB // NSLOT
            with sp.Fori(1, rounds) as r:
                for s in range(NSLOT):
                    sp.wait_ge(slab_used, NSLOT * (r - 1) + s + 1)
                    load(s, NSLOT * r + s)
            for k in range(rounds * NSLOT, NSLAB):
                sp.wait_ge(slab_used, k - NSLOT + 1)
                load(k, k)

            def load_pair(e, g):
                sp.dma_start(ring[:, (g % 2) * PAIR:(g % 2 + 1) * PAIR], experts[6 * e + g]).then_inc(pair_loaded[g % 2], 16)

            def load_down(e, i):
                sp.dma_start(ring[:, (2 + i) * PAIR:(3 + i) * PAIR], experts[6 * e + 4 + i]).then_inc(down_loaded[i], 16)

            def dense_gone(a, b):
                last = max(k for k in range(NSLAB) for s in [(k % NSLOT) * SLAB] if s < b and s + SLAB > a)
                sp.wait_ge(slab_used, last + 1)

            def block_loads(v, e):
                for g in range(4):
                    sp.wait_ge(block_used, 5 * v + g - 1 if g >= 2 else 5 * v + g - 2)
                    load_pair(e, g)
                for i in range(2):
                    sp.wait_ge(block_used, 5 * v)
                    load_down(e, i)

            for g in range(4):
                if g < 2:
                    dense_gone(g * PAIR, (g + 1) * PAIR)
                else:
                    sp.wait_ge(block_used, g - 1)
                load_pair(0, g)
                if g == 1:
                    for i in range(2):
                        dense_gone((2 + i) * PAIR, (3 + i) * PAIR)
                        load_down(0, i)
            with sp.Fori(1, NE) as v:
                block_loads(v, v)
            sp.wait_ge(route_ready, 1)
            count = sp.value_load(need[0:1, 0:1], min_val=0, max_val=T)
            with sp.If(count > CAP):
                for b in range(1, MAXB):
                    with sp.Fori(0, NE) as e:
                        block_loads(NE * b + e, e)
            with sp.Else():
                sp.nop()

        @block.tensor
        def _(pe):
            mm = nc.tensor.matmul

            def take_bank(n, more=0):
                if n >= 8:
                    pe.wait_ge(bank_read[n % 8], n // 8 + 3 * more)
                return bank(n)

            def wait_slab(k):
                pe.wait_ge(slot_loaded[k % NSLOT], 16 * (k // NSLOT + 1))
                return slab(k)

            def full(ins, n):
                ins.then_inc(bank_full[n % 8], 1)

            def uses_slab_before(ins, k):
                if k > 0:
                    ins.then_inc(slab_used, 1)

            def norm_sum(key, j):
                n = tiles[key]
                b = take_bank(n)
                for m in range(KC):
                    pe.wait_ge(sq_ready, KC * j + m + 1)
                    i = mm(b[:, 0:T], ones[:, :], sq[:, m, :], start=(m == 0), stop=(m == KC - 1))
                full(i, n)

            def project(key, l, src, width, ready=None, base=0):
                for m in range(12 if key == "in" else KC):
                    k = slabs[(key, l, m // 2)]
                    if m % 2 == 0:
                        w = wait_slab(k)
                    n = tiles[(key, l, m)]
                    b = take_bank(n)
                    for kc in range(KC):
                        if m == 0 and ready is not None:
                            pe.wait_ge(ready, base + kc + 1)
                        i = mm(b[:, 0:width], w[:, kc, (m % 2) * P:(m % 2 + 1) * P], src[:, kc, :],
                               start=(kc == 0), stop=(kc == KC - 1))
                        if m % 2 == 0 and kc == 0:
                            uses_slab_before(i, k)
                    full(i, n)

            pe.wait_ge(s_set, 2)
            n = tiles[("msq",)]
            b = take_bank(n)
            for m in range(KC):
                pe.wait_ge(msq_ready, m + 1)
                i = mm(b[:, 0:NM], ones[:, :], mn[:, m, :], start=(m == 0), stop=(m == KC - 1))
            full(i, n)
            for l in range(DEPTH):
                norm_sum(("ssq", 3 * l), 3 * l)
                project("in", l, xn, T, xn_ready, KC * 3 * l)
                project("mk", l, mn, NM, mn_ready, KC * l)
                if l == 0:
                    pe.wait_ge(s_gw, 16)
                    pe.wait_ge(s_pw, 16)
                    pe.wait_ge(s_con, 16)
                pe.wait_ge(cv_ready, l + 1)
                for gi, key in enumerate(("ga", "gx")):
                    for c in range(RC):
                        n = tiles[(key, l, c)]
                        b = take_bank(n)
                        full(mm(b[:, 0:T], gatew[:, l, gi, c, :], cv[:, c, :], start=True, stop=True), n)
                for s in range(4):
                    k = slabs[("mv", l, s)]
                    w = wait_slab(k)
                    for mc in range(MC):
                        n = tiles[("mv", l, s, mc)]
                        b = take_bank(n)
                        for kc in range(KC):
                            i = mm(b[:, 0:PIECE], mn[:, kc, mc * P:(mc + 1) * P], w[:, kc, :], start=(kc == 0), stop=(kc == KC - 1))
                            if mc == 0 and kc == 0:
                                uses_slab_before(i, k)
                        full(i, n)
                pe.wait_ge(z_ready, l + 1)
                for c in range(RC):
                    n = tiles[("pw", l, c)]
                    b = take_bank(n)
                    full(mm(b[:, 0:T], poolw[:, l, c, :], z[:, c, :], start=True, stop=True), n)
                for key, ready, o in (("psq", psq_ready, 0), ("rsq", rsq_ready, RC)):
                    n = tiles[(key, l)]
                    b = take_bank(n)
                    for c in range(RC):
                        pe.wait_ge(ready, RC * l + c + 1)
                        i = mm(b[:, 0:T], ones[:, :], sq[:, o + c, :], start=(c == 0), stop=(c == RC - 1))
                    full(i, n)
                project("out", l, xn, T, mixed_ready, KC * l)
                norm_sum(("ssq", 3 * l + 1), 3 * l + 1)
                project("mq", l, xn, T, xn_ready, KC * (3 * l + 1))
                for m in range(KC):
                    wait_read(pe, tiles[("mk", l, m)])
                    wait_read(pe, tiles[("mq", l, m)])
                for t in range(2):
                    for hp in range(2):
                        n = tiles[("sc", l, t, hp)]
                        b = take_bank(n)
                        for hh in range(2):
                            h = 2 * hp + hh
                            for c in range(HC):
                                i = mm(b[:, hh * NM:(hh + 1) * NM], q[:, HC * h + c, t * P:(t + 1) * P], kT[:, HC * h + c, :],
                                       start=(c == 0), stop=(c == HC - 1))
                        full(i, n)
                pe.wait_ge(qz_ready, l + 1)
                for h in range(NH):
                    n = tiles[("sc", l, 2, h // 2)]
                    if h % 2 == 0:
                        b = take_bank(n)
                    for half in range(2):
                        k = slabs[("kc", l, 2 * h + half)]
                        w = wait_slab(k)
                        for bb in range(4):
                            for c in range(HC):
                                i = mm(b[0:TS, (h % 2) * NM:(h % 2 + 1) * NM], qz[:, HC * h + c, 4 * half + bb, :], w[:, 2 * bb + c, :],
                                       start=(half + bb + c == 0), stop=(half * bb * c == 3))
                                if bb + c == 0:
                                    uses_slab_before(i, k)
                    if h % 2:
                        full(i, n)
                for h in range(NH):
                    n = tiles[("pt", l, h)]
                    b = take_bank(n)
                    for t in range(2):
                        pe.wait_ge(p_ready, 6 * l + 2 * t + h // 2 + 1)
                        for mc in range(MC):
                            i = nc.tensor.transpose(b[:, mc * TP + t * P:mc * TP + (t + 1) * P], pr[:, t, h, mc * P:(mc + 1) * P], ident)
                    full(i, n)
                for s in range(4):
                    for mc in range(MC):
                        wait_read(pe, tiles[("mv", l, s, mc)])
                for m in range(KC):
                    n = tiles[("pv", l, m)]
                    b = take_bank(n)
                    h = m // HC
                    wait_read(pe, tiles[("pt", l, h)])
                    for mc in range(MC):
                        i = mm(b[:, 0:TP], vN[:, mc, m * P:(m + 1) * P], pT[:, h, mc, :], start=(mc == 0), stop=(mc == MC - 1))
                    full(i, n)
                n = tiles[("pts", l)]
                b = take_bank(n)
                pe.wait_ge(p_ready, 6 * l + 6)
                for h in range(NH):
                    for mc in range(MC):
                        j = (h * MC + mc) * TS
                        i = nc.tensor.transpose(b[:, j:j + TS], pr[0:TS, 2, h, mc * P:(mc + 1) * P], ident[0:TS, 0:TS])
                full(i, n)
                pe.wait_ge(pz_ready, l + 1)
                for h in range(NH):
                    n = tiles[("pvs", l, h // 2)]
                    if h % 2 == 0:
                        b = take_bank(n)
                    for half in range(2):
                        k = slabs[("vc", l, 2 * h + half)]
                        w = wait_slab(k)
                        for bb in range(4):
                            for mc in range(MC):
                                i = mm(b[0:TS, (h % 2) * HD:(h % 2 + 1) * HD], pz[:, h, mc, 4 * half + bb, :], w[:, 2 * bb + mc, :],
                                       start=(half + bb + mc == 0), stop=(half * bb * mc == 3))
                                if bb + mc == 0:
                                    uses_slab_before(i, k)
                    if h % 2:
                        full(i, n)
                n = tiles[("ots", l)]
                b = take_bank(n)
                for hp in range(2):
                    wait_read(pe, tiles[("pvs", l, hp)])
                for c in range(KC):
                    i = nc.tensor.transpose(b[:, c * TS:(c + 1) * TS], o8[0:TS, c * P:(c + 1) * P], ident[0:TS, 0:TS])
                full(i, n)
                for m in range(KC):
                    wait_read(pe, tiles[("pv", l, m)])
                wait_read(pe, tiles[("ots", l)])
                project("mo", l, xn, T)
                norm_sum(("ssq", 3 * l + 2), 3 * l + 2)
                if l % 2 == 0:
                    for s in range(FC // 2):
                        for key in ("fg", "fu"):
                            k = slabs[(key, l, s)]
                            w = wait_slab(k)
                            for u in range(2):
                                n = tiles[(key, l, 2 * s + u)]
                                b = take_bank(n)
                                for kc in range(KC):
                                    if s == 0:
                                        pe.wait_ge(xn_ready, KC * (3 * l + 2) + kc + 1)
                                    i = mm(b[:, 0:T], w[:, kc, u * P:(u + 1) * P], xn[:, kc, :], start=(kc == 0), stop=(kc == KC - 1))
                                    if u == 0 and kc == 0:
                                        uses_slab_before(i, k)
                                full(i, n)
                    for mp in range(KC // 2):
                        nn = [tiles[("fd", l, 2 * mp + u)] for u in range(2)]
                        bb = [take_bank(n) for n in nn]
                        for kc in range(FC):
                            piece = mp * FC + kc
                            k = slabs[("fd", l, piece // 8)]
                            w = wait_slab(k) if piece % 8 == 0 else slab(k)
                            if mp == 0:
                                wait_read(pe, tiles[("fu", l, kc)])
                            for u in range(2):
                                i = mm(bb[u][:, 0:T], w[:, piece % 8, u * P:(u + 1) * P], hT[:, kc, :], start=(kc == 0), stop=(kc == FC - 1))
                                if kc == FC - 1:
                                    full(i, nn[u])
                                elif piece % 8 == 0 and u == 0:
                                    uses_slab_before(i, k)
            l = DEPTH - 1
            pe.wait_ge(s_rw, 16)
            n = tiles[("lg", l)]
            b = take_bank(n)
            pe.wait_ge(xn_ready, KC * (3 * l + 3))
            for t, (t0, rows) in enumerate(TOK):
                for kc in range(KC):
                    i = mm(b[0:rows, t * NE:(t + 1) * NE], xn[:, kc, t0:t0 + rows], rw[:, kc, :], start=(kc == 0), stop=(kc == KC - 1))
                    if t == 0 and kc == 0:
                        uses_slab_before(i, NSLAB)
            full(i, n)
            for t, (t0, rows) in enumerate(TOK):
                for hp in range(2):
                    n = tiles[("tk", l, t, hp)]
                    b = take_bank(n)
                    for c in range(4):
                        i = nc.tensor.transpose(b[0:rows, c * P:(c + 1) * P], xn[:, 4 * hp + c, t0:t0 + rows], ident)
                    full(i, n)
            n = tiles[("ps", l)]
            b = take_bank(n)
            pe.wait_ge(mask_ready, 1)
            for t in range(4):
                last = min(t, 2)
                for u in range(last + 1):
                    w = tri if u == t else ones[:, :]
                    i = mm(b[:, t * NE:(t + 1) * NE], w, msk[:, u, :], start=(u == 0), stop=(u == last))
            full(i, n)

            def gather(v, num):
                pe.wait_ge(gsel_ready, v + 1)
                for half in range(2):
                    n, more = num(f"X{half}")
                    b = take_bank(n, more)
                    for c in range(4):
                        for t, (t0, rows) in enumerate(TOK):
                            i = mm(b[:, c * P:(c + 1) * P], xtok[0:rows, t, (4 * half + c) * P:(4 * half + c + 1) * P], gsel[0:rows, t, :],
                                   start=(t == 0), stop=(t == 2))
                    full(i, n)

            def scatter(v, num, before, tail=False):
                n, more = num("S")
                b = take_bank(n, more)
                pe.wait_ge(wsel_ready, v + 1)
                for t, (t0, rows) in enumerate(TOK):
                    i = nc.tensor.transpose(b[:, t0:t0 + rows], wsel[0:rows, t, :], ident[0:rows, 0:rows])
                    if t == 0 and tail:
                        i.then_inc(block_used, 1)
                full(i, n)
                wait_read(pe, n, more)
                for u in range(2):
                    wait_read(pe, *before(f"D{u}"))
                for c in range(KC):
                    n, more = num(f"C{c}")
                    b = take_bank(n, more)
                    full(mm(b[:, 0:T], eo[:, c * P:(c + 1) * P], scat, start=True, stop=True), n)

            def turn_hidden(num, i3):
                n, more = num(f"T{i3}")
                b = take_bank(n, more)
                for g in ((0, 1), (2,), (3,))[i3]:
                    wait_read(pe, *num(f"U{g}"))
                for c in range(4 * i3, min(4 * i3 + 4, FEC)):
                    i = nc.tensor.transpose(b[:, (c % 4) * P:(c % 4 + 1) * P], eh[:, c * P:(c + 1) * P], ident)
                    if c % 4 == 0 and i3 < 2:
                        i.then_inc(block_used, 1)
                full(i, n)

            def expert(v, num, before, first, last):
                def group(g):
                    pe.wait_ge(pair_loaded[g % 2], 32 * v + 16 * (g // 2) + 16)
                    if g == 0:
                        for half in range(2):
                            wait_read(pe, *before(f"X{half}"))
                    for gi, name in enumerate("GU"):
                        n, more = num(f"{name}{g}")
                        b = take_bank(n, more)
                        for kc in range(KC):
                            i = mm(b[:, 0:GW], xg[:, kc, :], pair(g % 2)[:, gi, kc, :], start=(kc == 0), stop=(kc == KC - 1))
                            if gi == 0 and kc == 0 and (g in (1, 2) or (g == 0 and not first)):
                                i.then_inc(block_used, 1)
                        full(i, n)

                group(0)
                group(1)
                group(2)
                turn_hidden(num, 0)
                group(3)
                turn_hidden(num, 1)
                if not first:
                    scatter(v - 1, num, before)
                if not last:
                    gather(v + 1, num)
                turn_hidden(num, 2)
                nn = [num(f"D{u}") for u in range(2)]
                bb = [take_bank(*n) for n in nn]
                for kc in range(FEC):
                    if kc == 0:
                        pe.wait_ge(down_loaded[0], 16 * v + 16)
                    if kc == 5:
                        pe.wait_ge(down_loaded[1], 16 * v + 16)
                    if kc % 4 == 0:
                        wait_read(pe, *num(f"T{kc // 4}"))
                    for u in range(2):
                        i = mm(bb[u][:, :], ehT[:, kc, :], down[:, kc, u * 512:(u + 1) * 512], start=(kc == 0), stop=(kc == FEC - 1))
                        if kc == FEC - 1:
                            full(i, nn[u][0])

            def run_pass(p):
                v0, v1 = p.v0, p.v0 + p.nv - 1
                gather(v0, p.prologue)
                expert(v0, p.first, p.prologue, True, False)
                with pe.Fori(v0 + 1, v1) as v:
                    expert(v, p.middle(v), p.earlier(v), False, False)
                expert(v1, p.last, p.earlier(v1), False, True)
                scatter(v1, p.after, p.last, tail=True)

            for t in range(3):
                for hp in range(2):
                    wait_read(pe, tiles[("tk", l, t, hp)])
            run_pass(main)
            pe.wait_ge(route_ready, 1)
            count = pe.value_load(need[0:1, 0:1], min_val=0, max_val=T)
            with pe.If(count > CAP):
                run_pass(extra)
            with pe.Else():
                pe.nop()
            for m in range(KC):
                pe.wait_ge(fsq_ready, m + 1)
                i = mm(psum[0][:, 0:T], ones[:, :], sq[:, m, :], start=(m == 0), stop=(m == KC - 1))
            i.then_inc(fsum_ready, 1)

        @block.scalar
        def _(act):
            A = nc.scalar.activation
            act.dma_start(vec[:, :], vecs).then_inc(s_vec, 16)
            act.dma_start(con[:, :], consts).then_inc(s_con, 16)
            act.dma_start(gatew[:, :, :, :, :], gate_w).then_inc(s_gw, 16)
            act.dma_start(poolw[:, :, :, :], pool_w).then_inc(s_pw, 16)
            act.dma_start(rw[:, :, :], router_w).then_inc(s_rw, 16)
            chain = [0]

            def step(ins):
                chain[0] += 1
                ins.then_inc(act_chain, 1)
                return chain[0]

            def after(k):
                act.wait_ge(act_chain, k)

            def read(ins, n):
                ins.then_inc(bank_read[n % 8], 1)

            def squares(j, key=None, l=0):
                for m in range(KC):
                    if key is not None:
                        wait_read(act, tiles[(key, l, m)])
                    A(sq[:, m, :], x[:, m, :], ACT.Square).then_inc(sq_ready, 1)

            def root(n, width, scale, buf=0):
                wait_full(act, n)
                read(A(rms[:, buf, 0:width], bank(n)[:, 0:width], ACT.Sqrt, bias=eps[:, 0:1], scale=scale), n)

            act.wait_ge(s_set, 2)
            act.wait_ge(s_mem, 16)
            for m in range(KC):
                A(mn[:, m, :], mem[:, m, :], ACT.Square).then_inc(msq_ready, 1)
            act.wait_ge(s_x, 16)
            squares(0)
            root(tiles[("msq",)], NM, 1.0 / D, 1)
            for l in range(DEPTH):
                if l > 0:
                    squares(3 * l, "fd", l - 1)
                root(tiles[("ssq", 3 * l)], T, 1.0 / D)
                if l == 0:
                    act.wait_ge(decay_in, 1)
                    A(coef[:, 1, :], coef[:, 0, :], ACT.Exp).then_inc(decay_exp, 1)
                act.wait_ge(padded, l + 1)
                for m in range(12):
                    n = tiles[("in", l, m)]
                    wait_full(act, n)
                    c = m % RC
                    if m < RC:
                        A(cp[:, c, CW - 1:], bank(n)[:, 0:TP], ACT.Copy)
                        read(A(sconv[:, c, :, CW - 1], bank(n)[:, TP:T], ACT.Copy), n)
                    elif m < 2 * RC:
                        read(A(gel[:, c, :], bank(n)[:, 0:T], ACT.Gelu_apprx_tanh), n)
                    else:
                        A(pp[:, c, HIST:], bank(n)[:, 0:TP], ACT.Copy)
                        read(A(spool[:, c, :, 15], bank(n)[:, TP:T], ACT.Copy), n)
                if l > 0:
                    act.wait_ge(kv_written, 32 * l)
                for m in range(KC):
                    n = tiles[("mk", l, m)]
                    wait_full(act, n)
                    read(A(kT[:, m, :], bank(n)[:, 0:NM], ACT.Copy), n)
                for key, dst, name in (("ga", r_g, "gate_a_b"), ("gx", i_g, "gate_x_b")):
                    for c in range(RC):
                        n = tiles[(key, l, c)]
                        wait_full(act, n)
                        read(A(dst[:, c, :], bank(n)[:, 0:T], ACT.Sigmoid, bias=col(name, l, c)), n)
                act.wait_ge(coef_ready, 1)
                for c in range(RC):
                    wait_read(act, tiles[("ga", l, c)])
                    a = step(A(r_g[:, c, :], r_g[:, c, :], ACT.Tanh, scale=coef[:, 5, l * RC + c:l * RC + c + 1]))
                after(a)
                act.wait_ge(z_ready, l + 1)
                A(ml, r_g, ACT.Sqrt).then_inc(gates_ready, 1)
                for s in range(4):
                    for mc in range(MC):
                        n = tiles[("mv", l, s, mc)]
                        wait_full(act, n)
                        read(A(vN[:, mc, s * PIECE:(s + 1) * PIECE], bank(n)[:, 0:PIECE], ACT.Copy), n)
                for c in range(RC):
                    wait_read(act, tiles[("pw", l, c)])
                    A(sq[:, c, :], xn[:, c, :], ACT.Square).then_inc(psq_ready, 1)
                root(tiles[("psq", l)], T, 2.0 / D, 1)
                act.wait_ge(yr_ready, l + 1)
                for c in range(RC):
                    A(sq[:, RC + c, :], xn[:, RC + c, :], ACT.Square).then_inc(rsq_ready, 1)
                root(tiles[("rsq", l)], T, 2.0 / D)
                squares(3 * l + 1, "out", l)
                root(tiles[("ssq", 3 * l + 1)], T, 1.0 / D)
                for m in range(KC):
                    n = tiles[("mq", l, m)]
                    wait_full(act, n)
                    read(A(q[:, m, :], bank(n)[:, 0:T], ACT.Copy), n)
                for t in range(3):
                    rows = TOK[t][1]
                    for hp in range(2):
                        n = tiles[("sc", l, t, hp)]
                        act.wait_ge(max_ready, 6 * l + 2 * t + hp + 1)
                        for hh in range(2):
                            h = 2 * hp + hh
                            j = 4 * t + h
                            i = A(pr[0:rows, t, h, :], bank(n)[0:rows, hh * NM:(hh + 1) * NM], ACT.Exp,
                                  bias=nmx[0:rows, j:j + 1], scale=HD ** -0.5, accum_out=sm[0:rows, j:j + 1])
                            if hh:
                                read(i, n)
                            else:
                                i.then_inc(exp_done, 1)
                for h in range(NH):
                    n = tiles[("pt", l, h)]
                    wait_full(act, n)
                    read(A(pT[:, h, :, :].rearrange("p c t -> p (c t)"), bank(n)[:, :], ACT.Copy), n)
                for m in range(KC):
                    n = tiles[("pv", l, m)]
                    wait_full(act, n)
                    read(A(xn[:, m, 0:TP], bank(n)[:, 0:TP], ACT.Copy), n)
                squares(3 * l + 2, "mo", l)
                root(tiles[("ssq", 3 * l + 2)], T, 1.0 / D)
                if l % 2 == 0:
                    for m in range(FC):
                        n = tiles[("fg", l, m)]
                        wait_full(act, n)
                        if m >= 2:
                            wait_read(act, tiles[("fu", l, m - 2)])
                        read(A(sg[:, m % 2, :], bank(n)[:, 0:T], ACT.Silu), n)
            l = DEPTH - 1
            for t, (t0, rows) in enumerate(TOK):
                for hp in range(2):
                    n = tiles[("tk", l, t, hp)]
                    wait_full(act, n)
                    read(A(xtok[0:rows, t, hp * 512:(hp + 1) * 512], bank(n)[0:rows, :], ACT.Copy), n)
            act.wait_ge(lmax_ready, 1)
            A(ed, ed, ACT.Exp).then_inc(lexp_ready, 1)

            def gathered(num):
                for half in range(2):
                    n, more = num(f"X{half}")
                    wait_full(act, n, more)
                    read(A(xg[:, 4 * half:4 * half + 4, :].rearrange("p c s -> p (c s)"), bank(n)[:, :], ACT.Copy), n)

            def turned(num, i3):
                n, more = num(f"T{i3}")
                wait_full(act, n, more)
                k = min(4, FEC - 4 * i3)
                read(A(ehT[:, 4 * i3:4 * i3 + k, :].rearrange("p c s -> p (c s)"), bank(n)[:, 0:k * P], ACT.Copy), n)

            def scattered(num):
                n, more = num("S")
                wait_full(act, n, more)
                read(A(scat, bank(n)[:, 0:T], ACT.Copy), n)

            def expert(num, first, last):
                for g in range(4):
                    n, more = num(f"G{g}")
                    wait_full(act, n, more)
                    if g >= 2:
                        wait_read(act, *num(f"U{g - 2}"))
                    read(A(esg[:, g % 2, :], bank(n)[:, 0:GW], ACT.Silu), n)
                    if g >= 2:
                        turned(num, g - 2)
                if not first:
                    scattered(num)
                if not last:
                    gathered(num)
                turned(num, 2)
                for u in range(2):
                    n, more = num(f"D{u}")
                    wait_full(act, n, more)
                    read(A(eo[:, u * 512:(u + 1) * 512], bank(n)[:, :], ACT.Copy), n)

            def run_pass(p):
                v0, v1 = p.v0, p.v0 + p.nv - 1
                gathered(p.prologue)
                expert(p.first, True, False)
                with act.Fori(v0 + 1, v1) as v:
                    expert(p.middle(v), False, False)
                expert(p.last, False, True)
                scattered(p.after)

            run_pass(main)
            act.wait_ge(route_ready, 1)
            count = act.value_load(need[0:1, 0:1], min_val=0, max_val=T)
            with act.If(count > CAP):
                run_pass(extra)
            with act.Else():
                act.nop()
            act.wait_ge(x_final, 1)
            for m in range(KC):
                A(sq[:, m, :], x[:, m, :], ACT.Square).then_inc(fsq_ready, 1)
            act.wait_ge(fsum_ready, 1)
            A(rms[:, 0, :], psum[0][:, 0:T], ACT.Sqrt, bias=eps[:, 0:1], scale=1.0 / D).then_inc(frms_ready, 1)

        @block.vector
        def _(dve):
            V = nc.vector
            chain = [0]

            def step(ins):
                chain[0] += 1
                ins.then_inc(dve_chain, 1)
                return chain[0]

            def after(k):
                dve.wait_ge(dve_chain, k)

            def link(ins):
                after(step(ins))

            def read(ins, n):
                ins.then_inc(bank_read[n % 8], 1)

            def signal(ready):
                after(chain[0])
                dve.sem_inc(ready, 1)

            V.memset(ones[:, :], 1.0).then_inc(s_set, 1)
            V.memset(eps[:, :], EPS).then_inc(s_set, 1)

            dve.wait_ge(s_vec, 16)
            for l in range(DEPTH):
                k = l * LVEC + VEC["rglru_lambda"]
                link(V.tensor_scalar(coef[:, 5, l * RC:(l + 1) * RC], vec[:, k:k + RC], -1.0, 0.0, ALU.mult, ALU.max))
                link(V.tensor_scalar(coef[:, 0, l * RC:(l + 1) * RC], vec[:, k:k + RC], -1.0, None, ALU.mult))
                link(V.tensor_tensor(coef[:, 0, l * RC:(l + 1) * RC], coef[:, 0, l * RC:(l + 1) * RC], vec[:, k:k + RC], ALU.min))
            signal(decay_in)

            def invert(n, buf, width=T):
                wait_read(dve, n)
                link(V.reciprocal(rstd[:, buf, 0:width], rms[:, buf, 0:width]))

            def normed(j, l, name):
                invert(tiles[("ssq", j)], 0)
                for m in range(KC):
                    V.scalar_tensor_tensor(out=xn[:, m, :], in0=x[:, m, :], scalar=col(name, l, m), in1=rstd[:, 0, :],
                                           op0=ALU.mult, op1=ALU.mult).then_inc(xn_ready, 1)

            def residual(key, l):
                for m in range(KC):
                    n = tiles[(key, l, m)]
                    wait_full(dve, n)
                    read(V.tensor_tensor(x[:, m, :], bank(n)[:, 0:T], x[:, m, :], ALU.add), n)

            invert(tiles[("msq",)], 1, NM)
            for m in range(KC):
                V.tensor_tensor(mem[:, m, :], mem[:, m, :], rstd[:, 1, 0:NM], ALU.mult).then_inc(mem_normed, 1)
            for l in range(DEPTH):
                normed(3 * l, l, "norm_mix")
                if l == 0:
                    dve.wait_ge(decay_exp, 1)
                    e, s, s2, acc, out = (coef[:, i, :] for i in (1, 2, 3, 4, 5))
                    link(V.tensor_scalar(acc, e, 2.0, None, ALU.add))
                    link(V.reciprocal(acc, acc))
                    link(V.tensor_tensor(s, e, acc, ALU.mult))
                    link(V.tensor_tensor(s2, s, s, ALU.mult))
                    link(V.tensor_scalar(acc, s2, 1.0 / 19, None, ALU.mult))
                    for d in (17, 15, 13, 11, 9, 7, 5, 3):
                        link(V.scalar_tensor_tensor(out=acc, in0=acc, scalar=1.0 / d, in1=s2, op0=ALU.add, op1=ALU.mult))
                    link(V.scalar_tensor_tensor(out=acc, in0=acc, scalar=1.0, in1=s, op0=ALU.add, op1=ALU.mult))
                    link(V.scalar_tensor_tensor(out=out, in0=acc, scalar=2.0, in1=out, op0=ALU.mult, op1=ALU.add))
                    link(V.tensor_scalar(out, out, 4.0, None, ALU.mult))
                    signal(coef_ready)
                last = {}
                for k in range(CW):
                    for c in range(RC):
                        j = l * LVEC + VEC["conv_w"] + RC * k + c
                        w = vec[:, j:j + 1]
                        if k == 0:
                            wait_read(dve, tiles[("in", l, c)])
                            step(V.tensor_scalar(cv[:, c, 0:TP], cp[:, c, 0:TP], w, col("conv_b", l, c), ALU.mult, ALU.add))
                            last[c] = step(V.tensor_scalar(cv[:, c, TP:T], sconv[:, c, :, 0], w, col("conv_b", l, c), ALU.mult, ALU.add))
                        else:
                            after(last[c])
                            step(V.scalar_tensor_tensor(out=cv[:, c, 0:TP], in0=cp[:, c, k:k + TP], scalar=w, in1=cv[:, c, 0:TP],
                                                        op0=ALU.mult, op1=ALU.add))
                            last[c] = step(V.scalar_tensor_tensor(out=cv[:, c, TP:T], in0=sconv[:, c, :, k], scalar=w,
                                                                  in1=cv[:, c, TP:T], op0=ALU.mult, op1=ALU.add))
                signal(cv_ready)
                for c in range(RC):
                    wait_read(dve, tiles[("in", l, 2 * RC + c)])
                link(V.tensor_tensor(lad[0][:, :, 0:270], pp[:, :, 0:270], pp[:, :, 1:271], ALU.add))
                link(V.tensor_tensor(lad[1][:, 1:4, 0:268], lad[0][:, 1:4, 0:268], lad[0][:, 1:4, 2:270], ALU.add))
                link(V.tensor_tensor(lad[0][:, 2:4, 0:264], lad[1][:, 2:4, 0:264], lad[1][:, 2:4, 4:268], ALU.add))
                link(V.tensor_tensor(lad[1][:, 3, 0:256], lad[0][:, 3, 0:256], lad[0][:, 3, 8:264], ALU.add))
                if l == 0:
                    dve.wait_ge(s_con, 16)
                for g, w in enumerate(WINDOWS):
                    s = lad[g % 2][:, g, 16 - w:16 - w + TP]
                    step(V.tensor_reduce(ss[:, g, :], spool[:, g, :, 16 - w:16], AX_X, ALU.add))
                    k = step(V.tensor_tensor(s[:, 0:16], s[:, 0:16], corr[:, g, :], ALU.mult))
                after(k)
                for g, w in enumerate(WINDOWS):
                    s = lad[g % 2][:, g, 16 - w:16 - w + TP]
                    step(V.scalar_tensor_tensor(out=z[:, g, 0:TP], in0=s, scalar=1.0 / w, in1=pp[:, g, HIST:], op0=ALU.mult, op1=ALU.subtract))
                    step(V.scalar_tensor_tensor(out=z[:, g, TP:T], in0=ss[:, g, :], scalar=1.0 / w, in1=spool[:, g, :, 15],
                                                op0=ALU.mult, op1=ALU.subtract))
                signal(z_ready)
                dve.wait_ge(gates_ready, l + 1)
                k1 = step(V.tensor_scalar(dd, r_g, 1.0, None, ALU.add))
                for c in range(RC):
                    wait_read(dve, tiles[("gx", l, c)])
                step(V.tensor_tensor(i_g, i_g, cv, ALU.mult))
                after(k1)
                link(V.reciprocal(dd, dd))
                k3 = step(V.scalar_tensor_tensor(out=ml, in0=ml, scalar=2.0, in1=dd, op0=ALU.mult, op1=ALU.mult))
                step(V.tensor_scalar(r_g, dd, 2.0, -1.0, ALU.mult, ALU.add))
                after(k3)
                link(V.memset(ml[:, :, 0:1], 1.0))
                link(V.tensor_tensor(i_g, i_g, ml, ALU.mult))
                o = VEC_H0 + l * RC * TS
                h0 = vec[:, o:o + RC * TS].rearrange("p (c b) -> p c b", c=RC)
                k = step(V.tensor_tensor(cv[:, :, TP:T], r_g[:, :, TP:T], h0, ALU.mult))
                for c in range(RC):
                    step(V.tensor_tensor_scan(cv[:, c, 0:TP], r_g[:, c, 0:TP], i_g[:, c, 0:TP], 0.0, ALU.mult, ALU.add))
                after(k)
                step(V.tensor_tensor(cv[:, :, TP:T], cv[:, :, TP:T], i_g[:, :, TP:T], ALU.add))
                signal(h_last)
                for c in range(RC):
                    wait_read(dve, tiles[("in", l, RC + c)])
                wait_full(dve, tiles[("in", l, 11)])
                V.tensor_tensor(xn[:, RC:KC, :], cv, gel, ALU.mult).then_inc(yr_ready, 1)
                for c in range(RC):
                    n = tiles[("pw", l, c)]
                    wait_full(dve, n)
                    read(V.tensor_scalar(xn[:, c, :], bank(n)[:, 0:T], col("pool_scale", l, c), None, ALU.mult), n)
                for key, name, o, buf in (("psq", "out_norm_pool", 0, 1), ("rsq", "out_norm_rnn", RC, 0)):
                    invert(tiles[(key, l)], buf)
                    for c in range(RC):
                        V.scalar_tensor_tensor(out=xn[:, o + c, :], in0=xn[:, o + c, :], scalar=col(name, l, c), in1=rstd[:, buf, :],
                                               op0=ALU.mult, op1=ALU.mult).then_inc(mixed_ready, 1)
                dve.wait_ge(small_written, 96 * (l + 1))
                step(V.memset(qz, 0.0))
                step(V.memset(pz, 0.0))
                residual("out", l)
                normed(3 * l + 1, l, "norm_mem")
                after(chain[0])
                for c in range(KC):
                    wait_read(dve, tiles[("mq", l, c)])
                    step(V.tensor_copy(qz[:, c, :, :].rearrange("p b s -> p (b s)")[:, 0:64:TS + 1], q[:, c, TP:T]))
                signal(qz_ready)
                for t in range(3):
                    rows = TOK[t][1]
                    for hp in range(2):
                        n = tiles[("sc", l, t, hp)]
                        j = 4 * t + 2 * hp
                        wait_full(dve, n)
                        link(V.tensor_reduce(mx[0:rows, j:j + 2], bank(n)[0:rows, :].rearrange("p (h m) -> p h m", h=2), AX_X, ALU.max))
                        V.tensor_scalar(nmx[0:rows, j:j + 2], mx[0:rows, j:j + 2], -(HD ** -0.5), None, ALU.mult).then_inc(max_ready, 1)
                    for hp in range(2):
                        j = 4 * t + 2 * hp
                        dve.wait_ge(exp_done, 6 * l + 2 * t + hp + 1)
                        wait_read(dve, tiles[("sc", l, t, hp)])
                        link(V.reciprocal(rs[0:rows, j:j + 2], sm[0:rows, j:j + 2]))
                        for hh in range(2):
                            h = 2 * hp + hh
                            step(V.tensor_scalar(pr[0:rows, t, h, :], pr[0:rows, t, h, :], rs[0:rows, j + hh:j + hh + 1], None, ALU.mult))
                        signal(p_ready)
                n = tiles[("pts", l)]
                wait_full(dve, n)
                for h in range(NH):
                    for mc in range(MC):
                        j = (h * MC + mc) * TS
                        i = V.tensor_copy(pz[:, h, mc, :, :].rearrange("p b s -> p (b s)")[:, 0:64:TS + 1], bank(n)[:, j:j + TS])
                        if h * MC + mc == NH * MC - 1:
                            read(i, n)
                        else:
                            step(i)
                wait_read(dve, n)
                signal(pz_ready)
                for hp in range(2):
                    n = tiles[("pvs", l, hp)]
                    wait_full(dve, n)
                    read(V.tensor_copy(o8[0:TS, hp * 512:(hp + 1) * 512], bank(n)[0:TS, :]), n)
                n = tiles[("ots", l)]
                wait_full(dve, n)
                read(V.tensor_copy(xn[:, :, TP:T], bank(n)[:, 0:KC * TS].rearrange("p (c b) -> p c b", c=KC)), n)
                residual("mo", l)
                normed(3 * l + 2, l, "norm_ffn")
                if l % 2 == 0:
                    for m in range(FC):
                        n = tiles[("fu", l, m)]
                        wait_read(dve, tiles[("fg", l, m)])
                        wait_full(dve, n)
                        read(V.tensor_tensor(hT[:, m, :], bank(n)[:, 0:T], sg[:, m % 2, :], ALU.mult), n)
                    residual("fd", l)
            l = DEPTH - 1
            dve.wait_ge(kv_written, 32 * DEPTH)
            link(V.memset(rt[:, 0:320], 0.0))
            n = tiles[("lg", l)]
            wait_full(dve, n)
            for t, (t0, rows) in enumerate(TOK):
                i = V.tensor_copy(lg[0:rows, t, :], bank(n)[0:rows, t * NE:(t + 1) * NE])
                if t == 2:
                    read(i, n)
                else:
                    step(i)
            wait_read(dve, n)
            after(chain[0])
            for t in range(3):
                link(V.max(out=m8[:, t, :], in_=lg[:, t, :]))
                link(V.max_index(i8[:, t, :], m8[:, t, :], lg[:, t, :]))
            link(V.tensor_copy(fi, i8[:, :, :]))
            V.tensor_tensor(ed, m8[:, :, 1], m8[:, :, 0], ALU.subtract).then_inc(lmax_ready, 1)
            dve.wait_ge(lexp_ready, 1)
            link(V.tensor_scalar(g1a, ed, 1.0, None, ALU.add))
            link(V.reciprocal(g1, g1a))
            link(V.tensor_tensor(g2, ed, g1, ALU.mult))
            for t in range(3):
                link(V.tensor_scalar(oh[:, t, :], iota[:, 0:NE], fi[:, t, 0:1], valid[:, t:t + 1], ALU.is_equal, ALU.mult))
                link(V.tensor_scalar(msk[:, t, :], iota[:, 0:NE], fi[:, t, 1:2], valid[:, t:t + 1], ALU.is_equal, ALU.mult))
                link(V.tensor_scalar(wts[:, t, 0, :], oh[:, t, :], g1[:, t:t + 1], None, ALU.mult))
                link(V.scalar_tensor_tensor(out=wts[:, t, 0, :], in0=msk[:, t, :], scalar=g2[:, t:t + 1], in1=wts[:, t, 0, :],
                                            op0=ALU.mult, op1=ALU.add))
                link(V.tensor_tensor(msk[:, t, :], msk[:, t, :], oh[:, t, :], ALU.add))
                for b in range(1, MAXB):
                    step(V.tensor_copy(wts[:, t, b, :], wts[:, t, 0, :]))
            signal(mask_ready)
            n = tiles[("ps", l)]
            wait_full(dve, n)
            read(V.tensor_copy(pos, bank(n)[:, 0:32].rearrange("p (t e) -> p t e", t=4)), n)
            wait_read(dve, n)
            link(V.tensor_reduce(cmax, pos[:, 3, :], AX_X, ALU.max))
            link(V.tensor_copy(need[:, :], cmax))
            link(V.scalar_tensor_tensor(out=psm[:, :, 0, :], in0=pos[:, 0:3, :], scalar=1.0, in1=msk, op0=ALU.add, op1=ALU.mult))
            for b in range(MAXB - 1, -1, -1):
                link(V.tensor_scalar(psm[:, :, b, :], psm[:, :, 0, :], -1.0 - CAP * b, None, ALU.add))
            signal(route_ready)

            def gather_matrix(v):
                for t in range(3):
                    i = V.tensor_scalar(gsel[:, t, :], iota, pcol[:, t, bass.ds(v, 1)], None, ALU.is_equal)
                i.then_inc(gsel_ready, 1)

            def scatter_matrix(v):
                for t in range(3):
                    i = V.tensor_scalar(wsel[:, t, :], iota, pcol[:, t, bass.ds(v, 1)], wcol[:, t, bass.ds(v, 1)],
                                        ALU.is_equal, ALU.mult)
                i.then_inc(wsel_ready, 1)

            def combine(num):
                for c in range(KC):
                    n, more = num(f"C{c}")
                    wait_full(dve, n, more)
                    read(V.tensor_tensor(x[:, c, :], bank(n)[:, 0:T], x[:, c, :], ALU.add), n)

            def expert(v, num, before, first, last):
                if not last:
                    wait_full(dve, *before("X1"))
                    gather_matrix(v + 1)
                for g in range(4):
                    n, more = num(f"U{g}")
                    wait_read(dve, *num(f"G{g}"))
                    wait_full(dve, n, more)
                    if g == 0 and not first:
                        wait_full(dve, *before("T2"))
                    read(V.tensor_tensor(eh[:, g * GW:(g + 1) * GW], bank(n)[:, 0:GW], esg[:, g % 2, :], ALU.mult), n)
                if not first:
                    combine(num)
                scatter_matrix(v)

            def run_pass(p):
                v0, v1 = p.v0, p.v0 + p.nv - 1
                gather_matrix(v0)
                expert(v0, p.first, p.prologue, True, False)
                with dve.Fori(v0 + 1, v1) as v:
                    expert(v, p.middle(v), p.earlier(v), False, False)
                expert(v1, p.last, p.earlier(v1), False, True)
                combine(p.after)

            run_pass(main)
            count = dve.value_load(need[0:1, 0:1], min_val=0, max_val=T)
            with dve.If(count > CAP):
                run_pass(extra)
            with dve.Else():
                dve.nop()
            dve.drain().then_inc(x_final, 1)
            dve.wait_ge(frms_ready, 1)
            link(V.reciprocal(rstd[:, 0, :], rms[:, 0, :]))
            for m in range(KC):
                k = VEC_FINAL + m
                V.scalar_tensor_tensor(out=xn[:, m, :], in0=x[:, m, :], scalar=vec[:, k:k + 1], in1=rstd[:, 0, :], op0=ALU.mult,
                                       op1=ALU.mult).then_inc(y_ready, 1)

        @block.gpsimd
        def _(pool):
            G = nc.gpsimd
            pool.wait_ge(s_vec, 16)
            for l in range(DEPTH):
                if l > 0:
                    for m in range(KC):
                        wait_read(pool, tiles[("fd", l - 1, m)])
                G.memset(pp[:, :, 0:HIST], 0.0).then_inc(pool_chain, 1)
                G.memset(cp[:, :, 0:CW - 1], 0.0).then_inc(pool_chain, 1)
                o = VEC_POOL + l * RC * TS * HIST
                hist = vec[:, o:o + RC * TS * HIST].rearrange("p (c b t) -> p c b t", c=RC, b=TS)
                o = VEC_CONV + l * RC * TS * (CW - 1)
                taps = vec[:, o:o + RC * TS * (CW - 1)].rearrange("p (c b t) -> p c b t", c=RC, b=TS)
                G.tensor_copy(spool[:, :, :, 0:HIST], hist).then_inc(pool_chain, 1)
                G.tensor_copy(sconv[:, :, :, 0:CW - 1], taps).then_inc(pool_chain, 1)
                pool.wait_ge(pool_chain, 4 * (l + 1))
                pool.sem_inc(padded, 1)
                if l == 0:
                    pool.wait_ge(mem_normed, KC)
                for m in range(KC):
                    G.tensor_scalar(mn[:, m, :], mem[:, m, :], col("mem_norm", l, m), None, ALU.mult).then_inc(mn_ready, 1)
                for m in range(12):
                    wait_read(pool, tiles[("in", l, m)])
                pool.wait_ge(h_last, l + 1)
                for src, o, shape in ((pp[:, :, TP:TP + HIST], O_PP, (HIST,)), (cp[:, :, TP:TP + CW - 1], O_PC, (CW - 1,)),
                                      (cv[:, :, TP - 1:TP], O_PH, (1,)), (spool[:, :, :, 1:16], O_SP, (TS, HIST)),
                                      (sconv[:, :, :, 1:CW], O_SC, (TS, CW - 1)), (cv[:, :, TP:T], O_SH, (TS,))):
                    size = RC
                    for d in shape:
                        size *= d
                    dst = o_small[l][:, o:o + size]
                    dst = dst.rearrange("p (c t) -> p c t", c=RC) if len(shape) == 1 else \
                        dst.rearrange("p (c b t) -> p c b t", c=RC, b=TS)
                    with nc.allow_non_contiguous_dma(reason="one value per channel"):
                        pool.dma_start(dst, src).then_inc(small_written, 16)
                for m in range(KC):
                    wait_read(pool, tiles[("mk", l, m)])
                pool.dma_start(o_k[l], kT).then_inc(kv_written, 16)
                for s in range(4):
                    for mc in range(MC):
                        wait_read(pool, tiles[("mv", l, s, mc)])
                pool.dma_start(o_v[l], vN).then_inc(kv_written, 16)
            pool.wait_ge(y_ready, KC)
            pool.dma_start(o_y, xn[:, :, :]).then_inc(y_written, 16)
            pool.wait_ge(small_written, 96 * DEPTH)
            pool.wait_ge(kv_written, 32 * DEPTH)
            pool.wait_ge(y_written, 16)


def kernel(**inputs):
    import numpy as np
    import concourse.bacc as bacc
    from concourse.bass_utils import run_bass_kernel_spmd as run

    a = {k: np.asarray(v) for k, v in inputs.items()}

    def feat(m):
        r, f = m.shape
        return m.reshape(r, f // P, P).transpose(2, 1, 0)

    xs = feat(np.concatenate([a["x_prompt"].reshape(TP, D), a["x_sample"].reshape(TS, D)]))
    ms = feat(a["mem_prompt"].reshape(NM, D))
    cols = []
    for l in range(DEPTH):
        for name in ("norm_mix", "norm_mem", "mem_norm", "norm_ffn", "out_norm_pool", "out_norm_rnn", "pool_scale",
                     "conv_w", "conv_b", "gate_a_b", "gate_x_b", "rglru_lambda"):
            cols.append(a[name][l].reshape(-1, P).T)
    cols.append(a["final_norm"].reshape(-1, P).T)
    cols.append(a["state_h"].reshape(DEPTH, TS, RC, P).transpose(3, 0, 2, 1).reshape(P, -1))
    cols.append(a["state_conv"].reshape(DEPTH, TS, CW - 1, RC, P).transpose(4, 0, 3, 1, 2).reshape(P, -1))
    cols.append(a["state_pool"].reshape(DEPTH, TS, HIST, RC, P).transpose(4, 0, 3, 1, 2).reshape(P, -1))
    vecs = np.concatenate(cols, axis=1)

    con = np.zeros((P, NCONST), np.float32)
    con[:, C_ID:C_ID + P] = np.eye(P)
    con[:, C_TRI:C_TRI + P] = np.triu(np.ones((P, P)), 1)
    con[:, C_IOTA:C_IOTA + P] = np.arange(P)
    for g, w in enumerate(WINDOWS):
        con[:, C_CORR + 16 * g:C_CORR + 16 * g + 16] = w / np.minimum(np.arange(16) + 1, w)
    for t, (_, rows) in enumerate(TOK):
        con[:rows, C_VALID + t] = 1

    pw = a["pool_w"].transpose(2, 0, 1, 3)
    gw = np.zeros((P, DEPTH, 2, RC, P), np.float32)
    for i, name in enumerate(("gate_a_w", "gate_x_w")):
        w = a[name].reshape(DEPTH, RC, 2, 64, 64)
        for j in range(2):
            gw[64 * j:64 * j + 64, :, i, :, 64 * j:64 * j + 64] = w[:, :, j].transpose(2, 0, 1, 3)
    rw = a["router_w"][0].reshape(KC, P, NE).transpose(1, 0, 2)

    def columns(w, s):
        return w[:, s * PIECE:(s + 1) * PIECE].reshape(KC, P, PIECE).transpose(1, 0, 2)

    dense = np.empty((len(stream_plan()), P, 8, PIECE), np.float32)
    order = np.r_[D // 2:D, D:3 * D // 2, 0:D // 2]
    names = {"mk": "w_mk", "mv": "w_mv", "out": "w_out", "mq": "w_mq", "mo": "w_mo"}
    win = a["w_in"][:, :, order]
    ck = a["cache_mem_k"].reshape(DEPTH, 2, 4, NM, NH, HC, P)
    cvv = a["cache_mem_v"].reshape(DEPTH, 2, 4, MC, P, NH, HD)
    fd = a["ffn_w_down"].reshape(-1, FC, P, KC // 2, PIECE).transpose(0, 3, 1, 2, 4)
    for k, (kind, l, s) in enumerate(stream_plan()):
        if kind in names:
            dense[k] = columns(a[names[kind]][l], s)
        elif kind == "in":
            dense[k] = columns(win[l], s)
        elif kind == "fg":
            dense[k] = columns(a["ffn_w_gate"][l // 2], s)
        elif kind == "fu":
            dense[k] = columns(a["ffn_w_up"][l // 2], s)
        elif kind == "kc":
            dense[k] = ck[l, s % 2, :, :, s // 2].transpose(3, 0, 2, 1).reshape(P, 8, NM)
        elif kind == "vc":
            dense[k] = cvv[l, s % 2, :, :, :, s // 2].transpose(2, 0, 1, 3).reshape(P, 8, HD)
        else:
            dense[k] = fd[l // 2].reshape(-1, P, PIECE)[8 * s:8 * s + 8].transpose(1, 0, 2)

    ex = np.empty((NE, 6, P, PAIR), np.float32)
    for i, name in enumerate(("moe_w_gate", "moe_w_up")):
        w = a[name][0].reshape(NE, KC, P, 4, GW).transpose(0, 3, 2, 1, 4)
        ex[:, 0:4].reshape(NE, 4, P, 2, KC, GW)[:, :, :, i] = w
    w = a["moe_w_down"][0].reshape(NE, FEC, P, D).transpose(0, 2, 1, 3).reshape(NE, P, 2, PAIR)
    ex[:, 4:6] = w.transpose(0, 2, 1, 3)

    arrays = {"xT": xs, "memT": ms, "vecs": vecs, "consts": con, "pool_w": pw, "gate_w": gw, "router_w": rw,
              "dense": dense.reshape(-1, P, SLAB), "experts": ex.reshape(NE * 6, P, PAIR)}
    arrays = {k: np.ascontiguousarray(v) for k, v in arrays.items()}
    nc = bacc.Bacc("TRN2", target_bir_lowering=False, num_devices=1)
    args = [nc.dram_tensor(k, v.shape, F32, kind="ExternalInput").ap() for k, v in arrays.items()]
    outs = {"o_y": (P, KC, T), "o_small": (DEPTH, P, NOUT), "o_k": (DEPTH, P, KC, NM), "o_v": (DEPTH, P, MC, D)}
    args += [nc.dram_tensor(k, s, F32, kind="ExternalOutput").ap() for k, s in outs.items()]
    trunk_kernel(nc, *args)
    r = run(nc, [arrays], core_ids=[0]).results[0]

    y = r["o_y"].transpose(2, 1, 0).reshape(T, D)
    sm = r["o_small"]

    def part(o, *dims):
        size = RC * int(np.prod(dims))
        return sm[:, :, o:o + size].reshape(DEPTH, P, RC, *dims)

    half = D // 2
    pool_p = part(O_PP, HIST).transpose(0, 3, 2, 1).reshape(DEPTH, 1, HIST, half)
    conv_p = part(O_PC, CW - 1).transpose(0, 3, 2, 1).reshape(DEPTH, 1, CW - 1, half)
    h_p = part(O_PH).transpose(0, 2, 1).reshape(DEPTH, 1, half)
    pool_s = part(O_SP, TS, HIST).transpose(0, 3, 4, 2, 1).reshape(DEPTH, TS, HIST, half)
    conv_s = part(O_SC, TS, CW - 1).transpose(0, 3, 4, 2, 1).reshape(DEPTH, TS, CW - 1, half)
    h_s = part(O_SH, TS).transpose(0, 3, 2, 1).reshape(DEPTH, TS, half)
    mk = r["o_k"].transpose(0, 3, 2, 1).reshape(DEPTH, 1, NM, NH, HD)
    mv = r["o_v"].transpose(0, 2, 1, 3).reshape(DEPTH, 1, NM, NH, HD)
    return (y[:TP].reshape(1, TP, D), y[TP:].reshape(TS, 1, D), pool_p, conv_p, h_p, mk, mv, pool_s, conv_s, h_s)
```

```python
from contextlib import ExitStack

import concourse.bass as bass
from concourse import mybir

ALU = mybir.AluOpType
ACT = mybir.ActivationFunctionType
F32 = mybir.dt.float32
F32R = mybir.dt.float32r
U32 = mybir.dt.uint32
I32 = mybir.dt.int32
AX_X = mybir.AxisListType.X

P = 128
D = 1024
KC = D // P
TP, TS = 256, 8
T = TP + TS
DEPTH = 2
NM = 256
MC = NM // P
NH, HD = 4, 256
HC = HD // P
WINDOWS = (2, 4, 8, 16)
HIST = 15
CW = 4
RC = 4
FF = 2816
FC = FF // P
NE = 8
FE = FF // 2
FEC = FE // P
EPS = 1e-6

PIECE = 256
UNIT = 4 * PIECE
GW = FE // 4
EUNIT = KC // 2 * GW
ESLOTS = 6
RING = ESLOTS * EUNIT
SLOTS = RING // UNIT
NBUF = 3
EUNITS = 24
assert 4 * KC * GW * 2 // EUNIT == 16 and FEC * D // EUNIT == 8 and EUNITS % ESLOTS == 0 and EUNITS % NBUF == 0
HALVES = [(0, 12), (12, 22)]

VEC = {}
_n = 0
for _name, _cols in (("norm_mix", 8), ("norm_mem", 8), ("mem_norm", 8), ("norm_ffn", 8), ("out_norm_pool", 4),
                     ("out_norm_rnn", 4), ("pool_scale", 4), ("conv_w", 16), ("conv_b", 4), ("gate_a_b", 4),
                     ("gate_x_b", 4), ("rglru_lambda", 4)):
    VEC[_name] = _n
    _n += _cols
LVEC = _n
VEC_FINAL = DEPTH * LVEC
VEC_H0 = VEC_FINAL + KC
NVEC = VEC_H0 + DEPTH * RC * TS
C_ID, C_TRI, C_IOTA, C_CORR, C_VALID = 0, P, 2 * P, 3 * P, 3 * P + 4 * 16
NCONST = C_VALID + 3
O_PP = 0
O_PC = O_PP + RC * HIST
O_PH = O_PC + RC * (CW - 1)
O_SP = O_PH + RC
O_SC = O_SP + RC * TS * HIST
O_SH = O_SC + RC * TS * (CW - 1)
NOUT = O_SH + RC * TS

TOK = [(0, P), (P, P), (TP, TS)]
BLOCKS = NE
MAXB = (T + P - 1) // P
CAP = P


def stream_plan():
    out = []

    def add(kind, l, n):
        out.extend((kind, l, i) for i in range(n))

    for l in range(DEPTH):
        for kind, n in (("in", 12), ("mk", 8), ("mv", 8), ("out", 8), ("mq", 8), ("kc", 16), ("vc", 16), ("mo", 8)):
            add(kind, l, n)
        if l % 2 == 0:
            for half, (c0, c1) in enumerate(HALVES):
                for s in range(c0 // 2, c1 // 2):
                    out += [("fg", l, 2 * s), ("fg", l, 2 * s + 1), ("fu", l, 2 * s), ("fu", l, 2 * s + 1)]
                add(f"fd{half}", l, (c1 - c0))
    return out


RAW = ("kc", "vc")


def bank_plan():
    out = []
    for l in range(DEPTH):
        out += [("ssq", 3 * l)]
        out += [("in", l, m) for m in range(6)]
        if l == 0:
            out += [("msq",)]
        out += [("in", l, m) for m in range(6, 12)]
        out += [("mk", l, m) for m in range(8)]
        out += [("ga", l, c) for c in range(RC)] + [("gx", l, c) for c in range(RC)]
        out += [("mv", l, s, mc) for s in range(4) for mc in range(MC)]
        out += [("pw", l, c) for c in range(RC)]
        out += [("psq", l), ("rsq", l)]
        out += [("out", l, m) for m in range(KC)]
        out += [("ssq", 3 * l + 1)]
        out += [("mq", l, m) for m in range(KC)]
        out += [("sc", l, t, hp) for t in range(3) for hp in range(2)]
        out += [("pt", l, h) for h in range(NH)]
        out += [("pv", l, m) for m in range(KC)]
        out += [("pts", l)]
        out += [("pvs", l, hp) for hp in range(2)]
        out += [("ots", l)]
        out += [("mo", l, m) for m in range(KC)]
        out += [("ssq", 3 * l + 2)]
        if l % 2 == 0:
            for half, (c0, c1) in enumerate(HALVES):
                for s in range(c0 // 2, c1 // 2):
                    out += [("fg", l, 2 * s), ("fg", l, 2 * s + 1), ("fu", l, 2 * s), ("fu", l, 2 * s + 1)]
                out += [(f"fd{half}", l, m) for m in range(KC)]
        else:
            out += [("lg", l)]
            out += [("tk", l, t, hp) for t in range(3) for hp in range(2)]
            out += [("ps", l)]
    return out


def trunk_kernel(nc, xT, memT, vecs, taps, hists, consts, pool_w, gate_w, router_w, dense, experts,
                 o_y, o_small, o_k, o_v):
    units = {name: k for k, name in enumerate(stream_plan())}
    split = {name: k for k, name in enumerate(x for x in stream_plan() if x[0] not in RAW)}
    tiles = {name: n for n, name in enumerate(bank_plan())}
    NUNIT = len(units)
    NSPLIT = len(split)
    NT0 = len(tiles)

    HIDDEN = ["G0", "U0", "G1", "U1", "G2", "U2", "T0", "S", "G3", "U3", "T1"]
    COMBINE = [f"C{c}" for c in range(KC)]
    OUTPUT = ["X0", "X1", "T2", "D0", "D1"]
    MID = HIDDEN + COMBINE + OUTPUT
    FIRST = [x for x in HIDDEN if x != "S"] + OUTPUT
    LAST = [x for x in MID if x[0] != "X"]
    TAIL = ["S"] + COMBINE
    assert len(MID) == 24

    class Pass:

        def __init__(self, n0, v0, nv):
            self.n0, self.v0, self.nv = n0, v0, nv
            self.mid = n0 + 2 + len(FIRST)
            self.tail = self.mid + len(MID) * (nv - 2) + len(LAST)
            self.end = self.tail + len(TAIL)

        def first(self, kind):
            return self.n0 + 2 + FIRST.index(kind), 0

        def middle(self, v):
            return lambda kind: (self.mid + MID.index(kind), v - (self.v0 + 1))

        def last(self, kind):
            return self.mid + len(MID) * (self.nv - 2) + LAST.index(kind), 0

        def after(self, kind):
            return self.tail + TAIL.index(kind), 0

        def earlier(self, v):
            return lambda kind: (self.mid + MID.index(kind) - len(MID), v - (self.v0 + 1))

        def prologue(self, kind):
            return self.n0 + int(kind[1]), 0

    with ExitStack() as ctx:
        def sb(name, shape, dt=F32):
            return ctx.enter_context(nc.sbuf_tensor(name, shape, dt))

        def sem(name):
            return ctx.enter_context(nc.semaphore(name))

        ring = sb("ring", [P, RING])
        x = sb("x", [P, KC, T])
        sq = sb("sq", [P, KC, T])
        xh = sb("xh", [P, KC * T], F32R)
        xl = sb("xl", [P, KC * T], F32R)
        wh = sb("wh", [P, NBUF, EUNIT], F32R)
        wl = sb("wl", [P, NBUF, EUNIT], F32R)
        hh_t = sb("hidden_hi", [P, 12 * T], F32R)
        hl_t = sb("hidden_lo", [P, 12 * T], F32R)
        xgr = sb("gathered_parts", [P, 2 * KC * P], F32R)
        vec = sb("vec", [P, NVEC])
        con = sb("con", [P, NCONST])
        ones = sb("ones", [P, P])
        eps = sb("eps", [P, 1])
        rms = sb("rms", [P, 2, T])
        rstd = sb("rstd", [P, 2, T])
        mem = sb("mem", [P, KC, NM])
        poolw = sb("poolw", [P, RC, P])
        gatew = sb("gatew", [P, 2, RC, P])
        rw = sb("rw", [P, KC, NE])
        coef = sb("coef", [P, 6, DEPTH * RC])
        kv = sb("kv", [P, KC * NM + MC * D])
        kT = kv[:, 0:KC * NM].rearrange("p (c m) -> p c m", c=KC)
        vN = kv[:, KC * NM:].rearrange("p (c n) -> p c n", c=MC)

        def chunks(t, c, n):
            return t[:, 0:c * n].rearrange("p (c t) -> p c t", c=c)

        xhi, xlo = chunks(xh, KC, T), chunks(xl, KC, T)
        mhi, mlo = chunks(hh_t, KC, NM), chunks(hl_t, KC, NM)
        hhi, hlo = chunks(hh_t, 12, T), chunks(hl_t, 12, T)
        xn = sq
        small = sb("small", [P, 320])

        WORK = 9152
        work = sb("work", [P, WORK])
        at = [0]

        def take(n):
            at[0] += n
            assert at[0] <= WORK, at[0]
            return work[:, at[0] - n:at[0]]

        PADP = HIST + TP
        pp = take(RC * PADP).rearrange("p (c t) -> p c t", c=RC)
        spool = take(RC * TS * 16).rearrange("p (c b t) -> p c b t", c=RC, b=TS)
        PADC = CW - 1 + TP
        cp = take(RC * PADC).rearrange("p (c t) -> p c t", c=RC)
        sconv = take(RC * TS * CW).rearrange("p (c b t) -> p c b t", c=RC, b=TS)
        gel = take(RC * T).rearrange("p (c t) -> p c t", c=RC)
        cv = take(RC * T).rearrange("p (c t) -> p c t", c=RC)
        wA = take(RC * 270)
        wB = take(RC * 270)
        lad = [wA.rearrange("p (c t) -> p c t", c=RC), wB.rearrange("p (c t) -> p c t", c=RC)]
        r_g = take(RC * T).rearrange("p (c t) -> p c t", c=RC)
        i_g = take(RC * T).rearrange("p (c t) -> p c t", c=RC)
        ml = wB[:, 0:RC * T].rearrange("p (c t) -> p c t", c=RC)
        z = sq[:, 0:RC, :]
        tanh_w = sq[:, RC:2 * RC, :]
        yp, yr = r_g, i_g
        ss = small[:, 0:RC * TS].rearrange("p (c b) -> p c b", c=RC)
        mx = small[:, 32:32 + 12]
        nmx = small[:, 44:44 + 12]
        sm = small[:, 56:56 + 12]
        rs = small[:, 68:68 + 12]

        msq = kv[:, 0:KC * NM].rearrange("p (c m) -> p c m", c=KC)
        at[0] = 0
        pr = take(3 * NH * NM).rearrange("p (t h m) -> p t h m", t=3, h=NH)
        o8 = pr[:, 0:2, :, :].rearrange("p t h m -> p (t h m)")[:, 0:D]
        pT = take(NH * MC * TP).rearrange("p (h c t) -> p h c t", h=NH, c=MC)
        qz = take(KC * TS * TS).rearrange("p (c b s) -> p c b s", c=KC, b=TS)
        pz = take(NH * MC * TS * TS).rearrange("p (h c b s) -> p h c b s", h=NH, c=MC, b=TS)
        q = take(KC * T).rearrange("p (c t) -> p c t", c=KC)
        at[0] = 0
        sg = take(2 * T).rearrange("p (c t) -> p c t", c=2)
        hb = take(2 * T).rearrange("p (c t) -> p c t", c=2)
        at[0] = 0
        wsel = take(3 * CAP).rearrange("p (t s) -> p t s", t=3)
        esg = take(2 * GW).rearrange("p (i n) -> p i n", i=2)
        eh = take(FE)
        tokh, tokl = chunks(hh_t, 3, D), chunks(hl_t, 3, D)
        xgh = xgr[:, 0:KC * CAP].rearrange("p (c s) -> p c s", c=KC)
        xgl = xgr[:, KC * CAP:].rearrange("p (c s) -> p c s", c=KC)
        ehh, ehl = chunks(xh, FEC, CAP), chunks(xl, FEC, CAP)
        gsel = xh[:, FEC * CAP:(FEC + 3) * CAP].rearrange("p (t s) -> p t s", t=3)
        eo = kv[:, 0:D]
        scat = kv[:, D:D + T]
        rt = kv[:, 2 * D:3 * D]
        lg = rt[:, 0:24].rearrange("p (t e) -> p t e", t=3)
        m8 = rt[:, 24:48].rearrange("p (t e) -> p t e", t=3)
        fi = rt[:, 48:72].rearrange("p (t e) -> p t e", t=3)
        ed = rt[:, 72:75]
        g1 = rt[:, 75:78]
        g2 = rt[:, 78:81]
        oh = rt[:, 81:105].rearrange("p (t e) -> p t e", t=3)
        msk = rt[:, 105:129].rearrange("p (t e) -> p t e", t=3)
        wts = rt[:, 129:129 + 72].rearrange("p (t b e) -> p t b e", t=3, b=MAXB)
        wcol = rt[:, 129:129 + 72].rearrange("p (t v) -> p t v", t=3)
        psm = rt[:, 201:201 + 72].rearrange("p (t b e) -> p t b e", t=3, b=MAXB)
        pcol = rt[:, 201:201 + 72].rearrange("p (t v) -> p t v", t=3)
        pos = rt[:, 273:305].rearrange("p (t e) -> p t e", t=4)
        cmax = rt[:, 305:306]
        g1a = rt[:, 306:309]
        second = rt[:, 309:333].rearrange("p (t e) -> p t e", t=3)

        def per_token(a):
            return a.unsqueeze(2).broadcast_to([P, 3, NE])

        i8 = sb("i8", [P, 3, 8], U32)
        need = sb("need", [P, 1], I32)

        ident = con[:, C_ID:C_ID + P]
        tri = con[:, C_TRI:C_TRI + P]
        iota = con[:, C_IOTA:C_IOTA + P]
        corr = con[:, C_CORR:C_CORR + 64].rearrange("p (g t) -> p g t", g=4)
        valid = con[:, C_VALID:C_VALID + 3]

        psum = [ctx.enter_context(nc.psum_tensor(f"bank{b}", [P, 512], F32)) for b in range(8)]

        bank_full = [sem(f"bank_full{b}") for b in range(8)]
        bank_read = [sem(f"bank_read{b}") for b in range(8)]
        slot_loaded = [sem(f"slot_loaded{s}") for s in range(SLOTS)]
        slot_free = [sem(f"slot_free{s}") for s in range(SLOTS)]
        hi_ready = sem("weight_hi_ready")
        unit_used = sem("unit_used")
        eslot_loaded = [sem(f"eslot_loaded{s}") for s in range(ESLOTS)]
        eslot_free = [sem(f"eslot_free{s}") for s in range(ESLOTS)]
        ehi_ready = sem("expert_weight_hi_ready")
        eunit_used = sem("expert_unit_used")
        s_x = [sem(f"x_loaded{h}") for h in range(2)]
        s_vec = sem("vectors_loaded")
        s_mem = sem("mem_loaded")
        s_con = sem("consts_loaded")
        s_pw = sem("pool_w_loaded")
        s_gw = sem("gate_w_loaded")
        s_rw = sem("router_loaded")
        s_set = sem("constants_set")
        sq_ready = sem("squares_ready")
        xn_ready = sem("normed_ready")
        fn_ready = sem("normed_full_ready")
        xh_ready = sem("normed_hi_ready")
        oh_ready = sem("attended_hi_ready")
        h_ready = sem("hidden_parts_ready")
        mh_ready = sem("memory_hi_ready")
        xgh_ready = sem("gathered_hi_ready")
        ehh_ready = sem("expert_hidden_hi_ready")
        turn_done = sem("tokens_turned")
        msq_ready = sem("mem_squares_ready")
        mem_normed = sem("mem_normed")
        mn_ready = sem("gained_memory_ready")
        yp_ready = sem("y_pool_ready")
        padded = sem("zero_histories_set")
        hist_loaded = sem("sample_histories_loaded")
        cv_ready = sem("conv_ready")
        gates_ready = sem("gates_ready")
        z_ready = sem("pool_difference_ready")
        yr_ready = sem("y_rnn_ready")
        psq_ready = sem("y_pool_squares_ready")
        rsq_ready = sem("y_rnn_squares_ready")
        mixed_ready = sem("mixed_ready")
        decay_exp = sem("decay_exp_ready")
        decay_in = sem("decay_abs_ready")
        coef_ready = sem("decay_ready")
        h_last = sem("recurrence_ready")
        small_written = sem("small_outputs_written")
        kv_written = sem("keys_values_written")
        qz_ready = sem("sample_queries_ready")
        max_ready = sem("max_ready")
        exp_done = sem("exp_half_done")
        p_ready = sem("probs_ready")
        pz_ready = sem("sample_probs_ready")
        xos_ready = sem("sample_attended_ready")
        lmax_ready = sem("top_ready")
        lexp_ready = sem("gate_exp_ready")
        mask_ready = sem("mask_ready")
        route_ready = sem("route_ready")
        gsel_ready = sem("gather_matrix_ready")
        wsel_ready = sem("scatter_matrix_ready")
        x_final = sem("x_final")
        fsq_ready = sem("final_squares_ready")
        fsum_ready = sem("final_sum_ready")
        frms_ready = sem("final_rms_ready")
        y_ready = sem("y_ready")
        y_written = sem("y_written")
        dve_chain = sem("dve_chain")
        act_chain = sem("act_chain")
        pool_chain = sem("pool_chain")

        def col(name, l, c):
            k = l * LVEC + VEC[name] + c
            return vec[:, k:k + 1]

        def bank(n):
            return psum[n % 8]

        def raw(k):
            s = k % SLOTS
            return ring[:, s * UNIT:(s + 1) * UNIT]

        def eraw(s):
            return ring[:, s * EUNIT:(s + 1) * EUNIT]

        ends = {}
        for (kind, l, i), k in split.items():
            if kind in ("in", "mk", "out", "mq", "mo", "fg", "fu") and i % 2:
                ends[k] = tiles[(kind, l, i)]
            elif kind == "mv" and i % 2:
                ends[k] = tiles[(kind, l, i // 2, MC - 1)]
            elif kind[:2] == "fd":
                c0, c1 = HALVES[int(kind[2])]
                if 4 * (i + 1) % (c1 - c0) == 0:
                    ends[k] = tiles[(kind, l, 2 * (4 * (i + 1) // (c1 - c0)) - 1)]
        others = [k for k in range(NSPLIT) if k not in ends]

        def wait_used(eng, k):
            if k in ends:
                wait_full(eng, ends[k])
            else:
                eng.wait_ge(unit_used, others.index(k) + 1)

        EENDS = {4 * g + 1 + 2 * i: f"{'GU'[i]}{g}" for g in range(4) for i in range(2)}
        EENDS.update({19: "D0", 23: "D1"})
        EOTHERS = [j for j in range(EUNITS) if j not in EENDS]

        def wait_eused(eng, v, num, j):
            if j in EENDS:
                wait_full(eng, *num(EENDS[j]))
            else:
                eng.wait_ge(eunit_used, len(EOTHERS) * v + EOTHERS.index(j) + 1)

        def ewait(eng, sems, j, v, per=1):
            eng.wait_ge(sems[j % ESLOTS], per * (EUNITS // ESLOTS * v + j // ESLOTS + 1))

        def wait_full(eng, n, more=0):
            eng.wait_ge(bank_full[n % 8], n // 8 + 1 + 3 * more)

        def wait_read(eng, n, more=0):
            eng.wait_ge(bank_read[n % 8], n // 8 + 1 + 3 * more)

        class Splitter:

            def __init__(self, one):
                self.at, self.one = 0, one

            def upto(self, k):
                while self.at < min(k, NSPLIT):
                    self.one(self.at)
                    self.at += 1

        names = list(split)

        def start(kind, l):
            return split[(kind, l, 0)]

        def down_end(half, l, m):
            c0, c1 = HALVES[half]
            return start(f"fd{half}", l) + ((m // 2 + 1) * (c1 - c0) - 1) // 4

        def behind(kind, l, i, ahead, last):
            return min(split[(kind, l, i)] + ahead, last)

        block = ctx.enter_context(nc.Block())
        main = Pass(NT0, 0, NE)
        extra = Pass(main.end, NE, NE * (MAXB - 1))

        @block.sync
        def _(sp):
            for h in range(2):
                sp.dma_start(x[:, 4 * h:4 * h + 4, :], xT[:, 4 * h:4 * h + 4, :]).then_inc(s_x[h], 16)

            def load(k, dram_k):
                s = k % SLOTS
                sp.dma_start(raw(s), dense[dram_k]).then_inc(slot_loaded[s], 16)

            for k in range(SLOTS):
                load(k, k)
                if k == 3:
                    sp.dma_start(mem[:, :, :], memT).then_inc(s_mem, 16)
            rounds = NUNIT // SLOTS
            with sp.Fori(1, rounds) as r:
                for s in range(SLOTS):
                    sp.wait_ge(slot_free[s], r)
                    load(s, SLOTS * r + s)
            for k in range(rounds * SLOTS, NUNIT):
                sp.wait_ge(slot_free[k % SLOTS], k // SLOTS)
                load(k, k)

            def eload(e, j):
                s = j % ESLOTS
                sp.dma_start(eraw(s), experts[EUNITS * e + j]).then_inc(eslot_loaded[s], 16)

            def block_loads(v, e, j0=0):
                for j in range(j0, EUNITS):
                    sp.wait_ge(eslot_free[j % ESLOTS], EUNITS // ESLOTS * v + j // ESLOTS)
                    eload(e, j)

            for j in range(ESLOTS):
                for s in range(SLOTS):
                    if s * UNIT < (j + 1) * EUNIT and (s + 1) * UNIT > j * EUNIT:
                        sp.wait_ge(slot_free[s], (NUNIT - 1 - s) // SLOTS + 1)
                eload(0, j)
            block_loads(0, 0, ESLOTS)
            with sp.Fori(1, NE) as v:
                block_loads(v, v)
            sp.wait_ge(route_ready, 1)
            count = sp.value_load(need[0:1, 0:1], min_val=0, max_val=T)
            with sp.If(count > CAP):
                for b in range(1, MAXB):
                    with sp.Fori(0, NE) as e:
                        block_loads(NE * b + e, e)
            with sp.Else():
                sp.nop()

        @block.tensor
        def _(pe):
            mm = nc.tensor.matmul

            def take_bank(n, more=0):
                if n >= 8:
                    pe.wait_ge(bank_read[n % 8], n // 8 + 3 * more)
                return bank(n)

            def full(ins, n):
                ins.then_inc(bank_full[n % 8], 1)

            def product(out, s_hi, s_lo, m_hi, m_lo, start, stop, stationary_weights=True):
                if stationary_weights:
                    mm(out, s_hi, m_hi, start=start, stop=False)
                    mm(out, s_hi, m_lo, start=False, stop=False)
                    return mm(out, s_lo, m_hi, start=False, stop=stop)
                mm(out, s_hi, m_hi, start=start, stop=False)
                mm(out, s_lo, m_hi, start=False, stop=False)
                return mm(out, s_hi, m_lo, start=False, stop=stop)

            def unit(name):
                k = units[name]
                pe.wait_ge(slot_free[k % SLOTS], k // SLOTS + 1)
                b = split[name] % NBUF
                return [w[:, b, 0:UNIT].rearrange("p (k n) -> p k n", k=4) for w in (wh, wl)]

            def raw_unit(name):
                k = units[name]
                pe.wait_ge(slot_loaded[k % SLOTS], 16 * (k // SLOTS + 1))
                return raw(k).rearrange("p (k n) -> p k n", k=4)

            def frees(ins, name):
                ins.then_inc(slot_free[units[name] % SLOTS], 1)

            def norm_sum(key, j):
                n = tiles[key]
                b = take_bank(n)
                for m in range(KC):
                    pe.wait_ge(sq_ready, KC * j + m + 1)
                    i = mm(b[:, 0:T], ones[:, :], sq[:, m, :], start=(m == 0), stop=(m == KC - 1))
                full(i, n)

            def project_pair(key, l, s, hi, lo, width, ready=None, base=0):
                nn = [tiles[(key, l, 2 * s + u)] for u in range(2)]
                bb = [take_bank(n) for n in nn]
                for half in range(2):
                    w_hi, w_lo = unit((key, l, 2 * s + half))
                    for u in range(2):
                        for k4 in range(4):
                            kc = 4 * half + k4
                            if u == 0 and ready is not None:
                                pe.wait_ge(ready, base + kc + 1)
                            i = product(bb[u][:, 0:width], w_hi[:, k4, u * P:(u + 1) * P], w_lo[:, k4, u * P:(u + 1) * P],
                                        hi[:, kc, :], lo[:, kc, :], start=(kc == 0), stop=(kc == KC - 1))
                        if half:
                            full(i, nn[u])
                        elif u:
                            i.then_inc(unit_used, 1)

            def project(key, l, hi, lo, width, ready=None, base=0):
                for s in range(4):
                    project_pair(key, l, s, hi, lo, width, ready if s == 0 else None, base)

            pe.wait_ge(s_set, 2)
            for l in range(DEPTH):
                norm_sum(("ssq", 3 * l), 3 * l)
                for s in range(6):
                    if l == 0 and s == 3:
                        n = tiles[("msq",)]
                        b = take_bank(n)
                        for m in range(KC):
                            pe.wait_ge(msq_ready, m + 1)
                            i = mm(b[:, 0:NM], ones[:, :], msq[:, m, :], start=(m == 0), stop=(m == KC - 1))
                        full(i, n)
                    project_pair("in", l, s, xhi, xlo, T, xn_ready if s == 0 else None, KC * 3 * l)
                project("mk", l, mhi, mlo, NM, mn_ready, KC * l)
                pe.wait_ge(s_gw, 16 * (l + 1))
                pe.wait_ge(s_pw, 16 * (l + 1))
                pe.wait_ge(cv_ready, l + 1)
                for gi, key in enumerate(("ga", "gx")):
                    for c in range(RC):
                        n = tiles[(key, l, c)]
                        b = take_bank(n)
                        full(mm(b[:, 0:T], gatew[:, gi, c, :], cv[:, c, :], start=True, stop=True), n)
                for s in range(4):
                    nn = [tiles[("mv", l, s, mc)] for mc in range(MC)]
                    bb = [take_bank(n) for n in nn]
                    for half in range(2):
                        w_hi, w_lo = unit(("mv", l, 2 * s + half))
                        for mc in range(MC):
                            for k4 in range(4):
                                kc = 4 * half + k4
                                i = product(bb[mc][:, 0:PIECE], mhi[:, kc, mc * P:(mc + 1) * P], mlo[:, kc, mc * P:(mc + 1) * P],
                                            w_hi[:, k4, :], w_lo[:, k4, :], kc == 0, kc == KC - 1, False)
                            if half:
                                full(i, nn[mc])
                            elif mc:
                                i.then_inc(unit_used, 1)
                pe.wait_ge(z_ready, l + 1)
                for c in range(RC):
                    n = tiles[("pw", l, c)]
                    b = take_bank(n)
                    full(mm(b[:, 0:T], poolw[:, c, :], z[:, c, :], start=True, stop=True), n)
                for key, ready, o in (("psq", psq_ready, 0), ("rsq", rsq_ready, RC)):
                    n = tiles[(key, l)]
                    b = take_bank(n)
                    for c in range(RC):
                        pe.wait_ge(ready, RC * l + c + 1)
                        i = mm(b[:, 0:T], ones[:, :], sq[:, o + c, :], start=(c == 0), stop=(c == RC - 1))
                    full(i, n)
                project("out", l, xhi, xlo, T, mixed_ready, KC * l)
                norm_sum(("ssq", 3 * l + 1), 3 * l + 1)
                project("mq", l, xhi, xlo, T, xn_ready, KC * (3 * l + 1))
                for m in range(KC):
                    wait_read(pe, tiles[("mk", l, m)])
                    wait_read(pe, tiles[("mq", l, m)])
                for t in range(2):
                    for hp in range(2):
                        n = tiles[("sc", l, t, hp)]
                        b = take_bank(n)
                        for hh in range(2):
                            h = 2 * hp + hh
                            for c in range(HC):
                                i = mm(b[:, hh * NM:(hh + 1) * NM], q[:, HC * h + c, t * P:(t + 1) * P], kT[:, HC * h + c, :],
                                       start=(c == 0), stop=(c == HC - 1))
                        full(i, n)
                pe.wait_ge(qz_ready, l + 1)
                for u in range(16):
                    h = u // 4
                    n = tiles[("sc", l, 2, h // 2)]
                    if u % 8 == 0:
                        b = take_bank(n)
                    w = raw_unit(("kc", l, u))
                    for b2 in range(2):
                        for c in range(HC):
                            i = mm(b[0:TS, (h % 2) * NM:(h % 2 + 1) * NM], qz[:, HC * h + c, 2 * (u % 4) + b2, :], w[:, 2 * b2 + c, :],
                                   start=(u % 4 + b2 + c == 0), stop=(u % 4 == 3 and b2 + c == 2))
                            if b2 + c == 0 and u > 0:
                                frees(i, ("kc", l, u - 1))
                    if u % 8 == 7:
                        full(i, n)
                for h in range(NH):
                    n = tiles[("pt", l, h)]
                    b = take_bank(n)
                    for t in range(2):
                        pe.wait_ge(p_ready, 6 * l + 2 * t + h // 2 + 1)
                        for mc in range(MC):
                            i = nc.tensor.transpose(b[:, mc * TP + t * P:mc * TP + (t + 1) * P], pr[:, t, h, mc * P:(mc + 1) * P], ident)
                            if h + t + mc == 0:
                                frees(i, ("kc", l, 15))
                    full(i, n)
                for s in range(4):
                    for mc in range(MC):
                        wait_read(pe, tiles[("mv", l, s, mc)])
                for m in range(KC):
                    n = tiles[("pv", l, m)]
                    b = take_bank(n)
                    h = m // HC
                    wait_read(pe, tiles[("pt", l, h)])
                    for mc in range(MC):
                        i = mm(b[:, 0:TP], vN[:, mc, m * P:(m + 1) * P], pT[:, h, mc, :], start=(mc == 0), stop=(mc == MC - 1))
                    full(i, n)
                n = tiles[("pts", l)]
                b = take_bank(n)
                pe.wait_ge(p_ready, 6 * l + 6)
                for h in range(NH):
                    for mc in range(MC):
                        j = (h * MC + mc) * TS
                        i = nc.tensor.transpose(b[:, j:j + TS], pr[0:TS, 2, h, mc * P:(mc + 1) * P], ident[0:TS, 0:TS])
                full(i, n)
                pe.wait_ge(pz_ready, l + 1)
                for u in range(16):
                    h = u // 4
                    n = tiles[("pvs", l, h // 2)]
                    if u % 8 == 0:
                        b = take_bank(n)
                    w = raw_unit(("vc", l, u))
                    for b2 in range(2):
                        for mc in range(MC):
                            i = mm(b[0:TS, (h % 2) * HD:(h % 2 + 1) * HD], pz[:, h, mc, 2 * (u % 4) + b2, :], w[:, 2 * b2 + mc, :],
                                   start=(u % 4 + b2 + mc == 0), stop=(u % 4 == 3 and b2 + mc == 2))
                            if b2 + mc == 0 and u > 0:
                                frees(i, ("vc", l, u - 1))
                    if u % 8 == 7:
                        full(i, n)
                n = tiles[("ots", l)]
                b = take_bank(n)
                for hp in range(2):
                    wait_read(pe, tiles[("pvs", l, hp)])
                for c in range(KC):
                    i = nc.tensor.transpose(b[:, c * TS:(c + 1) * TS], o8[0:TS, c * P:(c + 1) * P], ident[0:TS, 0:TS])
                    if c == 0:
                        frees(i, ("vc", l, 15))
                full(i, n)
                for m in range(KC):
                    wait_read(pe, tiles[("pv", l, m)])
                wait_read(pe, tiles[("ots", l)])
                project("mo", l, xhi, xlo, T)
                norm_sum(("ssq", 3 * l + 2), 3 * l + 2)
                if l % 2 == 0:
                    for half, (c0, c1) in enumerate(HALVES):
                        for s in range(c0 // 2, c1 // 2):
                            for key in ("fg", "fu"):
                                first = s == 0 and key == "fg"
                                project_pair(key, l, s, xhi, xlo, T, xn_ready if first else None, KC * (3 * l + 2))
                        nk = c1 - c0
                        for mp in range(KC // 2):
                            nn = [tiles[(f"fd{half}", l, 2 * mp + u)] for u in range(2)]
                            bb = [take_bank(n) for n in nn]
                            for kc in range(nk):
                                piece = mp * nk + kc
                                if piece % 4 == 0 or kc == 0:
                                    w_hi, w_lo = unit((f"fd{half}", l, piece // 4))
                                if mp == 0:
                                    pe.wait_ge(h_ready, c0 + kc + 1)
                                for u in range(2):
                                    i = product(bb[u][:, 0:T], w_hi[:, piece % 4, u * P:(u + 1) * P], w_lo[:, piece % 4, u * P:(u + 1) * P],
                                                hhi[:, kc, :], hlo[:, kc, :], start=(kc == 0), stop=(kc == nk - 1))
                                    if kc == nk - 1:
                                        full(i, nn[u])
                                    elif piece % 4 == 3 and u == 1:
                                        i.then_inc(unit_used, 1)
            l = DEPTH - 1
            pe.wait_ge(s_rw, 16)
            n = tiles[("lg", l)]
            b = take_bank(n)
            pe.wait_ge(xn_ready, KC * (3 * l + 3))
            for t, (t0, rows) in enumerate(TOK):
                for kc in range(KC):
                    i = mm(b[0:rows, t * NE:(t + 1) * NE], xn[:, kc, t0:t0 + rows], rw[:, kc, :], start=(kc == 0), stop=(kc == KC - 1))
            full(i, n)
            for t, (t0, rows) in enumerate(TOK):
                for hp in range(2):
                    n = tiles[("tk", l, t, hp)]
                    b = take_bank(n)
                    for c in range(4):
                        i = nc.tensor.transpose(b[0:rows, c * P:(c + 1) * P], xn[:, 4 * hp + c, t0:t0 + rows], ident)
                    full(i, n)
            n = tiles[("ps", l)]
            b = take_bank(n)
            pe.wait_ge(mask_ready, 1)
            for t in range(4):
                last = min(t, 2)
                for u in range(last + 1):
                    w = tri if u == t else ones[:, :]
                    i = mm(b[:, t * NE:(t + 1) * NE], w, msk[:, u, :], start=(u == 0), stop=(u == last))
            full(i, n)

            def gather(v, num):
                pe.wait_ge(gsel_ready, v + 1)
                for half in range(2):
                    n, more = num(f"X{half}")
                    b = take_bank(n, more)
                    for c in range(4):
                        for t, (t0, rows) in enumerate(TOK):
                            f0 = (4 * half + c) * P
                            mm(b[:, c * P:(c + 1) * P], tokh[0:rows, t, f0:f0 + P], gsel[0:rows, t, :], start=(t == 0), stop=False)
                            i = mm(b[:, c * P:(c + 1) * P], tokl[0:rows, t, f0:f0 + P], gsel[0:rows, t, :], start=False, stop=(t == 2))
                    full(i, n)

            def turn_scatter(v, num):
                n, more = num("S")
                b = take_bank(n, more)
                pe.wait_ge(wsel_ready, v + 1)
                for t, (t0, rows) in enumerate(TOK):
                    i = nc.tensor.transpose(b[:, t0:t0 + rows], wsel[0:rows, t, :], ident[0:rows, 0:rows])
                full(i, n)

            def scatter(num, before):
                wait_read(pe, *num("S"))
                for u in range(2):
                    wait_read(pe, *before(f"D{u}"))
                for c in range(KC):
                    n, more = num(f"C{c}")
                    b = take_bank(n, more)
                    full(mm(b[:, 0:T], eo[:, c * P:(c + 1) * P], scat, start=True, stop=True), n)

            def turn_hidden(num, i3):
                n, more = num(f"T{i3}")
                b = take_bank(n, more)
                for g in ((0, 1), (2,), (3,))[i3]:
                    wait_read(pe, *num(f"U{g}"))
                for c in range(4 * i3, min(4 * i3 + 4, FEC)):
                    i = nc.tensor.transpose(b[:, (c % 4) * P:(c % 4 + 1) * P], eh[:, c * P:(c + 1) * P], ident)
                full(i, n)

            def expert(v, num, before, first, last):
                def eunit(j):
                    ewait(pe, eslot_free, j, v)
                    return wh[:, j % NBUF, :], wl[:, j % NBUF, :]

                def group(g):
                    if g == 0:
                        for half in range(2):
                            wait_read(pe, *before(f"X{half}"))
                    for gi, name in enumerate("GU"):
                        n, more = num(f"{name}{g}")
                        b = take_bank(n, more)
                        for half in range(2):
                            w_hi, w_lo = (w.rearrange("p (k n) -> p k n", k=4) for w in eunit(4 * g + 2 * gi + half))
                            for k4 in range(4):
                                kc = 4 * half + k4
                                i = product(b[:, 0:GW], xgh[:, kc, :], xgl[:, kc, :], w_hi[:, k4, :], w_lo[:, k4, :],
                                            kc == 0, kc == KC - 1, False)
                            if half:
                                full(i, n)
                            else:
                                i.then_inc(eunit_used, 1)

                group(0)
                group(1)
                group(2)
                turn_hidden(num, 0)
                if not first:
                    turn_scatter(v - 1, num)
                group(3)
                turn_hidden(num, 1)
                if not first:
                    scatter(num, before)
                if not last:
                    gather(v + 1, num)
                turn_hidden(num, 2)
                for g in range(4):
                    n, more = num(f"D{g // 2}")
                    if g % 2 == 0:
                        b = take_bank(n, more)
                    c0 = (g % 2) * PIECE
                    for half in range(2):
                        w_hi, w_lo = eunit(16 + 2 * g + half)
                        for kc in range(6 * half - half, 6 + 5 * half):
                            if g == 0 and half == 0 and kc % 4 == 0 or g == 0 and half == 1 and kc == 8:
                                wait_read(pe, *num(f"T{kc // 4}"))
                            lo, hi = max(kc * PIECE - half * EUNIT, 0), min((kc + 1) * PIECE - half * EUNIT, EUNIT)
                            off = c0 + lo + half * EUNIT - kc * PIECE
                            i = product(b[:, off:off + hi - lo], ehh[:, kc, :], ehl[:, kc, :], w_hi[:, lo:hi], w_lo[:, lo:hi],
                                        kc == 0, kc == FEC - 1, False)
                        if half and g % 2:
                            full(i, n)
                        else:
                            i.then_inc(eunit_used, 1)

            def run_pass(p):
                v0, v1 = p.v0, p.v0 + p.nv - 1
                gather(v0, p.prologue)
                expert(v0, p.first, p.prologue, True, False)
                with pe.Fori(v0 + 1, v1) as v:
                    expert(v, p.middle(v), p.earlier(v), False, False)
                expert(v1, p.last, p.earlier(v1), False, True)
                turn_scatter(v1, p.after)
                scatter(p.after, p.last)

            for t in range(3):
                for hp in range(2):
                    wait_read(pe, tiles[("tk", l, t, hp)])
            run_pass(main)
            pe.wait_ge(route_ready, 1)
            count = pe.value_load(need[0:1, 0:1], min_val=0, max_val=T)
            with pe.If(count > CAP):
                run_pass(extra)
            with pe.Else():
                pe.nop()
            for m in range(KC):
                pe.wait_ge(fsq_ready, m + 1)
                i = mm(psum[0][:, 0:T], ones[:, :], sq[:, m, :], start=(m == 0), stop=(m == KC - 1))
            i.then_inc(fsum_ready, 1)

        @block.scalar
        def _(act):
            A = nc.scalar.activation
            act.dma_start(vec[:, :], vecs).then_inc(s_vec, 16)
            act.dma_start(con[:, :], consts).then_inc(s_con, 16)
            act.dma_start(rw[:, :, :], router_w).then_inc(s_rw, 16)
            chain = [0]

            def step(ins):
                chain[0] += 1
                ins.then_inc(act_chain, 1)
                return chain[0]

            def after(k):
                act.wait_ge(act_chain, k)

            def read(ins, n):
                ins.then_inc(bank_read[n % 8], 1)

            def high_part(k):
                name = names[k]
                u = units[name]
                act.wait_ge(slot_loaded[u % SLOTS], 16 * (u // SLOTS + 1))
                if k >= NBUF:
                    wait_used(act, k - NBUF)
                A(wh[:, k % NBUF, 0:UNIT], raw(u), ACT.Copy).then_inc(hi_ready, 1)

            S = Splitter(high_part)

            def squares(j, key=None, l=0):
                for m in range(KC):
                    if key is not None:
                        wait_read(act, tiles[(key, l, m)])
                    A(sq[:, m, :], x[:, m, :], ACT.Square).then_inc(sq_ready, 1)

            def root(n, width, scale, buf=0):
                wait_full(act, n)
                read(A(rms[:, buf, 0:width], bank(n)[:, 0:width], ACT.Sqrt, bias=eps[:, 0:1], scale=scale), n)

            made = [0]

            def high_parts(between=None):
                for c in range(KC):
                    made[0] += 1
                    act.wait_ge(fn_ready, made[0])
                    A(xhi[:, c, :], sq[:, c, :], ACT.Copy).then_inc(xh_ready, 1)
                    if c == 3 and between is not None:
                        S.upto(between)

            act.wait_ge(s_set, 2)
            for m in range(KC):
                act.wait_ge(s_x[m // 4], 16)
                A(sq[:, m, :], x[:, m, :], ACT.Square).then_inc(sq_ready, 1)
            for l in range(DEPTH):
                S.upto(start("in", l) + 1)
                root(tiles[("ssq", 3 * l)], T, 1.0 / D)
                high_parts(start("in", l) + 3)
                S.upto(start("in", l) + 4)
                if l == 0:
                    act.wait_ge(decay_in, 1)
                    A(coef[:, 1, :], coef[:, 0, :], ACT.Exp).then_inc(decay_exp, 1)
                act.wait_ge(padded, 2 * (l + 1))
                act.wait_ge(hist_loaded, 32 * (l + 1))
                for m in range(12):
                    n = tiles[("in", l, m)]
                    wait_full(act, n)
                    c = m % RC
                    if m < RC:
                        A(cp[:, c, CW - 1:], bank(n)[:, 0:TP], ACT.Copy)
                        read(A(sconv[:, c, :, CW - 1], bank(n)[:, TP:T], ACT.Copy), n)
                    elif m < 2 * RC:
                        read(A(gel[:, c, :], bank(n)[:, 0:T], ACT.Gelu_apprx_tanh), n)
                    else:
                        A(pp[:, c, HIST:], bank(n)[:, 0:TP], ACT.Copy)
                        read(A(spool[:, c, :, 15], bank(n)[:, TP:T], ACT.Copy), n)
                    if m % 2:
                        S.upto(behind("in", l, m, 5, start("mk", l) + 2))
                    if l == 0 and m in (1, 3):
                        act.wait_ge(s_mem, 16)
                        for c in range(2 * m - 2, 2 * m + 2):
                            A(msq[:, c, :], mem[:, c, :], ACT.Square).then_inc(msq_ready, 1)
                    if l == 0 and m == 5:
                        root(tiles[("msq",)], NM, 1.0 / D, 1)
                    if m == 9:
                        if l == 0:
                            act.wait_ge(mem_normed, KC)
                        for c in range(KC):
                            A(mhi[:, c, :], mem[:, c, :], ACT.Copy, scale=col("mem_norm", l, c)).then_inc(mh_ready, 1)
                S.upto(start("mk", l) + 4)
                if l > 0:
                    act.wait_ge(kv_written, 32 * l)
                for m in range(KC):
                    n = tiles[("mk", l, m)]
                    wait_full(act, n)
                    read(A(kT[:, m, :], bank(n)[:, 0:NM], ACT.Copy), n)
                    if m % 2:
                        S.upto(behind("mk", l, m, 5, start("mv", l) + 2))
                for key, dst, name in (("ga", r_g, "gate_a_b"), ("gx", i_g, "gate_x_b")):
                    for c in range(RC):
                        n = tiles[(key, l, c)]
                        wait_full(act, n)
                        read(A(dst[:, c, :], bank(n)[:, 0:T], ACT.Sigmoid, bias=col(name, l, c)), n)
                S.upto(start("mv", l) + 3)
                act.wait_ge(coef_ready, 1)
                for c in range(RC):
                    wait_read(act, tiles[("ga", l, c)])
                    step(A(tanh_w[:, c, :], r_g[:, c, :], ACT.Tanh, scale=coef[:, 5, l * RC + c:l * RC + c + 1]))
                S.upto(start("mv", l) + 4)
                for c in range(RC):
                    k = step(A(r_g[:, c, :], r_g[:, c, :], ACT.Exp, scale=coef[:, 0, l * RC + c:l * RC + c + 1]))
                S.upto(start("mv", l) + 5)
                after(k)
                act.wait_ge(z_ready, l + 1)
                A(ml, tanh_w, ACT.Sqrt).then_inc(gates_ready, 1)
                for s in range(4):
                    for mc in range(MC):
                        n = tiles[("mv", l, s, mc)]
                        wait_full(act, n)
                        read(A(vN[:, mc, s * PIECE:(s + 1) * PIECE], bank(n)[:, 0:PIECE], ACT.Copy), n)
                    S.upto(behind("mv", l, 2 * s + 1, 5, start("out", l) + 2))
                act.wait_ge(yr_ready, l + 1)
                for c in range(RC):
                    A(sq[:, RC + c, :], yr[:, c, :], ACT.Square).then_inc(rsq_ready, 1)
                for c in range(RC):
                    wait_read(act, tiles[("pw", l, c)])
                    A(sq[:, c, :], yp[:, c, :], ACT.Square).then_inc(psq_ready, 1)
                root(tiles[("psq", l)], T, 2.0 / D, 1)
                root(tiles[("rsq", l)], T, 2.0 / D)
                high_parts(start("out", l) + 3)
                S.upto(start("out", l) + 4)
                for m in range(KC):
                    wait_read(act, tiles[("out", l, m)])
                    A(sq[:, m, :], x[:, m, :], ACT.Square).then_inc(sq_ready, 1)
                    if m % 2:
                        S.upto(behind("out", l, m, 5, start("mq", l) + 2))
                root(tiles[("ssq", 3 * l + 1)], T, 1.0 / D)
                high_parts(start("mq", l) + 3)
                S.upto(start("mq", l) + 4)
                for m in range(KC):
                    n = tiles[("mq", l, m)]
                    wait_full(act, n)
                    read(A(q[:, m, :], bank(n)[:, 0:T], ACT.Copy), n)
                    if m % 2:
                        S.upto(behind("mq", l, m, 5, start("mo", l)))
                for t in range(3):
                    rows = TOK[t][1]
                    for hp in range(2):
                        n = tiles[("sc", l, t, hp)]
                        act.wait_ge(max_ready, 6 * l + 2 * t + hp + 1)
                        for hh in range(2):
                            h = 2 * hp + hh
                            j = 4 * t + h
                            i = A(pr[0:rows, t, h, :], bank(n)[0:rows, hh * NM:(hh + 1) * NM], ACT.Exp,
                                  bias=nmx[0:rows, j:j + 1], scale=HD ** -0.5, accum_out=sm[0:rows, j:j + 1])
                            if hh:
                                read(i, n)
                            else:
                                i.then_inc(exp_done, 1)
                for h in range(NH):
                    n = tiles[("pt", l, h)]
                    wait_full(act, n)
                    read(A(pT[:, h, :, :].rearrange("p c t -> p (c t)"), bank(n)[:, :], ACT.Copy), n)
                for m in range(KC):
                    n = tiles[("pv", l, m)]
                    wait_full(act, n)
                    A(xhi[:, m, 0:TP], bank(n)[:, 0:TP], ACT.Copy).then_inc(oh_ready, 1)
                S.upto(start("mo", l) + 4)
                nxt = start("fg", l) if l % 2 == 0 else NSPLIT
                for m in range(KC):
                    wait_read(act, tiles[("mo", l, m)])
                    A(sq[:, m, :], x[:, m, :], ACT.Square).then_inc(sq_ready, 1)
                    if m % 2:
                        S.upto(behind("mo", l, m, 5, nxt + 2))
                root(tiles[("ssq", 3 * l + 2)], T, 1.0 / D)
                if l % 2 == 0:
                    high_parts(nxt + 3)
                    for half, (c0, c1) in enumerate(HALVES):
                        nxt = start(f"fd{half}", l)
                        S.upto(split[("fg", l, c0)] + 4)
                        for m in range(c0, c1):
                            n = tiles[("fg", l, m)]
                            wait_full(act, n)
                            if m >= 2:
                                act.wait_ge(h_ready, m - 1)
                            read(A(sg[:, m % 2, :], bank(n)[:, 0:T], ACT.Silu), n)
                            if m % 2:
                                S.upto(behind("fg", l, m, 7, nxt + 3))
                        S.upto(nxt + 3)
                        after_down = start("in", l + 1) if half else split[("fg", l, c1)]
                        for m in range(KC):
                            if m % 2 == 0:
                                S.upto(min(down_end(half, l, m) + 3, after_down + 2))
                            if half:
                                wait_read(act, tiles[(f"fd{half}", l, m)])
                                A(sq[:, m, :], x[:, m, :], ACT.Square).then_inc(sq_ready, 1)
            l = DEPTH - 1

            def first_highs(v0):
                for j in range(NBUF):
                    ewait(act, eslot_loaded, j, v0, 16)
                    if v0 == 0:
                        wait_used(act, max(k for k in range(NSPLIT) if k % NBUF == j))
                    else:
                        wait_full(act, *main.last("D1"))
                    A(wh[:, j, :], eraw(j), ACT.Copy).then_inc(ehi_ready, 1)

            first_highs(0)
            for t, (t0, rows) in enumerate(TOK):
                for hp in range(2):
                    n = tiles[("tk", l, t, hp)]
                    wait_full(act, n)
                    A(tokh[0:rows, t, hp * 512:(hp + 1) * 512], bank(n)[0:rows, :], ACT.Copy).then_inc(oh_ready, 1)
            act.wait_ge(lmax_ready, 1)
            A(ed, ed, ACT.Exp).then_inc(lexp_ready, 1)

            def ehigh(v, num, j):
                vv, jj = (v, j) if j < EUNITS else (v + 1, j - EUNITS)
                ewait(act, eslot_loaded, jj, vv, 16)
                wait_eused(act, v, num, j - NBUF)
                A(wh[:, jj % NBUF, :], eraw(jj % ESLOTS), ACT.Copy).then_inc(ehi_ready, 1)

            def gathered(num):
                for half in range(2):
                    n, more = num(f"X{half}")
                    wait_full(act, n, more)
                    A(xgh[:, 4 * half:4 * half + 4, :].rearrange("p c s -> p (c s)"), bank(n)[:, :], ACT.Copy).then_inc(xgh_ready, 1)

            def turned(num, i3):
                n, more = num(f"T{i3}")
                wait_full(act, n, more)
                k = min(4, FEC - 4 * i3)
                A(ehh[:, 4 * i3:4 * i3 + k, :].rearrange("p c s -> p (c s)"), bank(n)[:, 0:k * P], ACT.Copy).then_inc(ehh_ready, 1)

            def scattered(num):
                n, more = num("S")
                wait_full(act, n, more)
                read(A(scat, bank(n)[:, 0:T], ACT.Copy), n)

            def expert(v, num, first, last):
                at = [NBUF]

                def upto(k):
                    while at[0] < min(k, EUNITS if last else EUNITS + NBUF):
                        ehigh(v, num, at[0])
                        at[0] += 1

                def silu(g):
                    n, more = num(f"G{g}")
                    wait_full(act, n, more)
                    if g >= 2:
                        wait_read(act, *num(f"U{g - 2}"))
                    read(A(esg[:, g % 2, :], bank(n)[:, 0:GW], ACT.Silu), n)

                upto(4)
                silu(0)
                upto(8)
                silu(1)
                upto(12)
                silu(2)
                upto(15)
                turned(num, 0)
                if not first:
                    scattered(num)
                upto(16)
                silu(3)
                upto(19)
                turned(num, 1)
                if not last:
                    gathered(num)
                turned(num, 2)
                upto(23)
                for u in range(2):
                    n, more = num(f"D{u}")
                    wait_full(act, n, more)
                    read(A(eo[:, u * 512:(u + 1) * 512], bank(n)[:, :], ACT.Copy), n)
                    upto(27)

            def run_pass(p):
                v0, v1 = p.v0, p.v0 + p.nv - 1
                if v0 > 0:
                    first_highs(v0)
                gathered(p.prologue)
                expert(v0, p.first, True, False)
                with act.Fori(v0 + 1, v1) as v:
                    expert(v, p.middle(v), False, False)
                expert(v1, p.last, False, True)
                scattered(p.after)

            run_pass(main)
            act.wait_ge(route_ready, 1)
            count = act.value_load(need[0:1, 0:1], min_val=0, max_val=T)
            with act.If(count > CAP):
                run_pass(extra)
            with act.Else():
                act.nop()
            act.wait_ge(x_final, 1)
            for m in range(KC):
                A(sq[:, m, :], x[:, m, :], ACT.Square).then_inc(fsq_ready, 1)
            act.wait_ge(fsum_ready, 1)
            A(rms[:, 0, :], psum[0][:, 0:T], ACT.Sqrt, bias=eps[:, 0:1], scale=1.0 / D).then_inc(frms_ready, 1)

        @block.vector
        def _(dve):
            V = nc.vector
            chain = [0]

            def step(ins):
                chain[0] += 1
                ins.then_inc(dve_chain, 1)
                return chain[0]

            def after(k):
                dve.wait_ge(dve_chain, k)

            def link(ins):
                after(step(ins))

            def read(ins, n):
                ins.then_inc(bank_read[n % 8], 1)

            def signal(ready):
                after(chain[0])
                dve.sem_inc(ready, 1)

            V.memset(ones[:, :], 1.0).then_inc(s_set, 1)
            V.memset(eps[:, :], EPS).then_inc(s_set, 1)

            dve.wait_ge(s_vec, 16)
            for l in range(DEPTH):
                k = l * LVEC + VEC["rglru_lambda"]
                link(V.tensor_scalar(coef[:, 5, l * RC:(l + 1) * RC], vec[:, k:k + RC], -1.0, 0.0, ALU.mult, ALU.max))
                link(V.tensor_scalar(coef[:, 0, l * RC:(l + 1) * RC], vec[:, k:k + RC], -1.0, None, ALU.mult))
                link(V.tensor_tensor(coef[:, 0, l * RC:(l + 1) * RC], coef[:, 0, l * RC:(l + 1) * RC], vec[:, k:k + RC], ALU.min))
            signal(decay_in)

            def invert(n, buf, width=T):
                wait_read(dve, n)
                link(V.reciprocal(rstd[:, buf, 0:width], rms[:, buf, 0:width]))

            def low_part(k):
                u = units[names[k]]
                dve.wait_ge(hi_ready, k + 1)
                V.tensor_tensor(wl[:, k % NBUF, 0:UNIT], raw(u), wh[:, k % NBUF, 0:UNIT].bitcast(F32), ALU.subtract)\
                    .then_inc(slot_free[u % SLOTS], 1)

            S = Splitter(low_part)

            made = [0]

            def scaled_parts(src, l, name, buf, c0, c1, ready, between=None, o=0):
                for c in range(c0, c1 + 1):
                    if c < c1:
                        V.scalar_tensor_tensor(out=sq[:, c, :], in0=src[:, c - o, :], scalar=col(name, l, c - o),
                                               in1=rstd[:, buf, :], op0=ALU.mult, op1=ALU.mult).then_inc(fn_ready, 1)
                    if c > c0:
                        made[0] += 1
                        dve.wait_ge(xh_ready, made[0])
                        V.tensor_tensor(xlo[:, c - 1, :], sq[:, c - 1, :], xhi[:, c - 1, :].bitcast(F32), ALU.subtract).then_inc(ready, 1)
                    if between is not None and c == c0 + 4:
                        S.upto(between)

            def normed(j, l, name, between):
                invert(tiles[("ssq", j)], 0)
                scaled_parts(x, l, name, 0, 0, KC, xn_ready, between)

            def residual(key, l, ahead, last):
                for m in range(KC):
                    if callable(ahead) and m % 2 == 0:
                        S.upto(ahead(m))
                    n = tiles[(key, l, m)]
                    wait_full(dve, n)
                    read(V.tensor_tensor(x[:, m, :], bank(n)[:, 0:T], x[:, m, :], ALU.add), n)
                    if m % 2 and not callable(ahead):
                        S.upto(behind(key, l, m, ahead, last))

            for l in range(DEPTH):
                S.upto(start("in", l) + 1)
                normed(3 * l, l, "norm_mix", start("in", l) + 3)
                S.upto(start("in", l) + 4)
                if l == 0:
                    dve.wait_ge(decay_exp, 1)
                    e, s, s2, acc, out = (coef[:, i, :] for i in (1, 2, 3, 4, 5))
                    link(V.tensor_scalar(acc, e, 2.0, None, ALU.add))
                    link(V.reciprocal(acc, acc))
                    link(V.tensor_tensor(s, e, acc, ALU.mult))
                    link(V.tensor_tensor(s2, s, s, ALU.mult))
                    link(V.tensor_scalar(acc, s2, 1.0 / 19, None, ALU.mult))
                    for d in (17, 15, 13, 11, 9, 7, 5, 3):
                        link(V.scalar_tensor_tensor(out=acc, in0=acc, scalar=1.0 / d, in1=s2, op0=ALU.add, op1=ALU.mult))
                    link(V.scalar_tensor_tensor(out=acc, in0=acc, scalar=1.0, in1=s, op0=ALU.add, op1=ALU.mult))
                    link(V.scalar_tensor_tensor(out=out, in0=acc, scalar=2.0, in1=out, op0=ALU.mult, op1=ALU.add))
                    link(V.tensor_scalar(out, out, 4.0, None, ALU.mult))
                    link(V.tensor_scalar(coef[:, 0, :], out, -2.0, None, ALU.mult))
                    signal(coef_ready)
                last = {}

                def tap(k):
                    for c in range(RC):
                        j = l * LVEC + VEC["conv_w"] + RC * k + c
                        w = vec[:, j:j + 1]
                        if k == 0:
                            wait_read(dve, tiles[("in", l, c)])
                            step(V.tensor_scalar(cv[:, c, 0:TP], cp[:, c, 0:TP], w, col("conv_b", l, c), ALU.mult, ALU.add))
                            last[c] = step(V.tensor_scalar(cv[:, c, TP:T], sconv[:, c, :, 0], w, col("conv_b", l, c), ALU.mult, ALU.add))
                        else:
                            after(last[c])
                            step(V.scalar_tensor_tensor(out=cv[:, c, 0:TP], in0=cp[:, c, k:k + TP], scalar=w, in1=cv[:, c, 0:TP],
                                                        op0=ALU.mult, op1=ALU.add))
                            last[c] = step(V.scalar_tensor_tensor(out=cv[:, c, TP:T], in0=sconv[:, c, :, k], scalar=w,
                                                                  in1=cv[:, c, TP:T], op0=ALU.mult, op1=ALU.add))

                for s in range(6):
                    wait_full(dve, tiles[("in", l, 2 * s + 1)])
                    S.upto(behind("in", l, 2 * s + 1, 5, start("mk", l) + 2))
                    if s == 3 and l == 0:
                        invert(tiles[("msq",)], 1, NM)
                        for m in range(KC):
                            V.tensor_tensor(mem[:, m, :], mem[:, m, :], rstd[:, 1, 0:NM], ALU.mult).then_inc(mem_normed, 1)
                    elif s in (2, 3):
                        tap(s - 2)
                    elif s == 4:
                        for m in range(KC):
                            dve.wait_ge(mh_ready, KC * l + m + 1)
                            V.scalar_tensor_tensor(out=mlo[:, m, :], in0=mem[:, m, :], scalar=col("mem_norm", l, m),
                                                   in1=mhi[:, m, :].bitcast(F32), op0=ALU.mult, op1=ALU.subtract).then_inc(mn_ready, 1)
                S.upto(start("mk", l) + 4)
                for k in range(1 if l == 0 else 2, CW):
                    tap(k)
                    S.upto(start("mk", l) + 4 + k)
                signal(cv_ready)
                for c in range(RC):
                    wait_read(dve, tiles[("in", l, 2 * RC + c)])
                link(V.tensor_tensor(lad[0][:, :, 0:270], pp[:, :, 0:270], pp[:, :, 1:271], ALU.add))
                link(V.tensor_tensor(lad[1][:, 1:4, 0:268], lad[0][:, 1:4, 0:268], lad[0][:, 1:4, 2:270], ALU.add))
                S.upto(start("mk", l) + 8)
                link(V.tensor_tensor(lad[0][:, 2:4, 0:264], lad[1][:, 2:4, 0:264], lad[1][:, 2:4, 4:268], ALU.add))
                link(V.tensor_tensor(lad[1][:, 3, 0:256], lad[0][:, 3, 0:256], lad[0][:, 3, 8:264], ALU.add))
                S.upto(start("mv", l) + 1)
                if l == 0:
                    dve.wait_ge(s_con, 16)
                for g, w in enumerate(WINDOWS):
                    s = lad[g % 2][:, g, 16 - w:16 - w + TP]
                    step(V.tensor_reduce(ss[:, g, :], spool[:, g, :, 16 - w:16], AX_X, ALU.add))
                    k = step(V.tensor_tensor(s[:, 0:16], s[:, 0:16], corr[:, g, :], ALU.mult))
                after(k)
                for g, w in enumerate(WINDOWS):
                    s = lad[g % 2][:, g, 16 - w:16 - w + TP]
                    step(V.scalar_tensor_tensor(out=z[:, g, 0:TP], in0=s, scalar=1.0 / w, in1=pp[:, g, HIST:], op0=ALU.mult, op1=ALU.subtract))
                    step(V.scalar_tensor_tensor(out=z[:, g, TP:T], in0=ss[:, g, :], scalar=1.0 / w, in1=spool[:, g, :, 15],
                                                op0=ALU.mult, op1=ALU.subtract))
                signal(z_ready)
                S.upto(start("mv", l) + 5)
                dve.wait_ge(gates_ready, l + 1)
                k = step(V.scalar_tensor_tensor(out=ml, in0=r_g, scalar=1.0, in1=ml, op0=ALU.add, op1=ALU.mult))
                for c in range(RC):
                    wait_read(dve, tiles[("gx", l, c)])
                step(V.tensor_tensor(i_g, i_g, cv, ALU.mult))
                after(k)
                link(V.memset(ml[:, :, 0:1], 1.0))
                link(V.tensor_tensor(i_g, i_g, ml, ALU.mult))
                S.upto(start("mv", l) + 6)
                o = VEC_H0 + l * RC * TS
                h0 = vec[:, o:o + RC * TS].rearrange("p (c b) -> p c b", c=RC)
                k = step(V.tensor_tensor(cv[:, :, TP:T], r_g[:, :, TP:T], h0, ALU.mult))
                for c in range(RC):
                    step(V.tensor_tensor_scan(cv[:, c, 0:TP], r_g[:, c, 0:TP], i_g[:, c, 0:TP], 0.0, ALU.mult, ALU.add))
                S.upto(start("mv", l) + 7)
                after(k)
                step(V.tensor_tensor(cv[:, :, TP:T], cv[:, :, TP:T], i_g[:, :, TP:T], ALU.add))
                signal(h_last)
                for c in range(RC):
                    wait_read(dve, tiles[("in", l, RC + c)])
                V.tensor_tensor(yr, cv, gel, ALU.mult).then_inc(yr_ready, 1)
                S.upto(start("out", l) + 2)
                for c in range(RC):
                    n = tiles[("pw", l, c)]
                    wait_full(dve, n)
                    read(V.tensor_scalar(yp[:, c, :], bank(n)[:, 0:T], col("pool_scale", l, c), None, ALU.mult), n)
                for key, name, o, buf in (("psq", "out_norm_pool", 0, 1), ("rsq", "out_norm_rnn", RC, 0)):
                    invert(tiles[(key, l)], buf)
                    scaled_parts(yr if o else yp, l, name, buf, o, o + RC, mixed_ready, o=o)
                S.upto(start("out", l) + 4)
                dve.wait_ge(small_written, 96 * (l + 1))
                step(V.memset(qz, 0.0))
                step(V.memset(pz, 0.0))
                residual("out", l, 5, start("mq", l) + 2)
                normed(3 * l + 1, l, "norm_mem", start("mq", l) + 3)
                S.upto(start("mq", l) + 4)
                after(chain[0])
                for c in range(KC):
                    wait_read(dve, tiles[("mq", l, c)])
                    step(V.tensor_copy(qz[:, c, :, :].rearrange("p b s -> p (b s)")[:, 0:64:TS + 1], q[:, c, TP:T]))
                    if c % 2:
                        S.upto(behind("mq", l, c, 5, start("mo", l)))
                signal(qz_ready)
                for t in range(3):
                    rows = TOK[t][1]
                    for hp in range(2):
                        n = tiles[("sc", l, t, hp)]
                        j = 4 * t + 2 * hp
                        wait_full(dve, n)
                        link(V.tensor_reduce(mx[0:rows, j:j + 2], bank(n)[0:rows, :].rearrange("p (h m) -> p h m", h=2), AX_X, ALU.max))
                        V.tensor_scalar(nmx[0:rows, j:j + 2], mx[0:rows, j:j + 2], -(HD ** -0.5), None, ALU.mult).then_inc(max_ready, 1)
                    for hp in range(2):
                        j = 4 * t + 2 * hp
                        dve.wait_ge(exp_done, 6 * l + 2 * t + hp + 1)
                        wait_read(dve, tiles[("sc", l, t, hp)])
                        link(V.reciprocal(rs[0:rows, j:j + 2], sm[0:rows, j:j + 2]))
                        for hh in range(2):
                            h = 2 * hp + hh
                            step(V.tensor_scalar(pr[0:rows, t, h, :], pr[0:rows, t, h, :], rs[0:rows, j + hh:j + hh + 1], None, ALU.mult))
                        signal(p_ready)
                for m in range(KC):
                    n = tiles[("pv", l, m)]
                    dve.wait_ge(oh_ready, KC * l + m + 1)
                    read(V.tensor_tensor(xlo[:, m, 0:TP], bank(n)[:, 0:TP], xhi[:, m, 0:TP].bitcast(F32), ALU.subtract), n)
                n = tiles[("pts", l)]
                wait_full(dve, n)
                for h in range(NH):
                    for mc in range(MC):
                        j = (h * MC + mc) * TS
                        i = V.tensor_copy(pz[:, h, mc, :, :].rearrange("p b s -> p (b s)")[:, 0:64:TS + 1], bank(n)[:, j:j + TS])
                        if h * MC + mc == NH * MC - 1:
                            read(i, n)
                        else:
                            step(i)
                wait_read(dve, n)
                signal(pz_ready)
                for hp in range(2):
                    n = tiles[("pvs", l, hp)]
                    wait_full(dve, n)
                    read(V.tensor_copy(o8[0:TS, hp * 512:(hp + 1) * 512], bank(n)[0:TS, :]), n)
                    if hp == 0:
                        S.upto(start("mo", l) + 3)
                n = tiles[("ots", l)]
                wait_full(dve, n)
                attended = bank(n)[:, 0:KC * TS].rearrange("p (c b) -> p c b", c=KC)
                link(V.tensor_copy(xhi[:, :, TP:T], attended))
                read(V.tensor_tensor(xlo[:, :, TP:T], attended, xhi[:, :, TP:T].bitcast(F32), ALU.subtract), n)
                nxt = start("fg", l) if l % 2 == 0 else NSPLIT
                S.upto(start("mo", l) + 4)
                residual("mo", l, 5, nxt + 2)
                if l % 2 == 0:
                    normed(3 * l + 2, l, "norm_ffn", nxt + 3)
                    S.upto(nxt + 3)
                    for half, (c0, c1) in enumerate(HALVES):
                        nxt = start(f"fd{half}", l)
                        S.upto(split[("fg", l, c0)] + 6)
                        for s in range(c0 // 2, c1 // 2):
                            for m in (2 * s, 2 * s + 1):
                                n = tiles[("fu", l, m)]
                                wait_read(dve, tiles[("fg", l, m)])
                                wait_full(dve, n)
                                read(V.tensor_tensor(hb[:, m % 2, :], bank(n)[:, 0:T], sg[:, m % 2, :], ALU.mult), n)
                            for m in (2 * s, 2 * s + 1):
                                wait_read(dve, tiles[("fu", l, m)])
                                k = step(V.tensor_copy(hhi[:, m - c0, :], hb[:, m % 2, :]))
                            after(k)
                            for m in (2 * s, 2 * s + 1):
                                V.tensor_tensor(hlo[:, m - c0, :], hb[:, m % 2, :], hhi[:, m - c0, :].bitcast(F32), ALU.subtract)\
                                    .then_inc(h_ready, 1)
                            S.upto(behind("fu", l, 2 * s + 1, 7, nxt + 3))
                        after_down = start("in", l + 1) if half else split[("fg", l, c1)]
                        residual(f"fd{half}", l, lambda m: min(down_end(half, l, m) + 3, after_down + 2), None)
            def elow(v, j):
                vv, jj = (v, j) if j < EUNITS else (v + 1, j - EUNITS)
                dve.wait_ge(ehi_ready, EUNITS * vv + jj + 1)
                V.tensor_tensor(wl[:, jj % NBUF, :], eraw(jj % ESLOTS), wh[:, jj % NBUF, :].bitcast(F32), ALU.subtract)\
                    .then_inc(eslot_free[jj % ESLOTS], 1)

            l = DEPTH - 1
            invert(tiles[("ssq", 3 * l + 2)], 0)
            for m in range(KC):
                V.scalar_tensor_tensor(out=xn[:, m, :], in0=x[:, m, :], scalar=col("norm_ffn", l, m), in1=rstd[:, 0, :],
                                       op0=ALU.mult, op1=ALU.mult).then_inc(xn_ready, 1)
            dve.wait_ge(kv_written, 32 * DEPTH)
            link(V.memset(rt[:, 0:336], 0.0))
            for j in range(NBUF):
                elow(0, j)
            n = tiles[("lg", l)]
            wait_full(dve, n)
            for t, (t0, rows) in enumerate(TOK):
                i = V.tensor_copy(lg[0:rows, t, :], bank(n)[0:rows, t * NE:(t + 1) * NE])
                if t == 2:
                    read(i, n)
                else:
                    step(i)
            wait_read(dve, n)
            after(chain[0])
            for t in range(3):
                step(V.max(out=m8[:, t, :], in_=lg[:, t, :]))
            after(chain[0])
            V.tensor_tensor(ed, m8[:, :, 1], m8[:, :, 0], ALU.subtract).then_inc(lmax_ready, 1)
            for t in range(3):
                step(V.max_index(i8[:, t, :], m8[:, t, :], lg[:, t, :]))
            after(chain[0])
            link(V.tensor_copy(fi, i8[:, :, :]))
            link(V.scalar_tensor_tensor(out=fi, in0=fi, scalar=1.0, in1=per_token(valid), op0=ALU.add, op1=ALU.mult))
            experts1 = iota[:, 1:NE + 1].unsqueeze(1).broadcast_to([P, 3, NE])
            step(V.tensor_tensor(oh, experts1, per_token(fi[:, :, 0]), ALU.is_equal))
            link(V.tensor_tensor(second, experts1, per_token(fi[:, :, 1]), ALU.is_equal))
            link(V.tensor_tensor(msk, oh, second, ALU.add))
            signal(mask_ready)
            for t, (t0, rows) in enumerate(TOK):
                for hp in range(2):
                    n = tiles[("tk", l, t, hp)]
                    cols = slice(hp * 512, (hp + 1) * 512)
                    dve.wait_ge(oh_ready, KC * DEPTH + 2 * t + hp + 1)
                    read(V.tensor_tensor(tokl[0:rows, t, cols], bank(n)[0:rows, :], tokh[0:rows, t, cols].bitcast(F32), ALU.subtract), n)
            n = tiles[("ps", l)]
            wait_full(dve, n)
            read(V.tensor_copy(pos, bank(n)[:, 0:32].rearrange("p (t e) -> p t e", t=4)), n)
            wait_read(dve, n)
            step(V.tensor_reduce(cmax, pos[:, 3, :], AX_X, ALU.max))
            link(V.scalar_tensor_tensor(out=psm[:, :, 0, :], in0=pos[:, 0:3, :], scalar=1.0, in1=msk, op0=ALU.add, op1=ALU.mult))
            step(V.tensor_copy(need[:, :], cmax))
            for b in range(MAXB - 1, -1, -1):
                link(V.tensor_scalar(psm[:, :, b, :], psm[:, :, 0, :], -1.0 - CAP * b, None, ALU.add))
            signal(route_ready)

            def gather_matrix(v):
                for t in range(3):
                    i = V.tensor_scalar(gsel[:, t, :], iota, pcol[:, t, bass.ds(v, 1)], None, ALU.is_equal)
                i.then_inc(gsel_ready, 1)

            def scatter_matrix(v):
                for t in range(3):
                    i = V.tensor_scalar(wsel[:, t, :], iota, pcol[:, t, bass.ds(v, 1)], wcol[:, t, bass.ds(v, 1)],
                                        ALU.is_equal, ALU.mult)
                i.then_inc(wsel_ready, 1)

            def combine(num):
                for c in range(KC):
                    n, more = num(f"C{c}")
                    wait_full(dve, n, more)
                    read(V.tensor_tensor(x[:, c, :], bank(n)[:, 0:T], x[:, c, :], ALU.add), n)

            def gathered_low(v, num):
                for half in range(2):
                    n, more = num(f"X{half}")
                    dve.wait_ge(xgh_ready, 2 * v + half + 1)
                    read(V.tensor_tensor(xgl[:, 4 * half:4 * half + 4, :].rearrange("p c s -> p (c s)"), bank(n)[:, :],
                                         xgh[:, 4 * half:4 * half + 4, :].rearrange("p c s -> p (c s)").bitcast(F32), ALU.subtract), n)

            def turned_low(v, num, i3):
                n, more = num(f"T{i3}")
                dve.wait_ge(ehh_ready, 3 * v + i3 + 1)
                k = min(4, FEC - 4 * i3)
                read(V.tensor_tensor(ehl[:, 4 * i3:4 * i3 + k, :].rearrange("p c s -> p (c s)"), bank(n)[:, 0:k * P],
                                     ehh[:, 4 * i3:4 * i3 + k, :].rearrange("p c s -> p (c s)").bitcast(F32), ALU.subtract), n)

            def expert(v, num, before, first, last):
                at = [NBUF]

                def upto(k):
                    while at[0] < min(k, EUNITS if last else EUNITS + NBUF):
                        elow(v, at[0])
                        at[0] += 1

                def hidden(g):
                    n, more = num(f"U{g}")
                    wait_read(dve, *num(f"G{g}"))
                    wait_full(dve, n, more)
                    if g == 0 and not first:
                        wait_full(dve, *before("T2"))
                    read(V.tensor_tensor(eh[:, g * GW:(g + 1) * GW], bank(n)[:, 0:GW], esg[:, g % 2, :], ALU.mult), n)

                if not last:
                    wait_full(dve, *before("X1"))
                    gather_matrix(v + 1)
                upto(6)
                hidden(0)
                upto(10)
                hidden(1)
                upto(14)
                hidden(2)
                upto(15)
                turned_low(v, num, 0)
                upto(18)
                hidden(3)
                turned_low(v, num, 1)
                upto(19)
                if not first:
                    combine(num)
                if not last:
                    gathered_low(v + 1, num)
                turned_low(v, num, 2)
                scatter_matrix(v)
                upto(27)

            def run_pass(p):
                v0, v1 = p.v0, p.v0 + p.nv - 1
                if v0 > 0:
                    gather_matrix(v0)
                    for j in range(NBUF):
                        elow(v0, j)
                gathered_low(v0, p.prologue)
                expert(v0, p.first, p.prologue, True, False)
                with dve.Fori(v0 + 1, v1) as v:
                    expert(v, p.middle(v), p.earlier(v), False, False)
                expert(v1, p.last, p.earlier(v1), False, True)
                combine(p.after)

            gather_matrix(0)
            dve.wait_ge(lexp_ready, 1)
            link(V.tensor_scalar(g1a, ed, 1.0, None, ALU.add))
            link(V.reciprocal(g1, g1a))
            link(V.tensor_tensor(g2, ed, g1, ALU.mult))
            step(V.tensor_tensor(oh, oh, per_token(g1), ALU.mult))
            link(V.tensor_tensor(second, second, per_token(g2), ALU.mult))
            for b in range(MAXB):
                step(V.tensor_tensor(wts[:, :, b, :], oh, second, ALU.add))
            run_pass(main)
            count = dve.value_load(need[0:1, 0:1], min_val=0, max_val=T)
            with dve.If(count > CAP):
                run_pass(extra)
            with dve.Else():
                dve.nop()
            dve.drain().then_inc(x_final, 1)
            dve.wait_ge(frms_ready, 1)
            link(V.reciprocal(rstd[:, 0, :], rms[:, 0, :]))
            for m in range(KC):
                k = VEC_FINAL + m
                V.scalar_tensor_tensor(out=xn[:, m, :], in0=x[:, m, :], scalar=vec[:, k:k + 1], in1=rstd[:, 0, :], op0=ALU.mult,
                                       op1=ALU.mult).then_inc(y_ready, 1)

        @block.gpsimd
        def _(pool):
            G = nc.gpsimd
            pool.dma_start(gatew[:, :, :, :], gate_w[0]).then_inc(s_gw, 16)
            pool.dma_start(poolw[:, :, :], pool_w[0]).then_inc(s_pw, 16)
            for l in range(DEPTH):
                if l > 0:
                    for m in range(KC):
                        wait_read(pool, tiles[("fd1", l - 1, m)])
                G.memset(pp[:, :, 0:HIST], 0.0).then_inc(padded, 1)
                G.memset(cp[:, :, 0:CW - 1], 0.0).then_inc(padded, 1)
                pool.dma_start(spool.rearrange("p c b t -> p (c b t)"), hists[l]).then_inc(hist_loaded, 16)
                pool.dma_start(sconv.rearrange("p c b t -> p (c b t)"), taps[l]).then_inc(hist_loaded, 16)
                for m in range(12):
                    wait_read(pool, tiles[("in", l, m)])
                pool.wait_ge(h_last, l + 1)
                for src, o, shape in ((pp[:, :, TP:TP + HIST], O_PP, (HIST,)), (cp[:, :, TP:TP + CW - 1], O_PC, (CW - 1,)),
                                      (cv[:, :, TP - 1:TP], O_PH, (1,)), (spool[:, :, :, 1:16], O_SP, (TS, HIST)),
                                      (sconv[:, :, :, 1:CW], O_SC, (TS, CW - 1)), (cv[:, :, TP:T], O_SH, (TS,))):
                    size = RC
                    for d in shape:
                        size *= d
                    dst = o_small[l][:, o:o + size]
                    dst = dst.rearrange("p (c t) -> p c t", c=RC) if len(shape) == 1 else \
                        dst.rearrange("p (c b t) -> p c b t", c=RC, b=TS)
                    with nc.allow_non_contiguous_dma(reason="one value per channel"):
                        pool.dma_start(dst, src).then_inc(small_written, 16)
                for m in range(KC):
                    wait_read(pool, tiles[("mk", l, m)])
                pool.dma_start(o_k[l], kT).then_inc(kv_written, 16)
                for s in range(4):
                    for mc in range(MC):
                        wait_read(pool, tiles[("mv", l, s, mc)])
                pool.dma_start(o_v[l], vN).then_inc(kv_written, 16)
                if l + 1 < DEPTH:
                    for c in range(RC):
                        wait_full(pool, tiles[("gx", l, c)])
                        wait_full(pool, tiles[("pw", l, c)])
                    pool.dma_start(gatew[:, :, :, :], gate_w[l + 1]).then_inc(s_gw, 16)
                    pool.dma_start(poolw[:, :, :], pool_w[l + 1]).then_inc(s_pw, 16)
            pool.wait_ge(y_ready, KC)
            pool.dma_start(o_y, xn[:, :, :]).then_inc(y_written, 16)
            pool.wait_ge(small_written, 96 * DEPTH)
            pool.wait_ge(kv_written, 32 * DEPTH)
            pool.wait_ge(y_written, 16)


def kernel(**inputs):
    import numpy as np
    import concourse.bacc as bacc
    from concourse.bass_utils import run_bass_kernel_spmd as run

    a = {k: np.asarray(v) for k, v in inputs.items()}

    def feat(m):
        r, f = m.shape
        return m.reshape(r, f // P, P).transpose(2, 1, 0)

    xs = feat(np.concatenate([a["x_prompt"].reshape(TP, D), a["x_sample"].reshape(TS, D)]))
    ms = feat(a["mem_prompt"].reshape(NM, D))
    cols = []
    for l in range(DEPTH):
        for name in ("norm_mix", "norm_mem", "mem_norm", "norm_ffn", "out_norm_pool", "out_norm_rnn", "pool_scale",
                     "conv_w", "conv_b", "gate_a_b", "gate_x_b", "rglru_lambda"):
            cols.append(a[name][l].reshape(-1, P).T)
    cols.append(a["final_norm"].reshape(-1, P).T)
    cols.append(a["state_h"].reshape(DEPTH, TS, RC, P).transpose(3, 0, 2, 1).reshape(P, -1))
    vecs = np.concatenate(cols, axis=1)

    taps = np.zeros((DEPTH, P, RC, TS, CW), np.float32)
    taps[..., :CW - 1] = a["state_conv"].reshape(DEPTH, TS, CW - 1, RC, P).transpose(0, 4, 3, 1, 2)
    hists = np.zeros((DEPTH, P, RC, TS, HIST + 1), np.float32)
    hists[..., :HIST] = a["state_pool"].reshape(DEPTH, TS, HIST, RC, P).transpose(0, 4, 3, 1, 2)

    con = np.zeros((P, NCONST), np.float32)
    con[:, C_ID:C_ID + P] = np.eye(P)
    con[:, C_TRI:C_TRI + P] = np.triu(np.ones((P, P)), 1)
    con[:, C_IOTA:C_IOTA + P] = np.arange(P)
    for g, w in enumerate(WINDOWS):
        con[:, C_CORR + 16 * g:C_CORR + 16 * g + 16] = w / np.minimum(np.arange(16) + 1, w)
    for t, (_, rows) in enumerate(TOK):
        con[:rows, C_VALID + t] = 1

    pw = a["pool_w"].transpose(0, 2, 1, 3)
    gw = np.zeros((DEPTH, P, 2, RC, P), np.float32)
    for i, name in enumerate(("gate_a_w", "gate_x_w")):
        w = a[name].reshape(DEPTH, RC, 2, 64, 64)
        for j in range(2):
            gw[:, 64 * j:64 * j + 64, i, :, 64 * j:64 * j + 64] = w[:, :, j].transpose(0, 2, 1, 3)
    rw = a["router_w"][0].reshape(KC, P, NE).transpose(1, 0, 2)

    def columns(w, i):
        s, half = i // 2, i % 2
        return w[512 * half:512 * half + 512, s * PIECE:(s + 1) * PIECE].reshape(4, P, PIECE).transpose(1, 0, 2)

    dense = np.empty((len(stream_plan()), P, 4, PIECE), np.float32)
    order = np.r_[D // 2:D, D:3 * D // 2, 0:D // 2]
    names = {"mk": "w_mk", "mv": "w_mv", "out": "w_out", "mq": "w_mq", "mo": "w_mo"}
    win = a["w_in"][:, :, order]
    ck = a["cache_mem_k"].reshape(DEPTH, 4, 2, NM, NH, HC, P)
    cvv = a["cache_mem_v"].reshape(DEPTH, 4, 2, MC, P, NH, HD)
    fd = a["ffn_w_down"].reshape(-1, FC, P, KC // 2, PIECE)
    for k, (kind, l, i) in enumerate(stream_plan()):
        if kind in names:
            dense[k] = columns(a[names[kind]][l], i)
        elif kind == "in":
            dense[k] = columns(win[l], i)
        elif kind == "fg":
            dense[k] = columns(a["ffn_w_gate"][l // 2], i)
        elif kind == "fu":
            dense[k] = columns(a["ffn_w_up"][l // 2], i)
        elif kind == "kc":
            dense[k] = ck[l, i % 4, :, :, i // 4].transpose(3, 0, 2, 1).reshape(P, 4, NM)
        elif kind == "vc":
            dense[k] = cvv[l, i % 4, :, :, :, i // 4].transpose(2, 0, 1, 3).reshape(P, 4, HD)
        else:
            c0, c1 = HALVES[int(kind[2])]
            pieces = fd[l // 2, c0:c1].transpose(2, 0, 1, 3).reshape(-1, P, PIECE)
            dense[k] = pieces[4 * i:4 * i + 4].transpose(1, 0, 2)

    ex = np.empty((NE, EUNITS, P, EUNIT), np.float32)
    gu = ex[:, 0:16].reshape(NE, 4, 2, 2, P, 4, GW)
    for i, name in enumerate(("moe_w_gate", "moe_w_up")):
        gu[:, :, i] = a[name][0].reshape(NE, 2, 4, P, 4, GW).transpose(0, 4, 1, 3, 2, 5)
    ex[:, 0:16] = gu.reshape(NE, 16, P, EUNIT)
    w = a["moe_w_down"][0].reshape(NE, FEC, P, 4, PIECE).transpose(0, 3, 2, 1, 4).reshape(NE, 4, P, 2, EUNIT)
    ex[:, 16:] = w.transpose(0, 1, 3, 2, 4).reshape(NE, 8, P, EUNIT)

    arrays = {"xT": xs, "memT": ms, "vecs": vecs, "taps": taps.reshape(DEPTH, P, -1), "hists": hists.reshape(DEPTH, P, -1), "consts": con, "pool_w": pw, "gate_w": gw, "router_w": rw,
              "dense": dense.reshape(-1, P, UNIT), "experts": ex.reshape(NE * EUNITS, P, EUNIT)}
    arrays = {k: np.ascontiguousarray(v) for k, v in arrays.items()}
    nc = bacc.Bacc("TRN2", target_bir_lowering=False, num_devices=1)
    args = [nc.dram_tensor(k, v.shape, F32, kind="ExternalInput").ap() for k, v in arrays.items()]
    outs = {"o_y": (P, KC, T), "o_small": (DEPTH, P, NOUT), "o_k": (DEPTH, P, KC, NM), "o_v": (DEPTH, P, MC, D)}
    args += [nc.dram_tensor(k, s, F32, kind="ExternalOutput").ap() for k, s in outs.items()]
    trunk_kernel(nc, *args)
    r = run(nc, [arrays], core_ids=[0]).results[0]

    y = r["o_y"].transpose(2, 1, 0).reshape(T, D)
    sm = r["o_small"]

    def part(o, *dims):
        size = RC * int(np.prod(dims))
        return sm[:, :, o:o + size].reshape(DEPTH, P, RC, *dims)

    half = D // 2
    pool_p = part(O_PP, HIST).transpose(0, 3, 2, 1).reshape(DEPTH, 1, HIST, half)
    conv_p = part(O_PC, CW - 1).transpose(0, 3, 2, 1).reshape(DEPTH, 1, CW - 1, half)
    h_p = part(O_PH).transpose(0, 2, 1).reshape(DEPTH, 1, half)
    pool_s = part(O_SP, TS, HIST).transpose(0, 3, 4, 2, 1).reshape(DEPTH, TS, HIST, half)
    conv_s = part(O_SC, TS, CW - 1).transpose(0, 3, 4, 2, 1).reshape(DEPTH, TS, CW - 1, half)
    h_s = part(O_SH, TS).transpose(0, 3, 2, 1).reshape(DEPTH, TS, half)
    mk = r["o_k"].transpose(0, 3, 2, 1).reshape(DEPTH, 1, NM, NH, HD)
    mv = r["o_v"].transpose(0, 2, 1, 3).reshape(DEPTH, 1, NM, NH, HD)
    return (y[:TP].reshape(1, TP, D), y[TP:].reshape(TS, 1, D), pool_p, conv_p, h_p, mk, mv, pool_s, conv_s, h_s)
```

```python
from contextlib import ExitStack

import concourse.bass as bass
from concourse import mybir

ALU = mybir.AluOpType
ACT = mybir.ActivationFunctionType
F32 = mybir.dt.float32
F32R = mybir.dt.float32r
U32 = mybir.dt.uint32
I32 = mybir.dt.int32
AX_X = mybir.AxisListType.X

P = 128
D = 1024
KC = D // P
TP, TS = 256, 8
T = TP + TS
DEPTH = 2
NM = 256
MC = NM // P
NH, HD = 4, 256
HC = HD // P
WINDOWS = (2, 4, 8, 16)
HIST = 15
CW = 4
RC = 4
FF = 2816
FC = FF // P
NE = 8
FE = FF // 2
FEC = FE // P
EPS = 1e-6

PIECE = 256
UNIT = 4 * PIECE
GW = FE // 4
EUNIT = KC // 2 * GW
ESLOTS = 6
RING = ESLOTS * EUNIT
SLOTS = RING // UNIT
NBUF = 3
EUNITS = 24
assert 4 * KC * GW * 2 // EUNIT == 16 and FEC * D // EUNIT == 8 and EUNITS % ESLOTS == 0 and EUNITS % NBUF == 0
HALVES = [(0, 12), (12, 22)]

VEC = {}
_n = 0
for _name, _cols in (("norm_mix", 8), ("norm_mem", 8), ("mem_norm", 8), ("norm_ffn", 8), ("out_norm_pool", 4),
                     ("out_norm_rnn", 4), ("pool_scale", 4), ("conv_w", 16), ("conv_b", 4), ("gate_a_b", 4),
                     ("gate_x_b", 4), ("rglru_lambda", 4)):
    VEC[_name] = _n
    _n += _cols
LVEC = _n
VEC_FINAL = DEPTH * LVEC
VEC_H0 = VEC_FINAL + KC
NVEC = VEC_H0 + DEPTH * RC * TS
C_ID, C_TRI, C_IOTA, C_CORR, C_VALID = 0, P, 2 * P, 3 * P, 3 * P + 4 * 16
NCONST = C_VALID + 3
O_PP = 0
O_PC = O_PP + RC * HIST
O_PH = O_PC + RC * (CW - 1)
O_SP = O_PH + RC
O_SC = O_SP + RC * TS * HIST
O_SH = O_SC + RC * TS * (CW - 1)
NOUT = O_SH + RC * TS

TOK = [(0, P), (P, P), (TP, TS)]
BLOCKS = NE
MAXB = (T + P - 1) // P
CAP = P


KEYS_FIRST = (3, 2)
LATE = {0: [("kn", 0, 3), ("kf", 1, 2)], 1: [("kn", 1, 3)]}


def key_tile(l, m):
    if m // 2 < KEYS_FIRST[l]:
        return "mk", l, m
    return next((kind, at, m % 2) for at, late in LATE.items() for kind, layer, pair in late if (layer, pair) == (l, m // 2))


def stream_plan():
    out = []

    def add(kind, l, n):
        out.extend((kind, l, i) for i in range(n))

    for l in range(DEPTH):
        for kind, n in (("in", 12), ("mk", 2 * KEYS_FIRST[l]), ("mv", 8), ("out", 8), ("kn", 2), ("mq", 8), ("kc", 16),
                        ("vc", 16), ("mo", 8)):
            add(kind, l, n)
        if l % 2 == 0:
            add("kf", l, 2)
            for half, (c0, c1) in enumerate(HALVES):
                for s in range(c0 // 2, c1 // 2):
                    out += [("fg", l, 2 * s), ("fg", l, 2 * s + 1), ("fu", l, 2 * s), ("fu", l, 2 * s + 1)]
                add(f"fd{half}", l, (c1 - c0))
    return out


RAW = ("kc", "vc")


def bank_plan():
    out = []
    for l in range(DEPTH):
        out += [("ssq", 3 * l)]
        out += [("in", l, m) for m in range(6)]
        if l == 0:
            out += [("msq",)]
        out += [("in", l, m) for m in range(6, 12)]
        out += [("mk", l, m) for m in range(2 * KEYS_FIRST[l])]
        out += [("ga", l, c) for c in range(RC)] + [("gx", l, c) for c in range(RC)]
        out += [("mv", l, s, mc) for s in range(2) for mc in range(MC)]
        out += [("pw", l, c) for c in range(RC)]
        out += [("mv", l, 2, mc) for mc in range(MC)]
        out += [("psq", l)]
        out += [("mv", l, 3, mc) for mc in range(MC)]
        out += [("rsq", l)]
        out += [("out", l, m) for m in range(KC)]
        out += [("ssq", 3 * l + 1)]
        out += [("kn", l, u) for u in range(2)]
        out += [("mq", l, m) for m in range(KC)]
        out += [("sc", l, t, hp) for t in range(3) for hp in range(2)]
        out += [("pt", l, h) for h in range(NH)]
        out += [("pv", l, m) for m in range(KC)]
        out += [("pts", l)]
        out += [("pvs", l, hp) for hp in range(2)]
        out += [("ots", l)]
        out += [("mo", l, m) for m in range(KC)]
        out += [("ssq", 3 * l + 2)]
        if l % 2 == 0:
            out += [("kf", l, u) for u in range(2)]
            for half, (c0, c1) in enumerate(HALVES):
                for s in range(c0 // 2, c1 // 2):
                    out += [("fg", l, 2 * s), ("fg", l, 2 * s + 1), ("fu", l, 2 * s), ("fu", l, 2 * s + 1)]
                out += [(f"fd{half}", l, m) for m in range(KC)]
        else:
            out += [("lg", l, t) for t in range(3)]
            out += [("tk", l, t, hp) for t in range(3) for hp in range(2)]
            out += [("ps", l)]
    return out


def trunk_kernel(nc, xT, memT, vecs, taps, hists, consts, pool_w, gate_w, router_w, dense, experts,
                 o_y, o_small, o_k, o_v):
    units = {name: k for k, name in enumerate(stream_plan())}
    split = {name: k for k, name in enumerate(x for x in stream_plan() if x[0] not in RAW)}
    tiles = {name: n for n, name in enumerate(bank_plan())}
    NUNIT = len(units)
    NSPLIT = len(split)
    NT0 = len(tiles)

    HIDDEN = ["G0", "U0", "G1", "U1", "G2", "U2", "T0", "S", "G3", "U3", "T1"]
    COMBINE = [f"C{c}" for c in range(KC)]
    GATHER = [f"X{i}" for i in range(4)]
    OUTPUT = ["T2", "D0", "D1"]
    MID = ["a" + x for x in HIDDEN + COMBINE + OUTPUT] + ["b" + x for x in HIDDEN + COMBINE + GATHER + OUTPUT]
    FIRST = ["a" + x for x in HIDDEN + OUTPUT if x != "S"] + [x for x in MID if x[0] == "b"]
    LAST = [x for x in MID if x[1] != "X"]
    TAIL = ["S"] + COMBINE
    assert len(MID) == 48

    class Pass:

        def __init__(self, n0, v0, nv):
            self.n0, self.p0, self.np = n0, v0 // 2, nv // 2
            self.mid = n0 + len(GATHER) + len(FIRST)
            self.tail = self.mid + len(MID) * (self.np - 2) + len(LAST)
            self.end = self.tail + len(TAIL)

        def first(self, kind):
            return self.n0 + len(GATHER) + FIRST.index(kind), 0

        def middle(self, p):
            return lambda kind: (self.mid + MID.index(kind), 2 * (p - (self.p0 + 1)))

        def last(self, kind):
            return self.mid + len(MID) * (self.np - 2) + LAST.index(kind), 0

        def after(self, kind):
            return self.tail + TAIL.index(kind), 0

        def earlier(self, p):
            return lambda kind: (self.mid + MID.index("b" + kind) - len(MID), 2 * (p - (self.p0 + 1)))

        def prologue(self, kind):
            return self.n0 + GATHER.index(kind), 0

    def block_of(num, name):
        return lambda kind: num(name + kind)

    with ExitStack() as ctx:
        def sb(name, shape, dt=F32):
            return ctx.enter_context(nc.sbuf_tensor(name, shape, dt))

        def sem(name):
            return ctx.enter_context(nc.semaphore(name))

        ring = sb("ring", [P, RING])
        x = sb("x", [P, KC, T])
        sq = sb("sq", [P, KC, T])
        xh = sb("xh", [P, (FEC + 6) * P], F32R)
        xl = sb("xl", [P, (FEC + 2 * KC) * P], F32R)
        wh = sb("wh", [P, NBUF, EUNIT], F32R)
        wl = sb("wl", [P, NBUF, EUNIT], F32R)
        hh_t = sb("hidden_hi", [P, 12 * T], F32R)
        hl_t = sb("hidden_lo", [P, 12 * T], F32R)
        xg_t = sb("gathered_hi", [P, 2 * KC * P], F32R)
        vec = sb("vec", [P, NVEC])
        con = sb("con", [P, NCONST])
        ones = sb("ones", [P, P])
        eps = sb("eps", [P, 1])
        rms = sb("rms", [P, 2, T])
        rstd = sb("rstd", [P, 2, T])
        mem = sb("mem", [P, KC, NM])
        poolw = sb("poolw", [P, RC, P])
        gatew = sb("gatew", [P, 2, RC, P])
        rw = sb("rw", [P, KC, NE])
        coef = sb("coef", [P, 6, DEPTH * RC])
        kv = sb("kv", [P, KC * NM + MC * D])
        kT = kv[:, 0:KC * NM].rearrange("p (c m) -> p c m", c=KC)
        vN = kv[:, KC * NM:].rearrange("p (c n) -> p c n", c=MC)

        def chunks(t, c, n):
            return t[:, 0:c * n].rearrange("p (c t) -> p c t", c=c)

        xhi, xlo = chunks(xh, KC, T), chunks(xl, KC, T)
        mhi, mlo = chunks(hh_t, KC, NM), chunks(hl_t, KC, NM)
        hhi, hlo = chunks(hh_t, 12, T), chunks(hl_t, 12, T)
        xn = sq
        small = sb("small", [P, 96])

        WORK = 8096
        work = sb("work", [P, WORK])
        at = [0]

        def take(n):
            at[0] += n
            assert at[0] <= WORK, at[0]
            return work[:, at[0] - n:at[0]]

        PADP = HIST + TP
        pp = take(RC * PADP).rearrange("p (c t) -> p c t", c=RC)
        spool = take(RC * TS * 16).rearrange("p (c b t) -> p c b t", c=RC, b=TS)
        PADC = CW - 1 + TP
        cp = take(RC * PADC).rearrange("p (c t) -> p c t", c=RC)
        sconv = take(RC * TS * CW).rearrange("p (c b t) -> p c b t", c=RC, b=TS)
        cv = take(RC * T).rearrange("p (c t) -> p c t", c=RC)
        wA = take(RC * 270)
        wB = take(RC * 270)
        lad = [wA.rearrange("p (c t) -> p c t", c=RC), wB.rearrange("p (c t) -> p c t", c=RC)]
        r_g = take(RC * T).rearrange("p (c t) -> p c t", c=RC)
        i_g = take(RC * T).rearrange("p (c t) -> p c t", c=RC)
        ml = wB[:, 0:RC * T].rearrange("p (c t) -> p c t", c=RC)
        z = sq[:, 0:RC, :]
        gel = sq[:, RC:2 * RC, :]
        yr = i_g
        yp = wA[:, 0:RC * T].rearrange("p (c t) -> p c t", c=RC)
        ss = small[:, 0:RC * TS].rearrange("p (c b) -> p c b", c=RC)
        mx = small[:, 32:32 + 12]
        nmx = small[:, 44:44 + 12]
        sm = small[:, 56:56 + 12]
        rs = small[:, 68:68 + 12]

        msq = kv[:, 0:KC * NM].rearrange("p (c m) -> p c m", c=KC)
        at[0] = 0
        pr = take(3 * NH * NM).rearrange("p (t h m) -> p t h m", t=3, h=NH)
        o8 = pr[:, 0:2, :, :].rearrange("p t h m -> p (t h m)")[:, 0:D]
        pT = take(NH * MC * TP).rearrange("p (h c t) -> p h c t", h=NH, c=MC)
        qz = take(KC * TS * TS).rearrange("p (c b s) -> p c b s", c=KC, b=TS)
        pz = take(NH * MC * TS * TS).rearrange("p (h c b s) -> p h c b s", h=NH, c=MC, b=TS)
        q = sq
        at[0] = 0
        sg = take(2 * T).rearrange("p (c t) -> p c t", c=2)
        hb = take(2 * T).rearrange("p (c t) -> p c t", c=2)
        at[0] = 0
        wsel = take(3 * CAP).rearrange("p (t s) -> p t s", t=3)
        esg = take(2 * GW).rearrange("p (i n) -> p i n", i=2)
        eh = take(FE)
        tokh, tokl = chunks(hh_t, 3, D), chunks(hl_t, 3, D)
        xgh = xg_t[:, :].rearrange("p (c b s) -> p c b s", c=KC, b=2)
        xgl = xl[:, FEC * CAP:].rearrange("p (c b s) -> p c b s", c=KC, b=2)
        ehh, ehl = chunks(xh, FEC, CAP), chunks(xl, FEC, CAP)
        gsel = xh[:, FEC * CAP:(FEC + 6) * CAP].rearrange("p (t b s) -> p t b s", t=3, b=2)
        eo = kv[:, 0:D]
        scat = kv[:, D:D + T]
        rt = kv[:, 2 * D:3 * D]
        lg = rt[:, 0:24].rearrange("p (t e) -> p t e", t=3)
        m8 = rt[:, 24:48].rearrange("p (t e) -> p t e", t=3)
        fi = rt[:, 48:72].rearrange("p (t e) -> p t e", t=3)
        ed = rt[:, 72:75]
        g1 = rt[:, 75:78]
        g2 = rt[:, 78:81]
        oh = rt[:, 81:105].rearrange("p (t e) -> p t e", t=3)
        msk = rt[:, 105:129].rearrange("p (t e) -> p t e", t=3)
        wts = rt[:, 129:129 + 72].rearrange("p (t b e) -> p t b e", t=3, b=MAXB)
        wcol = rt[:, 129:129 + 72].rearrange("p (t v) -> p t v", t=3)
        psm = rt[:, 201:201 + 72].rearrange("p (t b e) -> p t b e", t=3, b=MAXB)
        pcol = rt[:, 201:201 + 72].rearrange("p (t v) -> p t v", t=3)
        pos = rt[:, 273:305].rearrange("p (t e) -> p t e", t=4)
        cmax = rt[:, 305:306]
        g1a = rt[:, 306:309]
        second = rt[:, 309:333].rearrange("p (t e) -> p t e", t=3)

        def per_token(a):
            return a.unsqueeze(2).broadcast_to([P, 3, NE])

        i8 = sb("i8", [P, 3, 8], U32)
        need = sb("need", [P, 1], I32)

        ident = con[:, C_ID:C_ID + P]
        tri = con[:, C_TRI:C_TRI + P]
        iota = con[:, C_IOTA:C_IOTA + P]
        corr = con[:, C_CORR:C_CORR + 64].rearrange("p (g t) -> p g t", g=4)
        valid = con[:, C_VALID:C_VALID + 3]

        psum = [ctx.enter_context(nc.psum_tensor(f"bank{b}", [P, 512], F32)) for b in range(8)]

        bank_full = [sem(f"bank_full{b}") for b in range(8)]
        bank_read = [sem(f"bank_read{b}") for b in range(8)]
        slot_loaded = [sem(f"slot_loaded{s}") for s in range(SLOTS)]
        slot_free = [sem(f"slot_free{s}") for s in range(SLOTS)]
        hi_ready = sem("weight_hi_ready")
        unit_used = sem("unit_used")
        eslot_loaded = [sem(f"eslot_loaded{s}") for s in range(ESLOTS)]
        eslot_free = [sem(f"eslot_free{s}") for s in range(ESLOTS)]
        ehi_ready = sem("expert_weight_hi_ready")
        eunit_used = sem("expert_unit_used")
        s_x = [sem(f"x_loaded{h}") for h in range(2)]
        s_vec = sem("vectors_loaded")
        s_mem = sem("mem_loaded")
        s_con = sem("consts_loaded")
        s_pw = sem("pool_w_loaded")
        s_gw = sem("gate_w_loaded")
        s_rw = sem("router_loaded")
        s_set = sem("constants_set")
        sq_ready = sem("squares_ready")
        xn_ready = sem("normed_ready")
        fn_ready = sem("normed_full_ready")
        xh_ready = sem("normed_hi_ready")
        oh_ready = sem("attended_hi_ready")
        h_ready = sem("hidden_parts_ready")
        mh_ready = sem("memory_hi_ready")
        xgh_ready = sem("gathered_hi_ready")
        ehh_ready = sem("expert_hidden_hi_ready")
        msq_ready = sem("mem_squares_ready")
        mem_normed = sem("mem_normed")
        mn_ready = sem("gained_memory_ready")
        padded = sem("zero_histories_set")
        hist_loaded = sem("sample_histories_loaded")
        cv_ready = sem("conv_ready")
        gates_ready = sem("gates_ready")
        z_ready = sem("pool_difference_ready")
        yr_ready = sem("y_rnn_ready")
        psq_ready = sem("y_pool_squares_ready")
        rsq_ready = sem("y_rnn_squares_ready")
        mixed_ready = sem("mixed_ready")
        decay_exp = sem("decay_exp_ready")
        decay_in = sem("decay_abs_ready")
        coef_ready = sem("decay_ready")
        h_last = sem("recurrence_ready")
        small_written = sem("small_outputs_written")
        kv_written = sem("keys_values_written")
        qz_ready = sem("sample_queries_ready")
        max_ready = sem("max_ready")
        exp_done = sem("exp_half_done")
        p_ready = sem("probs_ready")
        pz_ready = sem("sample_probs_ready")
        lmax_ready = sem("top_ready")
        lexp_ready = sem("gate_exp_ready")
        mask_ready = sem("mask_ready")
        route_ready = sem("route_ready")
        gsel_ready = sem("gather_matrix_ready")
        wsel_ready = sem("scatter_matrix_ready")
        x_final = sem("x_final")
        fsq_ready = sem("final_squares_ready")
        fsum_ready = sem("final_sum_ready")
        frms_ready = sem("final_rms_ready")
        y_ready = sem("y_ready")
        y_written = sem("y_written")
        dve_chain = sem("dve_chain")
        act_chain = sem("act_chain")

        def col(name, l, c):
            k = l * LVEC + VEC[name] + c
            return vec[:, k:k + 1]

        def bank(n):
            return psum[n % 8]

        def raw(k):
            s = k % SLOTS
            return ring[:, s * UNIT:(s + 1) * UNIT]

        def eraw(s):
            return ring[:, s * EUNIT:(s + 1) * EUNIT]

        ends = {}
        for (kind, l, i), k in split.items():
            if kind in ("in", "mk", "kn", "kf", "out", "mq", "mo", "fg", "fu") and i % 2:
                ends[k] = tiles[(kind, l, i)]
            elif kind == "mv" and i % 2:
                ends[k] = tiles[(kind, l, i // 2, MC - 1)]
            elif kind[:2] == "fd":
                c0, c1 = HALVES[int(kind[2])]
                if 4 * (i + 1) % (c1 - c0) == 0:
                    ends[k] = tiles[(kind, l, 2 * (4 * (i + 1) // (c1 - c0)) - 1)]
        others = [k for k in range(NSPLIT) if k not in ends]

        def wait_used(eng, k):
            if k in ends:
                wait_full(eng, ends[k])
            else:
                eng.wait_ge(unit_used, others.index(k) + 1)

        EENDS = {4 * g + 1 + 2 * i: f"{'GU'[i]}{g}" for g in range(4) for i in range(2)}
        EENDS.update({19: "D0", 23: "D1"})
        EOTHERS = [j for j in range(EUNITS) if j not in EENDS]

        def wait_eused(eng, v, num, j):
            if j in EENDS:
                wait_full(eng, *num(EENDS[j]))
            else:
                eng.wait_ge(eunit_used, len(EOTHERS) * v + EOTHERS.index(j) + 1)

        def ewait(eng, sems, j, v, per=1):
            eng.wait_ge(sems[j % ESLOTS], per * (EUNITS // ESLOTS * v + j // ESLOTS + 1))

        def wait_full(eng, n, more=0):
            eng.wait_ge(bank_full[n % 8], n // 8 + 1 + 3 * more)

        def wait_read(eng, n, more=0):
            eng.wait_ge(bank_read[n % 8], n // 8 + 1 + 3 * more)

        class Splitter:

            def __init__(self, one):
                self.at, self.one = 0, one

            def upto(self, k):
                while self.at < min(k, NSPLIT):
                    self.one(self.at)
                    self.at += 1

        names = list(split)

        def start(kind, l):
            return split[(kind, l, 0)]

        def down_end(half, l, m):
            c0, c1 = HALVES[half]
            return start(f"fd{half}", l) + ((m // 2 + 1) * (c1 - c0) - 1) // 4

        def behind(kind, l, i, ahead, last):
            return min(split[(kind, l, i)] + ahead, last)

        block = ctx.enter_context(nc.Block())
        main = Pass(NT0, 0, NE)
        extra = Pass(main.end, NE, NE * (MAXB - 1))

        @block.sync
        def _(sp):
            for h in range(2):
                sp.dma_start(x[:, 4 * h:4 * h + 4, :], xT[:, 4 * h:4 * h + 4, :]).then_inc(s_x[h], 16)

            def load(k, dram_k):
                s = k % SLOTS
                sp.dma_start(raw(s), dense[dram_k]).then_inc(slot_loaded[s], 16)

            for k in range(SLOTS):
                load(k, k)
                if k == 3:
                    sp.dma_start(mem[:, :, :], memT).then_inc(s_mem, 16)
            rounds = NUNIT // SLOTS
            with sp.Fori(1, rounds) as r:
                for s in range(SLOTS):
                    sp.wait_ge(slot_free[s], r)
                    load(s, SLOTS * r + s)
            for k in range(rounds * SLOTS, NUNIT):
                sp.wait_ge(slot_free[k % SLOTS], k // SLOTS)
                load(k, k)

            def eload(e, j):
                s = j % ESLOTS
                sp.dma_start(eraw(s), experts[EUNITS * e + j]).then_inc(eslot_loaded[s], 16)

            def block_loads(v, e, j0=0):
                for j in range(j0, EUNITS):
                    sp.wait_ge(eslot_free[j % ESLOTS], EUNITS // ESLOTS * v + j // ESLOTS)
                    eload(e, j)

            for j in range(ESLOTS):
                for s in range(SLOTS):
                    if s * UNIT < (j + 1) * EUNIT and (s + 1) * UNIT > j * EUNIT:
                        sp.wait_ge(slot_free[s], (NUNIT - 1 - s) // SLOTS + 1)
                eload(0, j)
            block_loads(0, 0, ESLOTS)
            with sp.Fori(1, NE) as v:
                block_loads(v, v)
            sp.wait_ge(route_ready, 1)
            count = sp.value_load(need[0:1, 0:1], min_val=0, max_val=T)
            with sp.If(count > CAP):
                for b in range(1, MAXB):
                    with sp.Fori(0, NE) as e:
                        block_loads(NE * b + e, e)
            with sp.Else():
                sp.nop()
            for c in range(0, KC, 2):
                sp.wait_ge(y_ready, c + 2)
                sp.dma_start(o_y[:, c:c + 2, :], xn[:, c:c + 2, :]).then_inc(y_written, 16)
            sp.wait_ge(y_written, 64)

        @block.tensor
        def _(pe):
            mm = nc.tensor.matmul

            def take_bank(n, more=0):
                if n >= 8:
                    pe.wait_ge(bank_read[n % 8], n // 8 + 3 * more)
                return bank(n)

            def full(ins, n):
                ins.then_inc(bank_full[n % 8], 1)

            def product(out, s_hi, s_lo, m_hi, m_lo, start, stop, stationary_weights=True):
                if stationary_weights:
                    mm(out, s_hi, m_hi, start=start, stop=False)
                    mm(out, s_hi, m_lo, start=False, stop=False)
                    return mm(out, s_lo, m_hi, start=False, stop=stop)
                mm(out, s_hi, m_hi, start=start, stop=False)
                mm(out, s_lo, m_hi, start=False, stop=False)
                return mm(out, s_hi, m_lo, start=False, stop=stop)

            def unit(name):
                k = units[name]
                pe.wait_ge(slot_free[k % SLOTS], k // SLOTS + 1)
                b = split[name] % NBUF
                return [w[:, b, 0:UNIT].rearrange("p (k n) -> p k n", k=4) for w in (wh, wl)]

            def raw_unit(name):
                k = units[name]
                pe.wait_ge(slot_loaded[k % SLOTS], 16 * (k // SLOTS + 1))
                return raw(k).rearrange("p (k n) -> p k n", k=4)

            def frees(ins, name):
                ins.then_inc(slot_free[units[name] % SLOTS], 1)

            def norm_sum(key, j):
                n = tiles[key]
                b = take_bank(n)
                for m in range(KC):
                    pe.wait_ge(sq_ready, KC * j + m + 1)
                    i = mm(b[:, 0:T], ones[:, :], sq[:, m, :], start=(m == 0), stop=(m == KC - 1))
                full(i, n)

            def mixer_sum(key, l, ready, o):
                n = tiles[(key, l)]
                b = take_bank(n)
                for c in range(RC):
                    pe.wait_ge(ready, RC * l + c + 1)
                    i = mm(b[:, 0:T], ones[:, :], sq[:, o + c, :], start=(c == 0), stop=(c == RC - 1))
                full(i, n)

            def project_pair(key, l, s, hi, lo, width, ready=None, base=0):
                nn = [tiles[(key, l, 2 * s + u)] for u in range(2)]
                bb = [take_bank(n) for n in nn]
                for half in range(2):
                    w_hi, w_lo = unit((key, l, 2 * s + half))
                    for u in range(2):
                        for k4 in range(4):
                            kc = 4 * half + k4
                            if u == 0 and ready is not None:
                                pe.wait_ge(ready, base + kc + 1)
                            i = product(bb[u][:, 0:width], w_hi[:, k4, u * P:(u + 1) * P], w_lo[:, k4, u * P:(u + 1) * P],
                                        hi[:, kc, :], lo[:, kc, :], start=(kc == 0), stop=(kc == KC - 1))
                        if half:
                            full(i, nn[u])
                        elif u:
                            i.then_inc(unit_used, 1)

            def project(key, l, hi, lo, width, ready=None, base=0):
                for s in range(KEYS_FIRST[l] if key == "mk" else 4):
                    project_pair(key, l, s, hi, lo, width, ready if s == 0 else None, base)

            pe.wait_ge(s_set, 2)
            for l in range(DEPTH):
                norm_sum(("ssq", 3 * l), 3 * l)
                for s in range(6):
                    if l == 0 and s == 3:
                        n = tiles[("msq",)]
                        b = take_bank(n)
                        for m in range(KC):
                            pe.wait_ge(msq_ready, m + 1)
                            i = mm(b[:, 0:NM], ones[:, :], msq[:, m, :], start=(m == 0), stop=(m == KC - 1))
                        full(i, n)
                    project_pair("in", l, s, xhi, xlo, T, xn_ready if s == 0 else None, KC * 3 * l)
                project("mk", l, mhi, mlo, NM, mn_ready, 2 * KC * l)
                pe.wait_ge(s_gw, 16 * (l + 1))
                pe.wait_ge(s_pw, 16 * (l + 1))
                pe.wait_ge(cv_ready, l + 1)
                for gi, key in enumerate(("ga", "gx")):
                    for c in range(RC):
                        n = tiles[(key, l, c)]
                        b = take_bank(n)
                        full(mm(b[:, 0:T], gatew[:, gi, c, :], cv[:, c, :], start=True, stop=True), n)
                for s in range(4):
                    if s == 2:
                        pe.wait_ge(z_ready, l + 1)
                        for c in range(RC):
                            n = tiles[("pw", l, c)]
                            b = take_bank(n)
                            full(mm(b[:, 0:T], poolw[:, c, :], z[:, c, :], start=True, stop=True), n)
                    elif s == 3:
                        mixer_sum("psq", l, psq_ready, 0)
                    nn = [tiles[("mv", l, s, mc)] for mc in range(MC)]
                    bb = [take_bank(n) for n in nn]
                    for half in range(2):
                        w_hi, w_lo = unit(("mv", l, 2 * s + half))
                        for mc in range(MC):
                            for k4 in range(4):
                                kc = 4 * half + k4
                                i = product(bb[mc][:, 0:PIECE], mhi[:, kc, mc * P:(mc + 1) * P], mlo[:, kc, mc * P:(mc + 1) * P],
                                            w_hi[:, k4, :], w_lo[:, k4, :], kc == 0, kc == KC - 1, False)
                            if half:
                                full(i, nn[mc])
                            elif mc:
                                i.then_inc(unit_used, 1)
                        if s == 3 and half == 0:
                            mixer_sum("rsq", l, rsq_ready, RC)
                project("out", l, xhi, xlo, T, mixed_ready, KC * l)
                norm_sum(("ssq", 3 * l + 1), 3 * l + 1)
                project_pair("kn", l, 0, mhi, mlo, NM)
                project("mq", l, xhi, xlo, T, xn_ready, KC * (3 * l + 1))
                for m in range(KC):
                    wait_read(pe, tiles[key_tile(l, m)])
                    wait_read(pe, tiles[("mq", l, m)])
                for t in range(2):
                    for hp in range(2):
                        n = tiles[("sc", l, t, hp)]
                        b = take_bank(n)
                        for hh in range(2):
                            h = 2 * hp + hh
                            for c in range(HC):
                                i = mm(b[:, hh * NM:(hh + 1) * NM], q[:, HC * h + c, t * P:(t + 1) * P], kT[:, HC * h + c, :],
                                       start=(c == 0), stop=(c == HC - 1))
                        full(i, n)
                pe.wait_ge(qz_ready, l + 1)
                for u in range(16):
                    h = u // 4
                    n = tiles[("sc", l, 2, h // 2)]
                    if u % 8 == 0:
                        b = take_bank(n)
                    w = raw_unit(("kc", l, u))
                    for b2 in range(2):
                        for c in range(HC):
                            i = mm(b[0:TS, (h % 2) * NM:(h % 2 + 1) * NM], qz[:, HC * h + c, 2 * (u % 4) + b2, :], w[:, 2 * b2 + c, :],
                                   start=(u % 4 + b2 + c == 0), stop=(u % 4 == 3 and b2 + c == 2))
                            if b2 + c == 0 and u > 0:
                                frees(i, ("kc", l, u - 1))
                    if u % 8 == 7:
                        full(i, n)
                for h in range(NH):
                    n = tiles[("pt", l, h)]
                    b = take_bank(n)
                    for t in range(2):
                        pe.wait_ge(p_ready, 6 * l + 2 * t + h // 2 + 1)
                        for mc in range(MC):
                            i = nc.tensor.transpose(b[:, mc * TP + t * P:mc * TP + (t + 1) * P], pr[:, t, h, mc * P:(mc + 1) * P], ident)
                            if h + t + mc == 0:
                                frees(i, ("kc", l, 15))
                    full(i, n)
                for s in range(4):
                    for mc in range(MC):
                        wait_read(pe, tiles[("mv", l, s, mc)])
                for m in range(KC):
                    n = tiles[("pv", l, m)]
                    b = take_bank(n)
                    h = m // HC
                    wait_read(pe, tiles[("pt", l, h)])
                    for mc in range(MC):
                        i = mm(b[:, 0:TP], vN[:, mc, m * P:(m + 1) * P], pT[:, h, mc, :], start=(mc == 0), stop=(mc == MC - 1))
                    full(i, n)
                n = tiles[("pts", l)]
                b = take_bank(n)
                pe.wait_ge(p_ready, 6 * l + 6)
                for h in range(NH):
                    for mc in range(MC):
                        j = (h * MC + mc) * TS
                        i = nc.tensor.transpose(b[:, j:j + TS], pr[0:TS, 2, h, mc * P:(mc + 1) * P], ident[0:TS, 0:TS])
                full(i, n)
                pe.wait_ge(pz_ready, l + 1)
                for u in range(16):
                    h = u // 4
                    n = tiles[("pvs", l, h // 2)]
                    if u % 8 == 0:
                        b = take_bank(n)
                    w = raw_unit(("vc", l, u))
                    for b2 in range(2):
                        for mc in range(MC):
                            i = mm(b[0:TS, (h % 2) * HD:(h % 2 + 1) * HD], pz[:, h, mc, 2 * (u % 4) + b2, :], w[:, 2 * b2 + mc, :],
                                   start=(u % 4 + b2 + mc == 0), stop=(u % 4 == 3 and b2 + mc == 2))
                            if b2 + mc == 0 and u > 0:
                                frees(i, ("vc", l, u - 1))
                    if u % 8 == 7:
                        full(i, n)
                n = tiles[("ots", l)]
                b = take_bank(n)
                for hp in range(2):
                    wait_read(pe, tiles[("pvs", l, hp)])
                for c in range(KC):
                    i = nc.tensor.transpose(b[:, c * TS:(c + 1) * TS], o8[0:TS, c * P:(c + 1) * P], ident[0:TS, 0:TS])
                    if c == 0:
                        frees(i, ("vc", l, 15))
                full(i, n)
                for m in range(KC):
                    wait_read(pe, tiles[("pv", l, m)])
                wait_read(pe, tiles[("ots", l)])
                project("mo", l, xhi, xlo, T)
                norm_sum(("ssq", 3 * l + 2), 3 * l + 2)
                if l % 2 == 0:
                    project_pair("kf", l, 0, mhi, mlo, NM, mn_ready, KC * (2 * l + 1))
                    for half, (c0, c1) in enumerate(HALVES):
                        for s in range(c0 // 2, c1 // 2):
                            for key in ("fg", "fu"):
                                first = s == 0 and key == "fg"
                                project_pair(key, l, s, xhi, xlo, T, xn_ready if first else None, KC * (3 * l + 2))
                        nk = c1 - c0
                        for mp in range(KC // 2):
                            nn = [tiles[(f"fd{half}", l, 2 * mp + u)] for u in range(2)]
                            bb = [take_bank(n) for n in nn]
                            for kc in range(nk):
                                piece = mp * nk + kc
                                if piece % 4 == 0 or kc == 0:
                                    w_hi, w_lo = unit((f"fd{half}", l, piece // 4))
                                if mp == 0:
                                    pe.wait_ge(h_ready, c0 + kc + 1)
                                for u in range(2):
                                    i = product(bb[u][:, 0:T], w_hi[:, piece % 4, u * P:(u + 1) * P], w_lo[:, piece % 4, u * P:(u + 1) * P],
                                                hhi[:, kc, :], hlo[:, kc, :], start=(kc == 0), stop=(kc == nk - 1))
                                    if kc == nk - 1:
                                        full(i, nn[u])
                                    elif piece % 4 == 3 and u == 1:
                                        i.then_inc(unit_used, 1)
            l = DEPTH - 1
            pe.wait_ge(s_rw, 16)
            nn = [tiles[("lg", l, t)] for t in range(3)]
            bb = [take_bank(n) for n in nn]
            for kc in range(KC):
                pe.wait_ge(xn_ready, KC * (3 * l + 2) + kc + 1)
                for t, (t0, rows) in enumerate(TOK):
                    i = mm(bb[t][0:rows, 0:NE], xn[:, kc, t0:t0 + rows], rw[:, kc, :], start=(kc == 0), stop=(kc == KC - 1))
                    if kc == KC - 1:
                        full(i, nn[t])
            for t, (t0, rows) in enumerate(TOK):
                for hp in range(2):
                    n = tiles[("tk", l, t, hp)]
                    b = take_bank(n)
                    for c in range(4):
                        i = nc.tensor.transpose(b[0:rows, c * P:(c + 1) * P], xn[:, 4 * hp + c, t0:t0 + rows], ident)
                    full(i, n)
            n = tiles[("ps", l)]
            b = take_bank(n)
            pe.wait_ge(mask_ready, 1)
            for t in range(4):
                last = min(t, 2)
                for u in range(last + 1):
                    w = tri if u == t else ones[:, :]
                    i = mm(b[:, t * NE:(t + 1) * NE], w, msk[:, u, :], start=(u == 0), stop=(u == last))
            full(i, n)

            def gather(p, num):
                pe.wait_ge(gsel_ready, p + 1)
                for x4 in range(4):
                    n, more = num(f"X{x4}")
                    b = take_bank(n, more)
                    for c in range(2):
                        out = b[:, c * 2 * CAP:(c + 1) * 2 * CAP]
                        for t, (t0, rows) in enumerate(TOK):
                            f0 = (2 * x4 + c) * P
                            slots = gsel[0:rows, t, :, :].rearrange("p b s -> p (b s)")
                            mm(out, tokh[0:rows, t, f0:f0 + P], slots, start=(t == 0), stop=False)
                            i = mm(out, tokl[0:rows, t, f0:f0 + P], slots, start=False, stop=(t == 2))
                    full(i, n)

            def turn_scatter(v, num):
                n, more = num("S")
                b = take_bank(n, more)
                pe.wait_ge(wsel_ready, v + 1)
                for t, (t0, rows) in enumerate(TOK):
                    i = nc.tensor.transpose(b[:, t0:t0 + rows], wsel[0:rows, t, :], ident[0:rows, 0:rows])
                full(i, n)

            def scatter(num, before):
                wait_read(pe, *num("S"))
                for u in range(2):
                    wait_read(pe, *before(f"D{u}"))
                for c in range(KC):
                    n, more = num(f"C{c}")
                    b = take_bank(n, more)
                    full(mm(b[:, 0:T], eo[:, c * P:(c + 1) * P], scat, start=True, stop=True), n)

            def turn_hidden(num, i3):
                n, more = num(f"T{i3}")
                b = take_bank(n, more)
                for g in ((0, 1), (2,), (3,))[i3]:
                    wait_read(pe, *num(f"U{g}"))
                for c in range(4 * i3, min(4 * i3 + 4, FEC)):
                    i = nc.tensor.transpose(b[:, (c % 4) * P:(c % 4 + 1) * P], eh[:, c * P:(c + 1) * P], ident)
                full(i, n)

            def expert(p, side, num, before, first, last):
                v = 2 * p + side

                def eunit(j):
                    ewait(pe, eslot_free, j, v)
                    return wh[:, j % NBUF, :], wl[:, j % NBUF, :]

                def group(g):
                    if g == 0 and side == 0:
                        for x in GATHER:
                            wait_read(pe, *before(x))
                    for gi, name in enumerate("GU"):
                        n, more = num(f"{name}{g}")
                        b = take_bank(n, more)
                        for half in range(2):
                            w_hi, w_lo = (w.rearrange("p (k n) -> p k n", k=4) for w in eunit(4 * g + 2 * gi + half))
                            for k4 in range(4):
                                kc = 4 * half + k4
                                i = product(b[:, 0:GW], xgh[:, kc, side, :], xgl[:, kc, side, :], w_hi[:, k4, :], w_lo[:, k4, :],
                                            kc == 0, kc == KC - 1, False)
                            if half:
                                full(i, n)
                            else:
                                i.then_inc(eunit_used, 1)

                group(0)
                group(1)
                group(2)
                turn_hidden(num, 0)
                if not first:
                    turn_scatter(v - 1, num)
                group(3)
                turn_hidden(num, 1)
                if not first:
                    scatter(num, before)
                if side == 1 and not last:
                    gather(p + 1, num)
                turn_hidden(num, 2)
                for u in range(2):
                    n, more = num(f"D{u}")
                    b = take_bank(n, more)
                    for part in range(4):
                        w_hi, w_lo = eunit(16 + 4 * u + part)
                        f0, f1 = part * EUNIT, (part + 1) * EUNIT
                        for kc in range(f0 // 512, (f1 - 1) // 512 + 1):
                            if u == 0 and kc % 4 == 0 and f0 <= kc * 512:
                                wait_read(pe, *num(f"T{kc // 4}"))
                            lo, hi = max(kc * 512, f0), min((kc + 1) * 512, f1)
                            i = product(b[:, lo - kc * 512:hi - kc * 512], ehh[:, kc, :], ehl[:, kc, :], w_hi[:, lo - f0:hi - f0],
                                        w_lo[:, lo - f0:hi - f0], kc == 0, kc == FEC - 1, False)
                        if part == 3:
                            full(i, n)
                        else:
                            i.then_inc(eunit_used, 1)

            def pair(p, num, prior, first=False, last=False):
                a, b = block_of(num, "a"), block_of(num, "b")
                expert(p, 0, a, prior, first, False)
                expert(p, 1, b, a, False, last)

            def run_pass(ps):
                p0, p1 = ps.p0, ps.p0 + ps.np - 1
                gather(p0, ps.prologue)
                pair(p0, ps.first, ps.prologue, first=True)
                with pe.Fori(p0 + 1, p1) as p:
                    pair(p, ps.middle(p), ps.earlier(p))
                pair(p1, ps.last, ps.earlier(p1), last=True)
                turn_scatter(2 * p1 + 1, ps.after)
                scatter(ps.after, block_of(ps.last, "b"))

            for t in range(3):
                for hp in range(2):
                    wait_read(pe, tiles[("tk", l, t, hp)])
            run_pass(main)
            pe.wait_ge(route_ready, 1)
            count = pe.value_load(need[0:1, 0:1], min_val=0, max_val=T)
            with pe.If(count > CAP):
                run_pass(extra)
            with pe.Else():
                pe.nop()
            for m in range(KC):
                pe.wait_ge(fsq_ready, m + 1)
                i = mm(psum[0][:, 0:T], ones[:, :], sq[:, m, :], start=(m == 0), stop=(m == KC - 1))
            i.then_inc(fsum_ready, 1)

        @block.scalar
        def _(act):
            A = nc.scalar.activation
            act.dma_start(vec[:, :], vecs).then_inc(s_vec, 16)
            act.dma_start(con[:, :], consts).then_inc(s_con, 16)
            act.dma_start(rw[:, :, :], router_w).then_inc(s_rw, 16)
            chain = [0]

            def step(ins):
                chain[0] += 1
                ins.then_inc(act_chain, 1)
                return chain[0]

            def after(k):
                act.wait_ge(act_chain, k)

            def read(ins, n):
                ins.then_inc(bank_read[n % 8], 1)

            def high_part(k):
                name = names[k]
                u = units[name]
                act.wait_ge(slot_loaded[u % SLOTS], 16 * (u // SLOTS + 1))
                if k >= NBUF:
                    wait_used(act, k - NBUF)
                A(wh[:, k % NBUF, 0:UNIT], raw(u), ACT.Copy).then_inc(hi_ready, 1)

            S = Splitter(high_part)

            def squares(j, key=None, l=0):
                for m in range(KC):
                    if key is not None:
                        wait_read(act, tiles[(key, l, m)])
                    A(sq[:, m, :], x[:, m, :], ACT.Square).then_inc(sq_ready, 1)

            def root(n, width, scale, buf=0):
                wait_full(act, n)
                read(A(rms[:, buf, 0:width], bank(n)[:, 0:width], ACT.Sqrt, bias=eps[:, 0:1], scale=scale), n)

            made = [0]

            def high_parts(c0=0, c1=KC, between=None):
                for c in range(c0, c1):
                    made[0] += 1
                    act.wait_ge(fn_ready, made[0])
                    A(xhi[:, c, :], sq[:, c, :], ACT.Copy).then_inc(xh_ready, 1)
                    if c == 3 and between is not None:
                        S.upto(between)

            def gained(l):
                for c in range(KC):
                    A(mhi[:, c, :], mem[:, c, :], ACT.Copy, scale=col("mem_norm", l, c)).then_inc(mh_ready, 1)

            def values(l, s):
                for mc in range(MC):
                    n = tiles[("mv", l, s, mc)]
                    wait_full(act, n)
                    read(A(vN[:, mc, s * PIECE:(s + 1) * PIECE], bank(n)[:, 0:PIECE], ACT.Copy), n)

            def keys(kind, l, pair):
                for u in range(2):
                    n = tiles[(kind, l, u)]
                    wait_full(act, n)
                    read(A(kT[:, 2 * pair + u, :], bank(n)[:, 0:NM], ACT.Copy), n)

            act.wait_ge(s_set, 2)
            for m in range(KC):
                act.wait_ge(s_x[m // 4], 16)
                A(sq[:, m, :], x[:, m, :], ACT.Square).then_inc(sq_ready, 1)
            for l in range(DEPTH):
                S.upto(start("in", l) + 1)
                root(tiles[("ssq", 3 * l)], T, 1.0 / D)
                high_parts(between=start("in", l) + 3 if l == 0 else None)
                S.upto(start("in", l) + 4)
                if l == 0:
                    act.wait_ge(decay_in, 1)
                    A(coef[:, 1, :], coef[:, 0, :], ACT.Exp).then_inc(decay_exp, 1)
                act.wait_ge(padded, 2 * (l + 1))
                act.wait_ge(hist_loaded, 32 * (l + 1))
                for m in range(12):
                    n = tiles[("in", l, m)]
                    wait_full(act, n)
                    c = m % RC
                    if m < RC:
                        A(cp[:, c, CW - 1:], bank(n)[:, 0:TP], ACT.Copy)
                        read(A(sconv[:, c, :, CW - 1], bank(n)[:, TP:T], ACT.Copy), n)
                    elif m < 2 * RC:
                        read(A(gel[:, c, :], bank(n)[:, 0:T], ACT.Gelu_apprx_tanh), n)
                    else:
                        A(pp[:, c, HIST:], bank(n)[:, 0:TP], ACT.Copy)
                        read(A(spool[:, c, :, 15], bank(n)[:, TP:T], ACT.Copy), n)
                    if m % 2:
                        S.upto(behind("in", l, m, 5, start("mk", l) + 2))
                    if l == 0 and m in (1, 3):
                        act.wait_ge(s_mem, 16)
                        for c in range(2 * m - 2, 2 * m + 2):
                            A(msq[:, c, :], mem[:, c, :], ACT.Square).then_inc(msq_ready, 1)
                    if l == 0 and m == 5:
                        root(tiles[("msq",)], NM, 1.0 / D, 1)
                    if m == 9:
                        if l == 0:
                            act.wait_ge(mem_normed, KC)
                        gained(l)
                S.upto(start("mk", l) + 4)
                if l > 0:
                    act.wait_ge(kv_written, 32 * l)
                for m in range(2 * KEYS_FIRST[l]):
                    n = tiles[("mk", l, m)]
                    wait_full(act, n)
                    read(A(kT[:, m, :], bank(n)[:, 0:NM], ACT.Copy), n)
                    if m % 2:
                        S.upto(behind("mk", l, m, 5, start("mv", l) + 2))
                for key, dst, name in (("ga", r_g, "gate_a_b"), ("gx", i_g, "gate_x_b")):
                    for c in range(RC):
                        n = tiles[(key, l, c)]
                        wait_full(act, n)
                        read(A(dst[:, c, :], bank(n)[:, 0:T], ACT.Sigmoid, bias=col(name, l, c)), n)
                S.upto(start("mv", l) + 3)
                act.wait_ge(coef_ready, 1)
                act.wait_ge(z_ready, l + 1)
                for c in range(RC):
                    wait_read(act, tiles[("ga", l, c)])
                    step(A(ml[:, c, :], r_g[:, c, :], ACT.Tanh, scale=coef[:, 5, l * RC + c:l * RC + c + 1]))
                S.upto(start("mv", l) + 4)
                for c in range(RC):
                    k = step(A(r_g[:, c, :], r_g[:, c, :], ACT.Exp, scale=coef[:, 0, l * RC + c:l * RC + c + 1]))
                S.upto(start("mv", l) + 5)
                values(l, 0)
                after(k)
                A(ml, ml, ACT.Sqrt).then_inc(gates_ready, 1)
                S.upto(start("mv", l) + 6)
                values(l, 1)
                S.upto(start("out", l))
                for c in range(RC):
                    wait_read(act, tiles[("pw", l, c)])
                    A(sq[:, c, :], yp[:, c, :], ACT.Square).then_inc(psq_ready, 1)
                values(l, 2)
                S.upto(start("out", l) + 1)
                root(tiles[("psq", l)], T, 2.0 / D, 1)
                act.wait_ge(yr_ready, l + 1)
                for c in range(RC):
                    A(sq[:, RC + c, :], yr[:, c, :], ACT.Square).then_inc(rsq_ready, 1)
                high_parts(0, RC)
                S.upto(start("out", l) + 2)
                root(tiles[("rsq", l)], T, 2.0 / D)
                high_parts(RC, KC)
                S.upto(start("out", l) + 3)
                values(l, 3)
                S.upto(start("out", l) + 4)
                for m in range(KC):
                    wait_read(act, tiles[("out", l, m)])
                    A(sq[:, m, :], x[:, m, :], ACT.Square).then_inc(sq_ready, 1)
                    if m % 2:
                        S.upto(behind("out", l, m, 5, start("kn", l) + 3))
                root(tiles[("ssq", 3 * l + 1)], T, 1.0 / D)
                high_parts(between=start("kn", l) + 4)
                keys("kn", l, LATE[l][0][2])
                S.upto(start("mq", l) + 4)
                for m in range(KC):
                    n = tiles[("mq", l, m)]
                    wait_full(act, n)
                    read(A(q[:, m, :], bank(n)[:, 0:T], ACT.Copy), n)
                    if m % 2:
                        S.upto(behind("mq", l, m, 5, start("mo", l)))
                for t in range(3):
                    rows = TOK[t][1]
                    for hp in range(2):
                        n = tiles[("sc", l, t, hp)]
                        act.wait_ge(max_ready, 6 * l + 2 * t + hp + 1)
                        for hh in range(2):
                            h = 2 * hp + hh
                            j = 4 * t + h
                            i = A(pr[0:rows, t, h, :], bank(n)[0:rows, hh * NM:(hh + 1) * NM], ACT.Exp,
                                  bias=nmx[0:rows, j:j + 1], scale=HD ** -0.5, accum_out=sm[0:rows, j:j + 1])
                            if hh:
                                read(i, n)
                            else:
                                i.then_inc(exp_done, 1)
                for h in range(NH):
                    n = tiles[("pt", l, h)]
                    wait_full(act, n)
                    read(A(pT[:, h, :, :].rearrange("p c t -> p (c t)"), bank(n)[:, :], ACT.Copy), n)
                for m in range(KC):
                    n = tiles[("pv", l, m)]
                    wait_full(act, n)
                    A(xhi[:, m, 0:TP], bank(n)[:, 0:TP], ACT.Copy).then_inc(oh_ready, 1)
                S.upto(start("mo", l) + 4)
                nxt = start("kf", l) if l % 2 == 0 else NSPLIT
                if l % 2 == 0:
                    gained(l + 1)
                for m in range(KC):
                    wait_read(act, tiles[("mo", l, m)])
                    A(sq[:, m, :], x[:, m, :], ACT.Square).then_inc(sq_ready, 1)
                    if m % 2:
                        S.upto(behind("mo", l, m, 5, nxt + 3))
                root(tiles[("ssq", 3 * l + 2)], T, 1.0 / D)
                if l % 2 == 0:
                    high_parts(between=nxt + 4)
                    act.wait_ge(kv_written, 32 * (l + 1))
                    keys("kf", l, LATE[l][1][2])
                    for half, (c0, c1) in enumerate(HALVES):
                        nxt = start(f"fd{half}", l)
                        S.upto(split[("fg", l, c0)] + 4)
                        for m in range(c0, c1):
                            n = tiles[("fg", l, m)]
                            wait_full(act, n)
                            if m >= 2:
                                act.wait_ge(h_ready, m - 1)
                            read(A(sg[:, m % 2, :], bank(n)[:, 0:T], ACT.Silu), n)
                            if m % 2:
                                S.upto(behind("fg", l, m, 7, nxt + 3))
                        S.upto(nxt + 3)
                        after_down = start("in", l + 1) if half else split[("fg", l, c1)]
                        for m in range(KC):
                            if m % 2 == 0:
                                S.upto(min(down_end(half, l, m) + 3, after_down + 2))
                            if half:
                                wait_read(act, tiles[(f"fd{half}", l, m)])
                                A(sq[:, m, :], x[:, m, :], ACT.Square).then_inc(sq_ready, 1)
                        S.upto(after_down + 3)
            l = DEPTH - 1

            def first_highs(v0):
                for j in range(NBUF):
                    ewait(act, eslot_loaded, j, v0, 16)
                    if v0 == 0:
                        wait_used(act, max(k for k in range(NSPLIT) if k % NBUF == j))
                    else:
                        wait_full(act, *main.last("bD1"))
                    A(wh[:, j, :], eraw(j), ACT.Copy).then_inc(ehi_ready, 1)

            first_highs(0)
            for t, (t0, rows) in enumerate(TOK):
                for hp in range(2):
                    n = tiles[("tk", l, t, hp)]
                    wait_full(act, n)
                    A(tokh[0:rows, t, hp * 512:(hp + 1) * 512], bank(n)[0:rows, :], ACT.Copy).then_inc(oh_ready, 1)
            act.wait_ge(lmax_ready, 1)
            A(ed, ed, ACT.Exp).then_inc(lexp_ready, 1)

            def ehigh(v, num, j):
                vv, jj = (v, j) if j < EUNITS else (v + 1, j - EUNITS)
                ewait(act, eslot_loaded, jj, vv, 16)
                wait_eused(act, v, num, j - NBUF)
                A(wh[:, jj % NBUF, :], eraw(jj % ESLOTS), ACT.Copy).then_inc(ehi_ready, 1)

            def gathered(num):
                for x4 in range(4):
                    n, more = num(f"X{x4}")
                    wait_full(act, n, more)
                    A(xgh[:, 2 * x4:2 * x4 + 2, :, :].rearrange("p c b s -> p (c b s)"), bank(n)[:, :], ACT.Copy).then_inc(xgh_ready, 1)

            def turned(num, i3):
                n, more = num(f"T{i3}")
                wait_full(act, n, more)
                k = min(4, FEC - 4 * i3)
                A(ehh[:, 4 * i3:4 * i3 + k, :].rearrange("p c s -> p (c s)"), bank(n)[:, 0:k * P], ACT.Copy).then_inc(ehh_ready, 1)

            def scattered(num):
                n, more = num("S")
                wait_full(act, n, more)
                read(A(scat, bank(n)[:, 0:T], ACT.Copy), n)

            def expert(p, side, num, first, last):
                v = 2 * p + side
                at = [NBUF]

                def upto(k):
                    while at[0] < min(k, EUNITS if last else EUNITS + NBUF):
                        ehigh(v, num, at[0])
                        at[0] += 1

                def silu(g):
                    n, more = num(f"G{g}")
                    wait_full(act, n, more)
                    if g >= 2:
                        wait_read(act, *num(f"U{g - 2}"))
                    read(A(esg[:, g % 2, :], bank(n)[:, 0:GW], ACT.Silu), n)

                upto(4)
                silu(0)
                upto(8)
                silu(1)
                upto(12)
                silu(2)
                upto(15)
                turned(num, 0)
                if not first:
                    scattered(num)
                upto(16)
                silu(3)
                upto(19)
                turned(num, 1)
                if side == 1 and not last:
                    gathered(num)
                turned(num, 2)
                upto(23)
                for u in range(2):
                    n, more = num(f"D{u}")
                    wait_full(act, n, more)
                    read(A(eo[:, u * 512:(u + 1) * 512], bank(n)[:, :], ACT.Copy), n)
                    upto(27)

            def pair(p, num, first=False, last=False):
                expert(p, 0, block_of(num, "a"), first, False)
                expert(p, 1, block_of(num, "b"), False, last)

            def run_pass(ps):
                p0, p1 = ps.p0, ps.p0 + ps.np - 1
                if p0 > 0:
                    first_highs(2 * p0)
                gathered(ps.prologue)
                pair(p0, ps.first, first=True)
                with act.Fori(p0 + 1, p1) as p:
                    pair(p, ps.middle(p))
                pair(p1, ps.last, last=True)
                scattered(ps.after)

            run_pass(main)
            act.wait_ge(route_ready, 1)
            count = act.value_load(need[0:1, 0:1], min_val=0, max_val=T)
            with act.If(count > CAP):
                run_pass(extra)
            with act.Else():
                act.nop()
            act.wait_ge(x_final, 1)
            for m in range(KC):
                A(sq[:, m, :], x[:, m, :], ACT.Square).then_inc(fsq_ready, 1)
            act.wait_ge(fsum_ready, 1)
            A(rms[:, 0, :], psum[0][:, 0:T], ACT.Sqrt, bias=eps[:, 0:1], scale=1.0 / D).then_inc(frms_ready, 1)

        @block.vector
        def _(dve):
            V = nc.vector
            chain = [0]

            def step(ins):
                chain[0] += 1
                ins.then_inc(dve_chain, 1)
                return chain[0]

            def after(k):
                dve.wait_ge(dve_chain, k)

            def link(ins):
                after(step(ins))

            def read(ins, n):
                ins.then_inc(bank_read[n % 8], 1)

            def signal(ready):
                after(chain[0])
                dve.sem_inc(ready, 1)

            V.memset(ones[:, :], 1.0).then_inc(s_set, 1)
            V.memset(eps[:, :], EPS).then_inc(s_set, 1)

            dve.wait_ge(s_vec, 16)
            for l in range(DEPTH):
                k = l * LVEC + VEC["rglru_lambda"]
                link(V.tensor_scalar(coef[:, 5, l * RC:(l + 1) * RC], vec[:, k:k + RC], -1.0, 0.0, ALU.mult, ALU.max))
                link(V.tensor_scalar(coef[:, 0, l * RC:(l + 1) * RC], vec[:, k:k + RC], -1.0, None, ALU.mult))
                link(V.tensor_tensor(coef[:, 0, l * RC:(l + 1) * RC], coef[:, 0, l * RC:(l + 1) * RC], vec[:, k:k + RC], ALU.min))
            signal(decay_in)

            def invert(n, buf, width=T):
                wait_read(dve, n)
                link(V.reciprocal(rstd[:, buf, 0:width], rms[:, buf, 0:width]))

            def low_part(k):
                u = units[names[k]]
                dve.wait_ge(hi_ready, k + 1)
                V.tensor_tensor(wl[:, k % NBUF, 0:UNIT], raw(u), wh[:, k % NBUF, 0:UNIT].bitcast(F32), ALU.subtract)\
                    .then_inc(slot_free[u % SLOTS], 1)

            S = Splitter(low_part)

            made = [0]

            def scaled_parts(src, l, name, buf, c0, c1, ready, between=None, o=0):
                for c in range(c0, c1 + 1):
                    if c < c1:
                        V.scalar_tensor_tensor(out=sq[:, c, :], in0=src[:, c - o, :], scalar=col(name, l, c - o),
                                               in1=rstd[:, buf, :], op0=ALU.mult, op1=ALU.mult).then_inc(fn_ready, 1)
                    if c > c0:
                        made[0] += 1
                        dve.wait_ge(xh_ready, made[0])
                        V.tensor_tensor(xlo[:, c - 1, :], sq[:, c - 1, :], xhi[:, c - 1, :].bitcast(F32), ALU.subtract).then_inc(ready, 1)
                    if between is not None and c == c0 + 4:
                        S.upto(between)

            def normed(j, l, name, between):
                invert(tiles[("ssq", j)], 0)
                scaled_parts(x, l, name, 0, 0, KC, xn_ready, between)

            def gained_low(l, k):
                for m in range(KC):
                    dve.wait_ge(mh_ready, KC * k + m + 1)
                    V.scalar_tensor_tensor(out=mlo[:, m, :], in0=mem[:, m, :], scalar=col("mem_norm", l, m),
                                           in1=mhi[:, m, :].bitcast(F32), op0=ALU.mult, op1=ALU.subtract).then_inc(mn_ready, 1)

            def residual(key, l, ahead, last):
                for m in range(KC):
                    if callable(ahead) and m % 2 == 0:
                        S.upto(ahead(m))
                    n = tiles[(key, l, m)]
                    wait_full(dve, n)
                    read(V.tensor_tensor(x[:, m, :], bank(n)[:, 0:T], x[:, m, :], ALU.add), n)
                    if m % 2 and not callable(ahead):
                        S.upto(behind(key, l, m, ahead, last))

            for l in range(DEPTH):
                S.upto(start("in", l) + 1)
                normed(3 * l, l, "norm_mix", start("in", l) + 3 if l == 0 else None)
                S.upto(start("in", l) + 4)
                if l == 0:
                    dve.wait_ge(decay_exp, 1)
                    e, s, s2, acc, out = (coef[:, i, :] for i in (1, 2, 3, 4, 5))
                    link(V.tensor_scalar(acc, e, 2.0, None, ALU.add))
                    link(V.reciprocal(acc, acc))
                    link(V.tensor_tensor(s, e, acc, ALU.mult))
                    link(V.tensor_tensor(s2, s, s, ALU.mult))
                    link(V.tensor_scalar(acc, s2, 1.0 / 19, None, ALU.mult))
                    for d in (17, 15, 13, 11, 9, 7, 5, 3):
                        link(V.scalar_tensor_tensor(out=acc, in0=acc, scalar=1.0 / d, in1=s2, op0=ALU.add, op1=ALU.mult))
                    link(V.scalar_tensor_tensor(out=acc, in0=acc, scalar=1.0, in1=s, op0=ALU.add, op1=ALU.mult))
                    link(V.scalar_tensor_tensor(out=out, in0=acc, scalar=2.0, in1=out, op0=ALU.mult, op1=ALU.add))
                    link(V.tensor_scalar(out, out, 4.0, None, ALU.mult))
                    link(V.tensor_scalar(coef[:, 0, :], out, -2.0, None, ALU.mult))
                    signal(coef_ready)
                last = {}

                def tap(k):
                    for c in range(RC):
                        j = l * LVEC + VEC["conv_w"] + RC * k + c
                        w = vec[:, j:j + 1]
                        if k == 0:
                            wait_read(dve, tiles[("in", l, c)])
                            step(V.tensor_scalar(cv[:, c, 0:TP], cp[:, c, 0:TP], w, col("conv_b", l, c), ALU.mult, ALU.add))
                            last[c] = step(V.tensor_scalar(cv[:, c, TP:T], sconv[:, c, :, 0], w, col("conv_b", l, c), ALU.mult, ALU.add))
                        else:
                            after(last[c])
                            step(V.scalar_tensor_tensor(out=cv[:, c, 0:TP], in0=cp[:, c, k:k + TP], scalar=w, in1=cv[:, c, 0:TP],
                                                        op0=ALU.mult, op1=ALU.add))
                            last[c] = step(V.scalar_tensor_tensor(out=cv[:, c, TP:T], in0=sconv[:, c, :, k], scalar=w,
                                                                  in1=cv[:, c, TP:T], op0=ALU.mult, op1=ALU.add))

                for s in range(6):
                    wait_full(dve, tiles[("in", l, 2 * s + 1)])
                    S.upto(behind("in", l, 2 * s + 1, 5, start("mk", l) + 2))
                    if s == 3 and l == 0:
                        invert(tiles[("msq",)], 1, NM)
                        for m in range(KC):
                            V.tensor_tensor(mem[:, m, :], mem[:, m, :], rstd[:, 1, 0:NM], ALU.mult).then_inc(mem_normed, 1)
                    elif s in (2, 3):
                        tap(s - 2)
                    elif s == 4:
                        gained_low(l, 2 * l)
                    elif s == 5:
                        tap(2 if l else 1)
                S.upto(start("mk", l) + 4)
                for k in range(3 if l else 2, CW):
                    tap(k)
                    S.upto(min(start("mk", l) + 4 + k, start("mv", l) + 2))
                signal(cv_ready)
                for c in range(RC):
                    wait_read(dve, tiles[("in", l, 2 * RC + c)])
                link(V.tensor_tensor(lad[0][:, :, 0:270], pp[:, :, 0:270], pp[:, :, 1:271], ALU.add))
                link(V.tensor_tensor(lad[1][:, 1:4, 0:268], lad[0][:, 1:4, 0:268], lad[0][:, 1:4, 2:270], ALU.add))
                S.upto(start("mv", l) + 2)
                link(V.tensor_tensor(lad[0][:, 2:4, 0:264], lad[1][:, 2:4, 0:264], lad[1][:, 2:4, 4:268], ALU.add))
                link(V.tensor_tensor(lad[1][:, 3, 0:256], lad[0][:, 3, 0:256], lad[0][:, 3, 8:264], ALU.add))
                S.upto(start("mv", l) + 1)
                if l == 0:
                    dve.wait_ge(s_con, 16)
                for g, w in enumerate(WINDOWS):
                    s = lad[g % 2][:, g, 16 - w:16 - w + TP]
                    step(V.tensor_reduce(ss[:, g, :], spool[:, g, :, 16 - w:16], AX_X, ALU.add))
                    k = step(V.tensor_tensor(s[:, 0:16], s[:, 0:16], corr[:, g, :], ALU.mult))
                after(k)
                for g, w in enumerate(WINDOWS):
                    s = lad[g % 2][:, g, 16 - w:16 - w + TP]
                    step(V.scalar_tensor_tensor(out=z[:, g, 0:TP], in0=s, scalar=1.0 / w, in1=pp[:, g, HIST:], op0=ALU.mult, op1=ALU.subtract))
                    step(V.scalar_tensor_tensor(out=z[:, g, TP:T], in0=ss[:, g, :], scalar=1.0 / w, in1=spool[:, g, :, 15],
                                                op0=ALU.mult, op1=ALU.subtract))
                signal(z_ready)
                S.upto(start("mv", l) + 5)
                for c in range(RC):
                    wait_read(dve, tiles[("gx", l, c)])
                step(V.tensor_tensor(i_g, i_g, cv, ALU.mult))
                dve.wait_ge(gates_ready, l + 1)
                k = step(V.scalar_tensor_tensor(out=ml, in0=r_g, scalar=1.0, in1=ml, op0=ALU.add, op1=ALU.mult))
                S.upto(start("mv", l) + 6)
                after(k)
                k = step(V.memset(ml[:, :, 0:1], 1.0))
                for c in range(RC):
                    n = tiles[("pw", l, c)]
                    wait_full(dve, n)
                    read(V.tensor_scalar(yp[:, c, :], bank(n)[:, 0:T], col("pool_scale", l, c), None, ALU.mult), n)
                after(k)
                link(V.tensor_tensor(i_g, i_g, ml, ALU.mult))
                S.upto(start("mv", l) + 7)
                o = VEC_H0 + l * RC * TS
                h0 = vec[:, o:o + RC * TS].rearrange("p (c b) -> p c b", c=RC)
                k = step(V.tensor_tensor(cv[:, :, TP:T], r_g[:, :, TP:T], h0, ALU.mult))
                for c in range(RC):
                    step(V.tensor_tensor_scan(cv[:, c, 0:TP], r_g[:, c, 0:TP], i_g[:, c, 0:TP], 0.0, ALU.mult, ALU.add))
                S.upto(start("mv", l) + 8)
                after(k)
                step(V.tensor_tensor(cv[:, :, TP:T], cv[:, :, TP:T], i_g[:, :, TP:T], ALU.add))
                signal(h_last)
                for c in range(RC):
                    wait_read(dve, tiles[("in", l, RC + c)])
                V.tensor_tensor(yr, cv, gel, ALU.mult).then_inc(yr_ready, 1)
                S.upto(start("out", l) + 1)
                invert(tiles[("psq", l)], 1)
                scaled_parts(yp, l, "out_norm_pool", 1, 0, RC, mixed_ready)
                S.upto(start("out", l) + 2)
                invert(tiles[("rsq", l)], 0)
                scaled_parts(yr, l, "out_norm_rnn", 0, RC, KC, mixed_ready, o=RC)
                S.upto(start("out", l) + 4)
                dve.wait_ge(small_written, 96 * (l + 1))
                step(V.memset(qz, 0.0))
                step(V.memset(pz, 0.0))
                residual("out", l, 5, start("kn", l) + 3)
                normed(3 * l + 1, l, "norm_mem", start("kn", l) + 4)
                S.upto(start("mq", l) + 4)
                after(chain[0])
                for c in range(KC):
                    wait_read(dve, tiles[("mq", l, c)])
                    step(V.tensor_copy(qz[:, c, :, :].rearrange("p b s -> p (b s)")[:, 0:64:TS + 1], q[:, c, TP:T]))
                    if c % 2:
                        S.upto(behind("mq", l, c, 5, start("mo", l)))
                signal(qz_ready)
                for t in range(3):
                    rows = TOK[t][1]
                    for hp in range(2):
                        n = tiles[("sc", l, t, hp)]
                        j = 4 * t + 2 * hp
                        wait_full(dve, n)
                        link(V.tensor_reduce(mx[0:rows, j:j + 2], bank(n)[0:rows, :].rearrange("p (h m) -> p h m", h=2), AX_X, ALU.max))
                        V.tensor_scalar(nmx[0:rows, j:j + 2], mx[0:rows, j:j + 2], -(HD ** -0.5), None, ALU.mult).then_inc(max_ready, 1)
                    for hp in range(2):
                        j = 4 * t + 2 * hp
                        dve.wait_ge(exp_done, 6 * l + 2 * t + hp + 1)
                        wait_read(dve, tiles[("sc", l, t, hp)])
                        link(V.reciprocal(rs[0:rows, j:j + 2], sm[0:rows, j:j + 2]))
                        for hh in range(2):
                            h = 2 * hp + hh
                            step(V.tensor_scalar(pr[0:rows, t, h, :], pr[0:rows, t, h, :], rs[0:rows, j + hh:j + hh + 1], None, ALU.mult))
                        signal(p_ready)
                for m in range(KC):
                    n = tiles[("pv", l, m)]
                    dve.wait_ge(oh_ready, KC * l + m + 1)
                    read(V.tensor_tensor(xlo[:, m, 0:TP], bank(n)[:, 0:TP], xhi[:, m, 0:TP].bitcast(F32), ALU.subtract), n)
                n = tiles[("pts", l)]
                wait_full(dve, n)
                for h in range(NH):
                    for mc in range(MC):
                        j = (h * MC + mc) * TS
                        i = V.tensor_copy(pz[:, h, mc, :, :].rearrange("p b s -> p (b s)")[:, 0:64:TS + 1], bank(n)[:, j:j + TS])
                        if h * MC + mc == NH * MC - 1:
                            read(i, n)
                        else:
                            step(i)
                wait_read(dve, n)
                signal(pz_ready)
                for hp in range(2):
                    n = tiles[("pvs", l, hp)]
                    wait_full(dve, n)
                    read(V.tensor_copy(o8[0:TS, hp * 512:(hp + 1) * 512], bank(n)[0:TS, :]), n)
                    if hp == 0:
                        S.upto(start("mo", l) + 3)
                n = tiles[("ots", l)]
                wait_full(dve, n)
                attended = bank(n)[:, 0:KC * TS].rearrange("p (c b) -> p c b", c=KC)
                link(V.tensor_copy(xhi[:, :, TP:T], attended))
                read(V.tensor_tensor(xlo[:, :, TP:T], attended, xhi[:, :, TP:T].bitcast(F32), ALU.subtract), n)
                nxt = start("kf", l) if l % 2 == 0 else NSPLIT
                S.upto(start("mo", l) + 4)
                if l % 2 == 0:
                    gained_low(l + 1, 2 * l + 1)
                residual("mo", l, 5, nxt + 3)
                if l % 2 == 0:
                    normed(3 * l + 2, l, "norm_ffn", nxt + 4)
                    for half, (c0, c1) in enumerate(HALVES):
                        nxt = start(f"fd{half}", l)
                        S.upto(split[("fg", l, c0)] + 6)
                        for s in range(c0 // 2, c1 // 2):
                            for m in (2 * s, 2 * s + 1):
                                n = tiles[("fu", l, m)]
                                wait_read(dve, tiles[("fg", l, m)])
                                wait_full(dve, n)
                                read(V.tensor_tensor(hb[:, m % 2, :], bank(n)[:, 0:T], sg[:, m % 2, :], ALU.mult), n)
                            for m in (2 * s, 2 * s + 1):
                                wait_read(dve, tiles[("fu", l, m)])
                                k = step(V.tensor_copy(hhi[:, m - c0, :], hb[:, m % 2, :]))
                            after(k)
                            for m in (2 * s, 2 * s + 1):
                                V.tensor_tensor(hlo[:, m - c0, :], hb[:, m % 2, :], hhi[:, m - c0, :].bitcast(F32), ALU.subtract)\
                                    .then_inc(h_ready, 1)
                            S.upto(behind("fu", l, 2 * s + 1, 7, nxt + 3))
                        after_down = start("in", l + 1) if half else split[("fg", l, c1)]
                        residual(f"fd{half}", l, lambda m: min(down_end(half, l, m) + 3, after_down + 2), None)
                        S.upto(after_down + 3)
            def elow(v, j):
                vv, jj = (v, j) if j < EUNITS else (v + 1, j - EUNITS)
                dve.wait_ge(ehi_ready, EUNITS * vv + jj + 1)
                V.tensor_tensor(wl[:, jj % NBUF, :], eraw(jj % ESLOTS), wh[:, jj % NBUF, :].bitcast(F32), ALU.subtract)\
                    .then_inc(eslot_free[jj % ESLOTS], 1)

            l = DEPTH - 1
            invert(tiles[("ssq", 3 * l + 2)], 0)
            for m in range(KC):
                V.scalar_tensor_tensor(out=xn[:, m, :], in0=x[:, m, :], scalar=col("norm_ffn", l, m), in1=rstd[:, 0, :],
                                       op0=ALU.mult, op1=ALU.mult).then_inc(xn_ready, 1)
            dve.wait_ge(kv_written, 32 * DEPTH)
            link(V.memset(rt[:, 0:336], 0.0))
            elow(0, 0)
            for t, (t0, rows) in enumerate(TOK):
                n = tiles[("lg", l, t)]
                wait_full(dve, n)
                read(V.tensor_copy(lg[0:rows, t, :], bank(n)[0:rows, 0:NE]), n)
            for t in range(3):
                wait_read(dve, tiles[("lg", l, t)])
            for t in range(3):
                step(V.max(out=m8[:, t, :], in_=lg[:, t, :]))
            after(chain[0])
            V.tensor_tensor(ed, m8[:, :, 1], m8[:, :, 0], ALU.subtract).then_inc(lmax_ready, 1)
            for t in range(3):
                step(V.max_index(i8[:, t, :], m8[:, t, :], lg[:, t, :]))
            after(chain[0])
            link(V.tensor_copy(fi, i8[:, :, :]))
            link(V.scalar_tensor_tensor(out=fi, in0=fi, scalar=1.0, in1=per_token(valid), op0=ALU.add, op1=ALU.mult))
            experts1 = iota[:, 1:NE + 1].unsqueeze(1).broadcast_to([P, 3, NE])
            step(V.tensor_tensor(oh, experts1, per_token(fi[:, :, 0]), ALU.is_equal))
            link(V.tensor_tensor(second, experts1, per_token(fi[:, :, 1]), ALU.is_equal))
            link(V.tensor_tensor(msk, oh, second, ALU.add))
            signal(mask_ready)
            for t, (t0, rows) in enumerate(TOK):
                for hp in range(2):
                    n = tiles[("tk", l, t, hp)]
                    cols = slice(hp * 512, (hp + 1) * 512)
                    dve.wait_ge(oh_ready, KC * DEPTH + 2 * t + hp + 1)
                    read(V.tensor_tensor(tokl[0:rows, t, cols], bank(n)[0:rows, :], tokh[0:rows, t, cols].bitcast(F32), ALU.subtract), n)
            n = tiles[("ps", l)]
            wait_full(dve, n)
            read(V.tensor_copy(pos, bank(n)[:, 0:32].rearrange("p (t e) -> p t e", t=4)), n)
            wait_read(dve, n)
            step(V.tensor_reduce(cmax, pos[:, 3, :], AX_X, ALU.max))
            link(V.scalar_tensor_tensor(out=psm[:, :, 0, :], in0=pos[:, 0:3, :], scalar=1.0, in1=msk, op0=ALU.add, op1=ALU.mult))
            step(V.tensor_copy(need[:, :], cmax))
            for b in range(MAXB - 1, -1, -1):
                link(V.tensor_scalar(psm[:, :, b, :], psm[:, :, 0, :], -1.0 - CAP * b, None, ALU.add))
            signal(route_ready)

            def gather_matrix(p):
                for t in range(3):
                    for side in range(2):
                        i = V.tensor_scalar(gsel[:, t, side, :], iota, pcol[:, t, bass.ds(2 * p + side, 1)], None, ALU.is_equal)
                i.then_inc(gsel_ready, 1)

            def scatter_matrix(v):
                for t in range(3):
                    i = V.tensor_scalar(wsel[:, t, :], iota, pcol[:, t, bass.ds(v, 1)], wcol[:, t, bass.ds(v, 1)],
                                        ALU.is_equal, ALU.mult)
                i.then_inc(wsel_ready, 1)

            def combine(num):
                for c in range(KC):
                    n, more = num(f"C{c}")
                    wait_full(dve, n, more)
                    read(V.tensor_tensor(x[:, c, :], bank(n)[:, 0:T], x[:, c, :], ALU.add), n)

            def gathered_low(p, num):
                for x4 in range(4):
                    n, more = num(f"X{x4}")
                    dve.wait_ge(xgh_ready, 4 * p + x4 + 1)
                    read(V.tensor_tensor(xgl[:, 2 * x4:2 * x4 + 2, :, :].rearrange("p c b s -> p (c b s)"), bank(n)[:, :],
                                         xgh[:, 2 * x4:2 * x4 + 2, :, :].rearrange("p c b s -> p (c b s)").bitcast(F32), ALU.subtract), n)

            def turned_low(v, num, i3):
                n, more = num(f"T{i3}")
                dve.wait_ge(ehh_ready, 3 * v + i3 + 1)
                k = min(4, FEC - 4 * i3)
                read(V.tensor_tensor(ehl[:, 4 * i3:4 * i3 + k, :].rearrange("p c s -> p (c s)"), bank(n)[:, 0:k * P],
                                     ehh[:, 4 * i3:4 * i3 + k, :].rearrange("p c s -> p (c s)").bitcast(F32), ALU.subtract), n)

            def expert(p, side, num, before, first, last):
                v = 2 * p + side
                at = [NBUF]

                def upto(k):
                    while at[0] < min(k, EUNITS if last and side == 1 else EUNITS + NBUF):
                        elow(v, at[0])
                        at[0] += 1

                def hidden(g):
                    n, more = num(f"U{g}")
                    wait_read(dve, *num(f"G{g}"))
                    wait_full(dve, n, more)
                    if g == 0 and not first:
                        wait_full(dve, *before("T2"))
                    read(V.tensor_tensor(eh[:, g * GW:(g + 1) * GW], bank(n)[:, 0:GW], esg[:, g % 2, :], ALU.mult), n)

                if side == 0 and not last:
                    wait_full(dve, *before("X3"))
                    gather_matrix(p + 1)
                upto(6)
                hidden(0)
                upto(10)
                hidden(1)
                upto(14)
                hidden(2)
                upto(15)
                turned_low(v, num, 0)
                upto(18)
                hidden(3)
                turned_low(v, num, 1)
                upto(19)
                if not first:
                    combine(num)
                if side == 1 and not last:
                    gathered_low(p + 1, num)
                turned_low(v, num, 2)
                scatter_matrix(v)
                upto(27)

            def pair(p, num, prior, first=False, last=False):
                a, b = block_of(num, "a"), block_of(num, "b")
                expert(p, 0, a, prior, first, last)
                expert(p, 1, b, a, False, last)

            def run_pass(ps):
                p0, p1 = ps.p0, ps.p0 + ps.np - 1
                if p0 > 0:
                    gather_matrix(p0)
                    for j in range(NBUF):
                        elow(2 * p0, j)
                gathered_low(p0, ps.prologue)
                pair(p0, ps.first, ps.prologue, first=True)
                with dve.Fori(p0 + 1, p1) as p:
                    pair(p, ps.middle(p), ps.earlier(p))
                pair(p1, ps.last, ps.earlier(p1), last=True)
                combine(ps.after)

            gather_matrix(0)
            for j in range(1, NBUF):
                elow(0, j)
            dve.wait_ge(lexp_ready, 1)
            link(V.tensor_scalar(g1a, ed, 1.0, None, ALU.add))
            link(V.reciprocal(g1, g1a))
            link(V.tensor_tensor(g2, ed, g1, ALU.mult))
            step(V.tensor_tensor(oh, oh, per_token(g1), ALU.mult))
            link(V.tensor_tensor(second, second, per_token(g2), ALU.mult))
            for b in range(MAXB):
                step(V.tensor_tensor(wts[:, :, b, :], oh, second, ALU.add))
            run_pass(main)
            count = dve.value_load(need[0:1, 0:1], min_val=0, max_val=T)
            with dve.If(count > CAP):
                run_pass(extra)
            with dve.Else():
                dve.nop()
            dve.drain().then_inc(x_final, 1)
            dve.wait_ge(frms_ready, 1)
            link(V.reciprocal(rstd[:, 0, :], rms[:, 0, :]))
            for m in range(KC):
                k = VEC_FINAL + m
                V.scalar_tensor_tensor(out=xn[:, m, :], in0=x[:, m, :], scalar=vec[:, k:k + 1], in1=rstd[:, 0, :], op0=ALU.mult,
                                       op1=ALU.mult).then_inc(y_ready, 1)

        @block.gpsimd
        def _(pool):
            G = nc.gpsimd
            pool.dma_start(gatew[:, :, :, :], gate_w[0]).then_inc(s_gw, 16)
            pool.dma_start(poolw[:, :, :], pool_w[0]).then_inc(s_pw, 16)
            for l in range(DEPTH):
                if l > 0:
                    for m in range(KC):
                        wait_read(pool, tiles[("fd1", l - 1, m)])
                G.memset(pp[:, :, 0:HIST], 0.0).then_inc(padded, 1)
                G.memset(cp[:, :, 0:CW - 1], 0.0).then_inc(padded, 1)
                pool.dma_start(spool.rearrange("p c b t -> p (c b t)"), hists[l]).then_inc(hist_loaded, 16)
                pool.dma_start(sconv.rearrange("p c b t -> p (c b t)"), taps[l]).then_inc(hist_loaded, 16)
                for m in range(12):
                    wait_read(pool, tiles[("in", l, m)])
                pool.wait_ge(h_last, l + 1)
                for src, o, shape in ((pp[:, :, TP:TP + HIST], O_PP, (HIST,)), (cp[:, :, TP:TP + CW - 1], O_PC, (CW - 1,)),
                                      (cv[:, :, TP - 1:TP], O_PH, (1,)), (spool[:, :, :, 1:16], O_SP, (TS, HIST)),
                                      (sconv[:, :, :, 1:CW], O_SC, (TS, CW - 1)), (cv[:, :, TP:T], O_SH, (TS,))):
                    size = RC
                    for d in shape:
                        size *= d
                    dst = o_small[l][:, o:o + size]
                    dst = dst.rearrange("p (c t) -> p c t", c=RC) if len(shape) == 1 else \
                        dst.rearrange("p (c b t) -> p c b t", c=RC, b=TS)
                    with nc.allow_non_contiguous_dma(reason="one value per channel"):
                        pool.dma_start(dst, src).then_inc(small_written, 16)
                for m in range(KC):
                    wait_read(pool, tiles[key_tile(l, m)])
                pool.dma_start(o_k[l], kT).then_inc(kv_written, 16)
                for s in range(4):
                    for mc in range(MC):
                        wait_read(pool, tiles[("mv", l, s, mc)])
                pool.dma_start(o_v[l], vN).then_inc(kv_written, 16)
                if l + 1 < DEPTH:
                    for c in range(RC):
                        wait_full(pool, tiles[("gx", l, c)])
                        wait_full(pool, tiles[("pw", l, c)])
                    pool.dma_start(gatew[:, :, :, :], gate_w[l + 1]).then_inc(s_gw, 16)
                    pool.dma_start(poolw[:, :, :], pool_w[l + 1]).then_inc(s_pw, 16)
            pool.wait_ge(small_written, 96 * DEPTH)
            pool.wait_ge(kv_written, 32 * DEPTH)


def kernel(**inputs):
    import numpy as np
    import concourse.bacc as bacc
    from concourse.bass_utils import run_bass_kernel_spmd as run

    a = {k: np.asarray(v) for k, v in inputs.items()}

    def feat(m):
        r, f = m.shape
        return m.reshape(r, f // P, P).transpose(2, 1, 0)

    xs = feat(np.concatenate([a["x_prompt"].reshape(TP, D), a["x_sample"].reshape(TS, D)]))
    ms = feat(a["mem_prompt"].reshape(NM, D))
    cols = []
    for l in range(DEPTH):
        for name in ("norm_mix", "norm_mem", "mem_norm", "norm_ffn", "out_norm_pool", "out_norm_rnn", "pool_scale",
                     "conv_w", "conv_b", "gate_a_b", "gate_x_b", "rglru_lambda"):
            cols.append(a[name][l].reshape(-1, P).T)
    cols.append(a["final_norm"].reshape(-1, P).T)
    cols.append(a["state_h"].reshape(DEPTH, TS, RC, P).transpose(3, 0, 2, 1).reshape(P, -1))
    vecs = np.concatenate(cols, axis=1)

    taps = np.zeros((DEPTH, P, RC, TS, CW), np.float32)
    taps[..., :CW - 1] = a["state_conv"].reshape(DEPTH, TS, CW - 1, RC, P).transpose(0, 4, 3, 1, 2)
    hists = np.zeros((DEPTH, P, RC, TS, HIST + 1), np.float32)
    hists[..., :HIST] = a["state_pool"].reshape(DEPTH, TS, HIST, RC, P).transpose(0, 4, 3, 1, 2)

    con = np.zeros((P, NCONST), np.float32)
    con[:, C_ID:C_ID + P] = np.eye(P)
    con[:, C_TRI:C_TRI + P] = np.triu(np.ones((P, P)), 1)
    con[:, C_IOTA:C_IOTA + P] = np.arange(P)
    for g, w in enumerate(WINDOWS):
        con[:, C_CORR + 16 * g:C_CORR + 16 * g + 16] = w / np.minimum(np.arange(16) + 1, w)
    for t, (_, rows) in enumerate(TOK):
        con[:rows, C_VALID + t] = 1

    pw = a["pool_w"].transpose(0, 2, 1, 3)
    gw = np.zeros((DEPTH, P, 2, RC, P), np.float32)
    for i, name in enumerate(("gate_a_w", "gate_x_w")):
        w = a[name].reshape(DEPTH, RC, 2, 64, 64)
        for j in range(2):
            gw[:, 64 * j:64 * j + 64, i, :, 64 * j:64 * j + 64] = w[:, :, j].transpose(0, 2, 1, 3)
    rw = a["router_w"][0].reshape(KC, P, NE).transpose(1, 0, 2)

    def columns(w, i):
        s, half = i // 2, i % 2
        return w[512 * half:512 * half + 512, s * PIECE:(s + 1) * PIECE].reshape(4, P, PIECE).transpose(1, 0, 2)

    dense = np.empty((len(stream_plan()), P, 4, PIECE), np.float32)
    order = np.r_[D // 2:D, D:3 * D // 2, 0:D // 2]
    names = {"mk": "w_mk", "mv": "w_mv", "out": "w_out", "mq": "w_mq", "mo": "w_mo"}
    win = a["w_in"][:, :, order]
    ck = a["cache_mem_k"].reshape(DEPTH, 4, 2, NM, NH, HC, P)
    cvv = a["cache_mem_v"].reshape(DEPTH, 4, 2, MC, P, NH, HD)
    fd = a["ffn_w_down"].reshape(-1, FC, P, KC // 2, PIECE)
    for k, (kind, l, i) in enumerate(stream_plan()):
        if kind in ("kn", "kf"):
            layer, pair = next(late[1:] for late in LATE[l] if late[0] == kind)
            dense[k] = columns(a["w_mk"][layer], 2 * pair + i)
        elif kind in names:
            dense[k] = columns(a[names[kind]][l], i)
        elif kind == "in":
            dense[k] = columns(win[l], i)
        elif kind == "fg":
            dense[k] = columns(a["ffn_w_gate"][l // 2], i)
        elif kind == "fu":
            dense[k] = columns(a["ffn_w_up"][l // 2], i)
        elif kind == "kc":
            dense[k] = ck[l, i % 4, :, :, i // 4].transpose(3, 0, 2, 1).reshape(P, 4, NM)
        elif kind == "vc":
            dense[k] = cvv[l, i % 4, :, :, :, i // 4].transpose(2, 0, 1, 3).reshape(P, 4, HD)
        else:
            c0, c1 = HALVES[int(kind[2])]
            pieces = fd[l // 2, c0:c1].transpose(2, 0, 1, 3).reshape(-1, P, PIECE)
            dense[k] = pieces[4 * i:4 * i + 4].transpose(1, 0, 2)

    ex = np.empty((NE, EUNITS, P, EUNIT), np.float32)
    gu = ex[:, 0:16].reshape(NE, 4, 2, 2, P, 4, GW)
    for i, name in enumerate(("moe_w_gate", "moe_w_up")):
        gu[:, :, i] = a[name][0].reshape(NE, 2, 4, P, 4, GW).transpose(0, 4, 1, 3, 2, 5)
    ex[:, 0:16] = gu.reshape(NE, 16, P, EUNIT)
    w = a["moe_w_down"][0].reshape(NE, FEC, P, 2, 512).transpose(0, 3, 2, 1, 4).reshape(NE, 2, P, 4, EUNIT)
    ex[:, 16:] = w.transpose(0, 1, 3, 2, 4).reshape(NE, 8, P, EUNIT)

    arrays = {"xT": xs, "memT": ms, "vecs": vecs, "taps": taps.reshape(DEPTH, P, -1),
              "hists": hists.reshape(DEPTH, P, -1), "consts": con, "pool_w": pw, "gate_w": gw, "router_w": rw,
              "dense": dense.reshape(-1, P, UNIT), "experts": ex.reshape(NE * EUNITS, P, EUNIT)}
    arrays = {k: np.ascontiguousarray(v) for k, v in arrays.items()}
    nc = bacc.Bacc("TRN2", target_bir_lowering=False, num_devices=1)
    args = [nc.dram_tensor(k, v.shape, F32, kind="ExternalInput").ap() for k, v in arrays.items()]
    outs = {"o_y": (P, KC, T), "o_small": (DEPTH, P, NOUT), "o_k": (DEPTH, P, KC, NM), "o_v": (DEPTH, P, MC, D)}
    args += [nc.dram_tensor(k, s, F32, kind="ExternalOutput").ap() for k, s in outs.items()]
    trunk_kernel(nc, *args)
    r = run(nc, [arrays], core_ids=[0]).results[0]

    y = r["o_y"].transpose(2, 1, 0).reshape(T, D)
    sm = r["o_small"]

    def part(o, *dims):
        size = RC * int(np.prod(dims))
        return sm[:, :, o:o + size].reshape(DEPTH, P, RC, *dims)

    half = D // 2
    pool_p = part(O_PP, HIST).transpose(0, 3, 2, 1).reshape(DEPTH, 1, HIST, half)
    conv_p = part(O_PC, CW - 1).transpose(0, 3, 2, 1).reshape(DEPTH, 1, CW - 1, half)
    h_p = part(O_PH).transpose(0, 2, 1).reshape(DEPTH, 1, half)
    pool_s = part(O_SP, TS, HIST).transpose(0, 3, 4, 2, 1).reshape(DEPTH, TS, HIST, half)
    conv_s = part(O_SC, TS, CW - 1).transpose(0, 3, 4, 2, 1).reshape(DEPTH, TS, CW - 1, half)
    h_s = part(O_SH, TS).transpose(0, 3, 2, 1).reshape(DEPTH, TS, half)
    mk = r["o_k"].transpose(0, 3, 2, 1).reshape(DEPTH, 1, NM, NH, HD)
    mv = r["o_v"].transpose(0, 2, 1, 3).reshape(DEPTH, 1, NM, NH, HD)
    return (y[:TP].reshape(1, TP, D), y[TP:].reshape(TS, 1, D), pool_p, conv_p, h_p, mk, mv, pool_s, conv_s, h_s)
```
